# Optimizing a Trainium2 kernel written in Bass

```python
import math
import jax, jax.numpy as jnp
from jax import lax
import numpy as np

D_MODEL = 1024
BATCH = 1
SEQ = 128
DEPTH = 1
DEC_BATCH = 1
DEC_SEQ = 128
PAST_LEN = 128

GRID_W = 64
N_POOL_GROUPS = 4
POOL_GROUP_DIM = 128
POOL_DIM = N_POOL_GROUPS * POOL_GROUP_DIM
POOL_WINDOWS = (2, 4, 8, 16)
N_HEADS = 8
HEAD_DIM = 64
ATTN_DIM = N_HEADS * HEAD_DIM
WIN_R = 8
WIN_C = 16
N_EXPERTS = 32
TOP_K = 4
D_FF = 1024
SWIGLU_LIMIT = 7.0
SWIGLU_ALPHA = 1.702
N_MOD = 6
Q_BLOCK = 128
RMS_EPS = 1e-6
NEG_INF = -1e30
ATTN_SCALE = HEAD_DIM ** -0.5
IN_DIM = POOL_DIM + 3 * ATTN_DIM + 2 * D_MODEL

kernel_name = "hybrid_pool_natten_moe_diffusion_step"

def rmsnorm(x, gain):
    x32 = x.astype(jnp.float32)
    y = x32 * lax.rsqrt(jnp.mean(x32 * x32, axis=-1, keepdims=True) + RMS_EPS)
    return (y * gain.astype(jnp.float32)).astype(x.dtype)

def modulation(cvec, w_ada, b_ada):
    return jnp.split(jax.nn.silu(cvec) @ w_ada + b_ada, N_MOD, axis=-1)

def pool_mixer(u, w_pool, pool_scale):
    B, T, _ = u.shape
    u32 = u.reshape(B, T, N_POOL_GROUPS, POOL_GROUP_DIM).astype(jnp.float32)
    cs = jnp.concatenate([jnp.zeros_like(u32[:, :1]), lax.cumsum(u32, axis=1)], axis=1)
    t = jnp.arange(T)
    outs = []
    for g, w in enumerate(POOL_WINDOWS):
        lo = jnp.clip(t - w // 2, 0, T)
        hi = jnp.clip(t - w // 2 + w, 0, T)
        s = cs[:, hi, g] - cs[:, lo, g]
        cnt = (hi - lo).astype(jnp.float32)[None, :, None]
        outs.append(s / cnt - u32[:, :, g])
    p = jnp.stack(outs, axis=2).astype(u.dtype)
    y = jnp.einsum('btgc,gcd->btgd', p, w_pool)
    return y.reshape(B, T, POOL_DIM) * pool_scale

def split_heads(z):
    B, T, _ = z.shape
    return z.reshape(B, T, N_HEADS, HEAD_DIM).transpose(0, 2, 1, 3)

def merge_heads(o):
    B, H, T, dh = o.shape
    return o.transpose(0, 2, 1, 3).reshape(B, T, H * dh)

def ctx_attention(q, k, v):
    B, H, L, dh = q.shape
    nb = L // Q_BLOCK
    qb = q.reshape(B, H, nb, Q_BLOCK, dh).transpose(2, 0, 1, 3, 4)

    def block(qi):
        s = jnp.einsum('bhqd,bhkd->bhqk', qi, k).astype(jnp.float32) * ATTN_SCALE
        p = jax.nn.softmax(s, axis=-1).astype(v.dtype)
        return jnp.einsum('bhqk,bhkd->bhqd', p, v)

    o = lax.map(block, qb)
    return o.transpose(1, 2, 0, 3, 4).reshape(B, H, L, dh)

def na_latent_attention(q, k, v, kc, vc, rpb):
    B, H, T, dh = q.shape
    rows = T // GRID_W
    kr = min(WIN_R, rows)
    r = jnp.arange(rows)
    row_start = jnp.clip(r - kr // 2, 0, rows - kr)
    row_idx = row_start[:, None] + jnp.arange(kr)[None, :]
    col = jnp.arange(GRID_W)
    col_start = jnp.clip(col - WIN_C // 2, 0, GRID_W - WIN_C)
    nk = kr * GRID_W

    qg = q.reshape(B, H, rows, GRID_W, dh)
    kg = k.reshape(B, H, rows, GRID_W, dh)[:, :, row_idx].reshape(B, H, rows, nk, dh)
    vg = v.reshape(B, H, rows, GRID_W, dh)[:, :, row_idx].reshape(B, H, rows, nk, dh)

    key_col = jnp.tile(col, kr)
    key_row = row_idx[:, jnp.repeat(jnp.arange(kr), GRID_W)]
    dr = key_row - r[:, None]
    dc = key_col[None, :] - col[:, None]
    in_win = (key_col[None, :] >= col_start[:, None]) & (key_col[None, :] < col_start[:, None] + WIN_C)
    bias = rpb[:, (dr + WIN_R - 1)[:, None, :],
               jnp.clip(dc + WIN_C - 1, 0, 2 * WIN_C - 2)[None, :, :]].astype(jnp.float32)

    s_loc = jnp.einsum('bhrqd,bhrkd->bhrqk', qg, kg).astype(jnp.float32) * ATTN_SCALE + bias[None]
    s_loc = jnp.where(in_win[None, None, None], s_loc, NEG_INF)
    s_ctx = jnp.einsum('bhrqd,bhld->bhrql', qg, kc).astype(jnp.float32) * ATTN_SCALE
    p = jax.nn.softmax(jnp.concatenate([s_loc, s_ctx], axis=-1), axis=-1).astype(v.dtype)
    o = (jnp.einsum('bhrqk,bhrkd->bhrqd', p[..., :nk], vg)
         + jnp.einsum('bhrql,bhld->bhrqd', p[..., nk:], vc))
    return o.reshape(B, H, T, dh)

def mixing_branches(h, w_in, w_pool, pool_scale, w_pa, w_pb, w_out, attend):
    z = h @ w_in
    u_pool, q, k, v, ga, gb = jnp.split(
        z, [POOL_DIM, POOL_DIM + ATTN_DIM, POOL_DIM + 2 * ATTN_DIM,
            POOL_DIM + 3 * ATTN_DIM, POOL_DIM + 3 * ATTN_DIM + D_MODEL], axis=-1)
    a = pool_mixer(u_pool, w_pool, pool_scale) @ w_pa
    kh, vh = split_heads(k), split_heads(v)
    o = merge_heads(attend(split_heads(q), kh, vh)) @ w_pb
    merged = jax.nn.sigmoid(ga) * a + jax.nn.sigmoid(gb) * o
    return merged @ w_out, kh, vh

def moe(h, w_router, b_router, w_up, b_up, w_down, b_down):
    shp = h.shape
    x = h.reshape(-1, shp[-1])
    logits = (x @ w_router + b_router).astype(jnp.float32)
    top_vals, top_idx = lax.top_k(logits, TOP_K)
    wts = jax.nn.softmax(top_vals, axis=-1)
    combine = jnp.sum(jax.nn.one_hot(top_idx, N_EXPERTS, dtype=jnp.float32) * wts[..., None], axis=1)
    combine = combine.astype(x.dtype)

    def expert(acc, xs):
        wu, bu, wd, bd, g = xs
        gu = x @ wu + bu
        gate, up = gu[:, :D_FF], gu[:, D_FF:]
        gate = jnp.minimum(gate, SWIGLU_LIMIT)
        up = jnp.clip(up, -SWIGLU_LIMIT, SWIGLU_LIMIT)
        glu = gate * jax.nn.sigmoid(SWIGLU_ALPHA * gate)
        y = ((up + 1.0) * glu) @ wd + bd
        return acc + g[:, None] * y, None

    acc, _ = lax.scan(expert, jnp.zeros_like(x), (w_up, b_up, w_down, b_down, combine.T))
    return acc.reshape(shp)

def setup_inputs(seed: int = 0) -> dict:
    key = jax.random.key(seed)
    ks = jax.random.split(key, 32)
    n = jax.random.normal
    f = jnp.float32
    D = D_MODEL
    return {
        "x_prompt": n(ks[0], (BATCH, SEQ, D), f),
        "x_sample": n(ks[1], (DEC_BATCH, DEC_SEQ, D), f),
        "cache_k": n(ks[2], (DEC_BATCH, DEPTH, N_HEADS, PAST_LEN, HEAD_DIM), f),
        "cache_v": n(ks[3], (DEC_BATCH, DEPTH, N_HEADS, PAST_LEN, HEAD_DIM), f),
        "c": n(ks[4], (DEC_BATCH, D), f),
        "c_ctx": n(ks[5], (D,), f),
        "w_ada": n(ks[6], (DEPTH, D, N_MOD * D), f) * (0.5 * D ** -0.5),
        "b_ada": n(ks[7], (DEPTH, N_MOD * D), f) * 0.02,
        "g_mix": 1.0 + 0.05 * n(ks[8], (DEPTH, D), f),
        "w_in": n(ks[9], (DEPTH, D, IN_DIM), f) * D ** -0.5,
        "w_pool": n(ks[10], (DEPTH, N_POOL_GROUPS, POOL_GROUP_DIM, POOL_GROUP_DIM), f) * POOL_GROUP_DIM ** -0.5,
        "pool_scale": 1.0 + 0.05 * n(ks[11], (DEPTH, POOL_DIM), f),
        "w_pa": n(ks[12], (DEPTH, POOL_DIM, D), f) * POOL_DIM ** -0.5,
        "w_pb": n(ks[13], (DEPTH, ATTN_DIM, D), f) * ATTN_DIM ** -0.5,
        "rpb": n(ks[14], (DEPTH, N_HEADS, 2 * WIN_R - 1, 2 * WIN_C - 1), f) * 0.2,
        "w_out": n(ks[15], (DEPTH, D, D), f) * D ** -0.5,
        "g_ffn": 1.0 + 0.05 * n(ks[16], (DEPTH, D), f),
        "w_router": n(ks[17], (DEPTH, D, N_EXPERTS), f) * D ** -0.5,
        "b_router": n(ks[18], (DEPTH, N_EXPERTS), f) * 0.01,
        "w_up": n(ks[19], (DEPTH, N_EXPERTS, D, 2 * D_FF), f) * D ** -0.5,
        "b_up": n(ks[20], (DEPTH, N_EXPERTS, 2 * D_FF), f) * 0.02,
        "w_down": n(ks[21], (DEPTH, N_EXPERTS, D_FF, D), f) * D_FF ** -0.5,
        "b_down": n(ks[22], (DEPTH, N_EXPERTS, D), f) * 0.02,
        "g_final": 1.0 + 0.05 * n(ks[23], (D,), f),
    }

def reference(x_prompt, x_sample, cache_k, cache_v, c, c_ctx, w_ada, b_ada, g_mix, w_in, w_pool,
              pool_scale, w_pa, w_pb, rpb, w_out, g_ffn, w_router, b_router, w_up, b_up, w_down,
              b_down, g_final):
    xp = x_prompt
    xs = x_sample
    new_k, new_v = [], []
    for l in range(DEPTH):
        moe_args = (w_router[l], b_router[l], w_up[l], b_up[l], w_down[l], b_down[l])
        mix_args = (w_in[l], w_pool[l], pool_scale[l], w_pa[l], w_pb[l], w_out[l])

        sh_m, sc_m, gt_m, sh_f, sc_f, gt_f = modulation(c_ctx[None, None, :], w_ada[l], b_ada[l])
        h = rmsnorm(xp, g_mix[l]) * (1.0 + sc_m) + sh_m
        mix, kh, vh = mixing_branches(h, *mix_args, ctx_attention)
        xp = xp + gt_m * mix
        h = rmsnorm(xp, g_ffn[l]) * (1.0 + sc_f) + sh_f
        xp = xp + gt_f * moe(h, *moe_args)
        new_k.append(kh)
        new_v.append(vh)

        kc, vc, rpb_l = cache_k[:, l], cache_v[:, l], rpb[l]
        sh_m, sc_m, gt_m, sh_f, sc_f, gt_f = modulation(c[:, None, :], w_ada[l], b_ada[l])
        h = rmsnorm(xs, g_mix[l]) * (1.0 + sc_m) + sh_m
        mix, _, _ = mixing_branches(
            h, *mix_args, lambda q, k, v: na_latent_attention(q, k, v, kc, vc, rpb_l))
        xs = xs + gt_m * mix
        h = rmsnorm(xs, g_ffn[l]) * (1.0 + sc_f) + sh_f
        xs = xs + gt_f * moe(h, *moe_args)

    y_prompt = rmsnorm(xp, g_final)
    y_sample = rmsnorm(xs, g_final)
    new_cache_k = jnp.stack(new_k, axis=1)
    new_cache_v = jnp.stack(new_v, axis=1)
    return (y_prompt, y_sample, new_cache_k, new_cache_v)


_drawn_inputs = setup_inputs


def setup_inputs(seed=0):
    import zlib

    import numpy as np

    out = dict(_drawn_inputs(seed))
    spreads = {}
    factors = {'pool_scale': 3.849,
     'rpb': 64.0,
     'b_router': 5.259,
     'b_up': 8.0,
     'b_down': 8.0,
     'cache_k': 4.015,
     'cache_v': 3.301}
    for name, (base, spread) in spreads.items():
        noise = np.random.default_rng([zlib.crc32(name.encode()), seed]).standard_normal(out[name].shape)
        drawn = base * np.exp(spread * noise) if base else spread * noise
        out[name] = __import__('jax').numpy.asarray(drawn.astype(out[name].dtype))
    for name, factor in factors.items():
        out[name] = (out[name] * factor).astype(out[name].dtype)
    return out
```

```python
from contextlib import ExitStack

import concourse.bass as bass
from concourse import mybir

F32 = mybir.dt.float32
BF16 = mybir.dt.bfloat16
I32 = mybir.dt.int32
ALU = mybir.AluOpType
ACT = mybir.ActivationFunctionType
AX = mybir.AxisListType

P = 128
D = 1024
KB = D // P
TOK = 2 * P
HEADS, DH = 8, 64
GRID_W, WIN_C, WIN_R = 64, 16, 8
RPB_W = 2 * WIN_C - 1
RPB_H = (2 * WIN_R - 1) * RPB_W
SCALE = DH ** -0.5
NEG = -1e30
EPS = 1e-6
E, TOPK, FF = 32, 4, 1024
LIMIT, ALPHA = 7.0, 1.702
HALF = 512
PAD = 8
PW = P + 2 * PAD

SLOT = 2048
RING = 16
RING0 = 9
ORDER = [10, 11, 12, 3, 4, 5, 6, 7, 8, 0, 1, 2, 9, 13, 14, 15]
CAP = 64
PAIRS = E // 2
ROUNDS = TOK // CAP
BODY = 2
UPC = 16
DNC = 8
PC = UPC + DNC
BC = BODY * PC
LAPS = BC // RING
VEC = 28

C_ADA0, C_IN, C_ADA1, C_ADA2, C_PA, C_PB, C_OUT, C_END = 0, 8, 24, 32, 40, 42, 44, 48
IN_ORDER = [1, 2, 3, 0, 4, 5, 6, 7]


def layer_kernel(nc, A_x_prompt, A_x_sample, A_cache_k, A_cache_v, A_c, A_c_ctx, A_w_ada, A_b_ada, A_g_mix,
                 A_w_in, A_w_pool, A_pool_scale, A_w_pa, A_w_pb, A_rpb, A_w_out, A_g_ffn, A_w_router,
                 A_b_router, A_w_up, A_b_up, A_w_down, A_b_down, A_g_final,
                 y_prompt, y_sample, new_k, new_v):
    w_in_v = A_w_in[0].rearrange("(k p) n -> p k n", p=P)
    w_ada_v = A_w_ada[0].rearrange("(k p) n -> p k n", p=P)
    w_pa_v = A_w_pa[0].rearrange("(k p) n -> p k n", p=P)
    w_pb_v = A_w_pb[0].rearrange("(k p) n -> p k n", p=P)
    w_out_v = A_w_out[0].rearrange("(k p) n -> p k n", p=P)
    w_up_v = A_w_up[0].rearrange("e (k p) n -> e p k n", p=P)
    w_down_v = A_w_down[0].rearrange("e (k p) n -> e p k n", p=P)

    with ExitStack() as ctx:
        def sb(name, shape, dt=F32):
            return ctx.enter_context(nc.sbuf_tensor(name, shape, dt))

        def sem(name):
            return ctx.enter_context(nc.semaphore(name))

        ring = sb("ring", [P, RING, SLOT])
        arena = sb("arena", [P, 12800])
        x = sb("x", [P, 2, D])
        gtf = sb("gtf", [P, 2, D])
        bparts = sb("bparts", [96, 2 * FF], BF16)
        sel = sb("sel", [96, E], BF16)
        selbuf = sb("selbuf", [96, 2, CAP], BF16)
        ident = sb("ident", [P, P])
        iota = sb("iota", [P, CAP])
        iota_i = sb("iota_i", [P, CAP], I32)
        tab = sb("tab", [P, PAIRS + 1, 8])
        cur = sb("cur", [P, 8])
        small = sb("small", [P, 256])
        flags = sb("flags", [P, 4], I32)

        def region(at, *shape):
            n = 1
            for s in shape:
                n *= s
            ap = arena[:, at:at + n]
            if len(shape) == 2:
                ap = ap.rearrange("p (a b) -> p a b", a=shape[0])
            if len(shape) == 3:
                ap = ap.rearrange("p (a b c) -> p a b c", a=shape[0], b=shape[1])
            return ap

        def in_slot(s, at, *shape):
            n = 1
            for v in shape:
                n *= v
            ap = ring[:, s, at:at + n]
            if len(shape) == 2:
                ap = ap.rearrange("p (a b) -> p a b", a=shape[0])
            if len(shape) == 3:
                ap = ap.rearrange("p (a b c) -> p a b c", a=shape[0], b=shape[1])
            return ap

        acc = region(0, 2, D)
        h2 = region(2048, 2, D)
        xgT = region(4096, 2, KB, P)
        oh = region(6144, 2, P)
        wo = region(6400, 2, P)
        woT = region(6656, 2, P)
        gate = region(6912, D)
        sig = region(7936, D)
        hid = region(8960, D)
        hT = region(9984, KB, P)
        yb = region(11008, D)
        sgA = region(0, KB, TOK)
        sgB = region(2048, KB, TOK)
        PTp = region(4096, HEADS, P)
        PTs = region(5120, 2, HEADS, P)
        xn = region(4096, 2, D)
        oT = region(7168, 4, TOK)
        pooled = region(8192, 4, TOK)
        yT = region(9216, 4, TOK)
        modrow = region(10240, 3, HALF)
        modT = region(11776, 4, P)
        knew = region(12288, HALF)
        h2T = region(4096, KB, TOK)
        sqj = region(6144, 2, D)
        combT = region(6144, TOK)[0:E, :]
        bup = region(0, 2 * FF)
        brem = region(2048, 2 * FF)
        bada = gtf[:, :, :].rearrange("p a b -> p (a b)")[:, 0:3 * HALF].rearrange("p (a b) -> p a b", a=3)
        tmp = region(8192, 2, HALF)
        hTm = in_slot(10, 0, KB, TOK)
        biasM = in_slot(11, 0, HEADS, P)
        bias_rev = in_slot(13, 0, HEADS, P)
        flip = in_slot(12, 1664, P)
        kc = in_slot(11, 1024, HALF)
        vc = in_slot(11, 1536, HALF)
        upad = in_slot(12, 0, 4, 2, PW)
        kcT = in_slot(12, 1152, 4, P)
        Ss = in_slot(13, 0, HEADS, TOK)
        qT = in_slot(14, 0, 4, TOK)
        kT = in_slot(14, 1024, 4, TOK)
        Sp = in_slot(15, 0, HEADS, P)
        vm = in_slot(15, 1024, 2, HALF)
        gtm = in_slot(13, 0, 2, D)
        Af = in_slot(14, 0, 2, D)
        shf = in_slot(15, 0, 2, D)

        vecs = sb("vecs", [VEC, P])
        cT = sb("cT", [P, VEC])
        gffn = in_slot(9, 0, D)
        cs = in_slot(9, 1024, KB, 32)
        wpool = in_slot(9, 1280, 4, P)
        pscr = region(6144, 2, 2, PW)
        cnt = region(6720, 4, PW)
        wrt = sb("wrt", [P, KB, E])
        brt = sb("brt", [P, E])
        bdn = region(9216, D)[0:E, :]
        selrow = sb("selrow", [P, 2, P])
        tri = sb("tri", [P, P])
        ones = sb("ones", [P, P])
        rt = sb("rt", [P, 2, 8, E])

        Am = small[:, 0:16].rearrange("p (g k) -> p g k", g=2)
        ssq = small[:, 16:18]
        rstd = small[:, 18:20]
        mx = small[:, 20:36].rearrange("p (a b) -> p a b", a=2)
        ssum = small[:, 36:52].rearrange("p (a b) -> p a b", a=2)
        rsum = small[:, 52:68].rearrange("p (a b) -> p a b", a=2)
        top8 = small[:, 68:84].rearrange("p (a b) -> p a b", a=2)
        misc = small[:, 84:100]

        gfin = in_slot(ORDER[0], 0, D)

        ps = ctx.enter_context(nc.psum_tensor("ps", [P, 8, HALF], F32))

        pro_loaded = [sem(f"pro_loaded{s}") for s in range(RING0)]
        moe_loaded = [sem(f"moe_loaded{s}") for s in range(RING)]
        pro_used, moe_free = sem("pro_used"), sem("moe_free")
        L = {n: sem("ld_" + n) for n in ("vec", "x0", "x1", "bada", "bup", "gffn", "rpb", "kc", "vc", "wpool",
                                         "wrt", "brt", "bdn", "gfin")}
        pool_step, dve_step, act_step = sem("pool_step"), sem("dve_step"), sem("act_step")
        const_ready, bias_ready, split_done = sem("const_ready"), sem("bias_ready"), sem("split_done")
        vec_t, vec_c, silu_ready = sem("vec_t"), sem("vec_c"), sem("silu_ready")
        ssq_ready, root_ready, xn_ready = sem("ssq_ready"), sem("root_ready"), sem("xn_ready")
        kc_t, kcT_ready, x_t = sem("kc_t"), sem("kcT_ready"), sem("x_t")
        row_ready, modT_done, A_ready = sem("row_ready"), sem("modT_done"), sem("A_ready")
        hT_ready, z_read = sem("hT_ready"), sem("z_read")
        S_done, S_read, mx_ready, exp_done = sem("S_done"), sem("S_read"), sem("mx_ready"), sem("exp_done")
        prob_ready, PT_done, PT_read = sem("prob_ready"), sem("PT_done"), sem("PT_read")
        k_t, knew_ready = sem("k_t"), sem("knew_ready")
        O_done, oT_ready, pooled_ready, pool_done, yT_ready = (sem("O_done"), sem("oT_ready"), sem("pooled_ready"),
                                                               sem("pool_done"), sem("yT_ready"))
        bc_done, bc_read, Af_ready = sem("bc_done"), sem("bc_read"), sem("Af_ready")
        br_done, br_read, merged_ready = sem("br_done"), sem("br_read"), sem("merged_ready")
        x2_ready, h2_ready, h2_t, h2T_ready = sem("x2_ready"), sem("h2_ready"), sem("h2_t"), sem("h2T_ready")
        logit_done, mask_ready, rank_done, e_ready, top_ready = (sem("logit_done"), sem("mask_ready"),
                                                                 sem("rank_done"), sem("e_ready"), sem("top_ready"))
        comb_ready, comb_t, combT_ready, bd_done = sem("comb_ready"), sem("comb_t"), sem("combT_ready"), sem("bd_done")
        flag_ready, tab_ready = sem("flag_ready"), sem("tab_ready")
        oh_ready, wo_ready, gath_done, xg_ready, sel_ready = (sem("oh_ready"), sem("wo_ready"), sem("gath_done"),
                                                              sem("xg_ready"), sem("sel_ready"))
        u_read, g_ready, sig_ready, hid_ready = sem("u_read"), sem("g_ready"), sem("sig_ready"), sem("hid_ready")
        scat_done, acc_done, woT_done, woT_ready = sem("scat_done"), sem("acc_done"), sem("woT_done"), sem("woT_ready")
        hT_done, hTe_ready, y_ready = sem("hT_done"), sem("hTe_ready"), sem("y_ready")
        cur_ready, glu_ready = sem("cur_ready"), sem("glu_ready")
        fin_ss, fin_ready, last_scat, stored = sem("fin_ss"), sem("fin_ready"), sem("last_scat"), sem("stored")
        kv_stored, bias_t, bias_copied = sem("kv_stored"), sem("bias_t"), sem("bias_copied")

        GB, YB = 4, 6

        block = ctx.enter_context(nc.Block())

        def further_rounds(eng, run):
            eng.wait_ge(flag_ready, 1)
            for r in range(1, ROUNDS):
                more = eng.value_load(flags[0:1, r:r + 1], min_val=0, max_val=1)
                with eng.If(more > 0):
                    run(r)

        @block.sync
        def _(sp):
            def mixing_chunk(c):
                s = ring[:, c % RING0, :]
                if c < C_IN:
                    return s, w_ada_v[:, c, 0:SLOT]
                if c < C_ADA1:
                    j, h = (c - C_IN) // 2, (c - C_IN) % 2
                    col = IN_ORDER[j] * HALF
                    return (s.rearrange("p (k n) -> p k n", k=4), w_in_v[:, 4 * h:4 * h + 4, col:col + HALF])
                if c < C_PA:
                    m, k = (c - C_ADA1) // KB + 1, (c - C_ADA1) % KB
                    return s, w_ada_v[:, k, m * SLOT:(m + 1) * SLOT]
                s = s.rearrange("p (k n) -> p k n", k=2)
                if c < C_PB:
                    k, w = 2 * (c - C_PA), w_pa_v
                elif c < C_OUT:
                    k, w = 2 * (c - C_PB), w_pb_v
                else:
                    k, w = 2 * (c - C_OUT), w_out_v
                return s, w[:, k:k + 2, :]

            for c in range(C_END):
                if c >= RING0:
                    sp.wait_ge(pro_used, c - RING0 + 1)
                dst, src = mixing_chunk(c)
                sp.dma_start(dst, src).then_inc(pro_loaded[c % RING0], 16)

            def stream(I, i):
                n0 = sp.snap(I * BC)
                for h in range(BODY):
                    for c in range(PC):
                        n = h * PC + c
                        a = c % 2
                        e = i * (2 * BODY) + (2 * h + a)
                        slot = ring[:, ORDER[n % RING], :]
                        sp.wait_ge(moe_free, n0 + (n + 1))
                        if c < UPC:
                            src = w_up_v[e, :, c // 2, :]
                            dst = slot
                        else:
                            f = 2 * ((c - UPC) // 2)
                            src = w_down_v[e, :, f:f + 2, :]
                            dst = slot.rearrange("p (k n) -> p k n", k=2)
                        sp.dma_start(dst, src).then_inc(moe_loaded[n % RING], 16)

            with sp.Fori(0, PAIRS // BODY) as i:
                stream(i, i)

            def run(r):
                with sp.Fori(0, PAIRS // BODY) as i:
                    stream(i + r * (PAIRS // BODY), i)
            further_rounds(sp, run)

            sp.wait_ge(last_scat, 1)
            sp.dma_start(gfin, A_g_final.rearrange("(a n) -> a n", a=1).to_broadcast([P, D])).then_inc(L["gfin"], 16)
            sp.wait_ge(fin_ready, 1)
            sp.dma_start(y_prompt[0], x[:, 0, :]).then_inc(stored, 16)
            sp.wait_ge(fin_ready, 2)
            sp.dma_start(y_sample[0], x[:, 1, :]).then_inc(stored, 16)
            sp.wait_ge(stored, 32)
            sp.wait_ge(kv_stored, 32)

        @block.gpsimd
        def _(pool):
            def part_load(dst, src, s):
                pool.dma_start(dst, src).then_inc(s, 16)

            part_load(kc, A_cache_k[0, 0].rearrange("h l d -> l h d"), L["kc"])
            for r in range(2):
                for kr in range(2):
                    for par in range(2):
                        at = par * RPB_H + (kr - r + WIN_R - 1) * RPB_W + WIN_C - GRID_W
                        src = bass.AP(A_rpb.tensor, A_rpb.offset + at,
                                      [[1, GRID_W], [2 * RPB_H, 4], [1, GRID_W]])
                        dst = bias_rev[64 * r:64 * r + 64, 4 * par:4 * par + 4, 64 * kr:64 * kr + 64]
                        part_load(dst, src, L["rpb"])
            for q in range(3):
                part_load(bup[32 * q:32 * q + 32, :], A_b_up[0], L["bup"])

            k = [0]

            def link(ins):
                k[0] += 1
                ins.then_inc(pool_step, 1)
                pool.wait_ge(pool_step, k[0])

            link(nc.gpsimd.memset(ident[:, :], 0.0))
            link(nc.gpsimd.affine_select(out=ident[:, :], in_=ident[:, :], compare_op=ALU.not_equal, fill=1.0,
                                         base=0, pattern=[[-1, P]], channel_multiplier=1))
            pool.sem_inc(const_ready, 1)
            link(nc.gpsimd.memset(flip, 0.0))
            for total in (GRID_W - 1, 3 * GRID_W - 1):
                link(nc.gpsimd.affine_select(out=flip, in_=flip, compare_op=ALU.not_equal, fill=1.0,
                                             base=-total, pattern=[[1, P]], channel_multiplier=1))
            pool.sem_inc(const_ready, 1)
            link(nc.gpsimd.memset(ones[:, :], 1.0))
            link(nc.gpsimd.memset(tri[:, :], 1.0))
            link(nc.gpsimd.memset(selrow[:, :, :], 0.0))
            link(nc.gpsimd.memset(sel[:, :], 1.0))
            link(nc.gpsimd.iota(iota_i[:, :], [[1, CAP]], base=0, channel_multiplier=0))
            link(nc.gpsimd.affine_select(out=tri[:, :], in_=tri[:, :], compare_op=ALU.is_gt, fill=0.0,
                                         base=0, pattern=[[1, P]], channel_multiplier=-1))
            for q in range(4):
                v = selrow[32 * q:32 * q + 32, :, :]
                link(nc.gpsimd.affine_select(out=v, in_=v, compare_op=ALU.not_equal, fill=1.0,
                                             base=0, pattern=[[-16, 2], [0, P]], channel_multiplier=1))
            for q in range(3):
                v = sel[32 * q:32 * q + 32, :]
                link(nc.gpsimd.affine_select(out=v, in_=v, compare_op=ALU.is_equal, fill=0.0,
                                             base=0, pattern=[[-1, E]], channel_multiplier=1))
            link(nc.gpsimd.tensor_copy(iota[:, :], iota_i[:, :]))
            pool.sem_inc(const_ready, 1)
            pool.wait_ge(bias_copied, 1)
            for r in range(2):
                for kr in range(2):
                    v = biasM[64 * r:64 * r + 64, :, 64 * kr:64 * kr + GRID_W - WIN_C]
                    link(nc.gpsimd.affine_select(out=v, in_=v, compare_op=ALU.is_ge, fill=NEG, base=WIN_C // 2,
                                                 pattern=[[0, HEADS], [1, GRID_W - WIN_C]], channel_multiplier=-1))
                    v = biasM[64 * r:64 * r + 64, :, 64 * kr + WIN_C:64 * kr + GRID_W]
                    ins = nc.gpsimd.affine_select(out=v, in_=v, compare_op=ALU.is_ge, fill=NEG,
                                                  base=WIN_C // 2 - 1 - WIN_C,
                                                  pattern=[[0, HEADS], [-1, GRID_W - WIN_C]], channel_multiplier=1)
                    link(ins)
            pool.sem_inc(bias_ready, 1)
            pool.wait_ge(L["bup"], 48)
            link(nc.gpsimd.tensor_copy(bparts[:, :], bup[0:96, :]))
            for q in (1, 2):
                link(nc.gpsimd.tensor_tensor(brem[32 * q:32 * q + 32, :], bup[32 * q:32 * q + 32, :],
                                             bparts[32 * q:32 * q + 32, :], ALU.subtract))
                link(nc.gpsimd.tensor_copy(bparts[32 * q:32 * q + 32, :], brem[32 * q:32 * q + 32, :]))
            link(nc.gpsimd.tensor_tensor(bup[64:96, :], brem[64:96, :], bparts[64:96, :], ALU.subtract))
            nc.gpsimd.tensor_copy(bparts[64:96, :], bup[64:96, :]).then_inc(split_done, 1)
            pool.wait_ge(split_done, 1)
            pool.wait_ge(z_read, 3)
            pool.dma_start(new_v[0, 0].rearrange("h l d -> l h d"),
                           vm[:, 0, :].rearrange("p (h d) -> p h d", h=HEADS)).then_inc(kv_stored, 16)
            pool.wait_ge(knew_ready, 1)
            pool.dma_start(new_k[0, 0].rearrange("h l d -> l h d"),
                           knew.rearrange("p (h d) -> p h d", h=HEADS)).then_inc(kv_stored, 16)

            def body(I, i):
                P0 = pool.snap(I * BODY)
                e0 = pool.snap(i * (2 * BODY))
                for h in range(BODY):
                    pool.wait_ge(u_read, P0 + (h + 1))
                    nc.gpsimd.tensor_copy(selbuf[:, :, :], sel[:, bass.ds(e0 + 2 * h, 2)].unsqueeze(2)
                                          .to_broadcast([96, 2, CAP])).then_inc(sel_ready, 1)

            with pool.Fori(0, PAIRS // BODY) as i:
                body(i, i)

            def run(r):
                with pool.Fori(0, PAIRS // BODY) as i:
                    body(i + r * (PAIRS // BODY), i)
            further_rounds(pool, run)

        @block.scalar
        def _(act):
            for row, src in ((0, A_c_ctx), (8, A_c[0]), (16, A_g_mix[0])):
                act.dma_start(vecs[row:row + 8, :], src.rearrange("(k p) -> k p", p=P)).then_inc(L["vec"], 16)
            act.dma_start(vecs[24:28, :], A_pool_scale[0].rearrange("(k p) -> k p", p=P)).then_inc(L["vec"], 16)
            act.dma_start(x[:, 0, :], A_x_prompt[0]).then_inc(L["x0"], 16)
            act.dma_start(x[:, 1, :], A_x_sample[0]).then_inc(L["x1"], 16)
            for q in range(4):
                src = A_b_ada[0].rearrange("(m q n) -> q m n", q=4, m=3)[q:q + 1]
                act.dma_start(bada[32 * q:32 * q + 32, :, :], src.to_broadcast([32, 3, HALF])).then_inc(L["bada"], 16)
            act.dma_start(vc.rearrange("p (h d) -> p h d", h=HEADS),
                          A_cache_v[0, 0].rearrange("h l d -> l h d")).then_inc(L["vc"], 16)
            act.dma_start(wpool[:, :, :], A_w_pool[0].rearrange("g c d -> c g d")).then_inc(L["wpool"], 16)
            act.dma_start(gffn, A_g_ffn.to_broadcast([P, D])).then_inc(L["gffn"], 16)
            act.dma_start(wrt[:, :, :], A_w_router[0].rearrange("(k p) n -> p k n", p=P)).then_inc(L["wrt"], 16)
            act.dma_start(brt[:, :], A_b_router.to_broadcast([P, E])).then_inc(L["brt"], 16)

            for t in range(2):
                act.wait_ge(L[f"x{t}"], 16)
                nc.scalar.activation(xn[:, t, :], x[:, t, :], ACT.Square,
                                     accum_out=ssq[:, t:t + 1]).then_inc(ssq_ready, 1)
            act.wait_ge(A_ready, 1)
            nc.scalar.activation(rstd, misc[:, 0:2], ACT.Sqrt).then_inc(root_ready, 1)
            act.wait_ge(vec_c, 1)
            nc.scalar.activation(misc[:, 0:16], cT[:, 0:16], ACT.Sigmoid).then_inc(silu_ready, 1)
            act.wait_ge(kc_t, 1)
            nc.scalar.activation(kcT, ps[:, 6, :].rearrange("p (a b) -> p a b", a=4), ACT.Copy).then_inc(kcT_ready, 1)
            act.wait_ge(bias_t, 1)
            nc.scalar.activation(biasM, ps[:, 6:8, :].rearrange("p a (b c) -> p (a b) c", b=4), ACT.Copy)\
                .then_inc(bias_copied, 1)
            act.wait_ge(A_ready, 2)
            act.wait_ge(x_t, 2)
            for t in range(2):
                for j in range(4, KB):
                    nc.scalar.activation(hTm[:, j, t * P:(t + 1) * P], ps[:, 2 + 2 * t, (j % 4) * P:(j % 4 + 1) * P],
                                         ACT.Identity, bias=modT[:, j % 4, 32 + 16 * t:33 + 16 * t],
                                         scale=Am[:, t, j:j + 1]).then_inc(hT_ready, 1)

            def z_out(cc):
                act.wait_ge(pro_used, C_IN + 2 * cc + 2)
                bank = 2 * (cc % 2)
                for b in range(2):
                    src = ps[:, bank + b, :]
                    if cc < 2:
                        dst, f = (qT, kT)[cc][:, 2 * b:2 * b + 2, :], ACT.Copy
                        src = src.rearrange("p (a b) -> p a b", a=2)
                    elif cc == 2:
                        dst, f = vm[:, b, :], ACT.Copy
                    elif cc == 3:
                        dst, f = upad[:, 2 * b:2 * b + 2, :, PAD:PAD + P], ACT.Copy
                        src = src.rearrange("p (a t n) -> p a t n", a=2, t=2)
                    else:
                        g = sgA if cc < 6 else sgB
                        j = 4 * (cc % 2) + 2 * b
                        dst, f = g[:, j:j + 2, :], ACT.Sigmoid
                        src = src.rearrange("p (a b) -> p a b", a=2)
                    ins = nc.scalar.activation(dst, src, f)
                ins.then_inc(z_read, 1)

            z_out(0)
            z_out(1)
            z_out(2)
            act.wait_ge(mx_ready, 1)
            for hh in range(HEADS):
                nc.scalar.activation(Sp[:, hh, :], ps[:, 4 + hh // 4, (hh % 4) * P:(hh % 4 + 1) * P], ACT.Exp,
                                     bias=mx[:, 0, hh:hh + 1], scale=SCALE,
                                     accum_out=ssum[:, 0, hh:hh + 1]).then_inc(exp_done, 1)
            act.wait_ge(pooled_ready, 1)
            z_out(3)
            act.wait_ge(k_t, 1)
            nc.scalar.activation(knew, ps[:, 6, :], ACT.Copy).then_inc(knew_ready, 1)
            act.wait_ge(mx_ready, 2)
            for hh in range(HEADS):
                nc.scalar.activation(Ss[:, hh, :], Ss[:, hh, :], ACT.Exp, bias=mx[:, 1, hh:hh + 1],
                                     accum_out=ssum[:, 1, hh:hh + 1]).then_inc(exp_done, 1)
            act.wait_ge(split_done, 1)
            z_out(4)

            def pt_out(n):
                act.wait_ge(PT_done, n + 1)
                bank = (6, 4, 6)[n]
                dst = (PTp, PTs[:, 0], PTs[:, 1])[n]
                for b in range(2):
                    ins = nc.scalar.activation(dst[:, 4 * b:4 * b + 4, :],
                                               ps[:, bank + b, :].rearrange("p (a b) -> p a b", a=4), ACT.Copy)
                ins.then_inc(PT_read, 1)

            pt_out(0)
            z_out(5)
            pt_out(1)
            z_out(6)
            pt_out(2)
            z_out(7)
            act.wait_ge(O_done, 1)
            for t in range(2):
                ins = nc.scalar.activation(oT[:, :, t * P:(t + 1) * P],
                                           ps[:, t, :].rearrange("p (a b) -> p a b", a=4), ACT.Copy)
            ins.then_inc(oT_ready, 1)
            act.wait_ge(pool_done, 1)
            for g in range(4):
                ins = nc.scalar.activation(yT[:, g, :], ps[:, 4 + g // 2, (g % 2) * TOK:(g % 2 + 1) * TOK], ACT.Copy,
                                           scale=cT[:, 24 + g:25 + g])
            ins.then_inc(yT_ready, 1)

            for n in range(4):
                m, t = n // 2, n % 2
                act.wait_ge(bc_done, n + 1)
                b = 4 * (n % 2)
                if m == 0:
                    nc.scalar.activation(gtm[:, t, :].rearrange("p (a b) -> p a b", a=2), ps[:, b:b + 2, :], ACT.Copy)
                    nc.scalar.activation(shf[:, t, :].rearrange("p (a b) -> p a b", a=2), ps[:, b + 2:b + 4, :],
                                         ACT.Copy).then_inc(bc_read, 1)
                else:
                    nc.scalar.activation(gtf[:, t, :].rearrange("p (a b) -> p a b", a=2), ps[:, b + 2:b + 4, :],
                                         ACT.Copy).then_inc(bc_read, 1)
            act.wait_ge(br_done, KB)
            act.dma_start(bdn, A_b_down[0]).then_inc(L["bdn"], 16)
            for t in range(2):
                act.wait_ge(x2_ready, t + 1)
                nc.scalar.activation(sqj[:, t, :], x[:, t, :], ACT.Square, accum_out=ssq[:, t:t + 1]).then_inc(ssq_ready, 1)
            act.wait_ge(A_ready, 3)
            nc.scalar.activation(rstd, misc[:, 0:2], ACT.Sqrt).then_inc(root_ready, 1)
            for b in range(4):
                act.wait_ge(h2_t, b + 1)
                t, jh = b // 2, b % 2
                nc.scalar.activation(h2T[:, 4 * jh:4 * jh + 4, t * P:(t + 1) * P],
                                     ps[:, 4 + b, :].rearrange("p (a b) -> p a b", a=4), ACT.Copy).then_inc(h2T_ready, 1)
            for t in range(2):
                act.wait_ge(top_ready, t + 1)
                nc.scalar.activation(rt[:, t, 1, :], rt[:, t, 0, :], ACT.Exp, bias=misc[:, 4 + t:5 + t]).then_inc(e_ready, 1)
            act.wait_ge(comb_t, 1)
            nc.scalar.activation(combT, ps[0:E, 1, 0:TOK], ACT.Copy).then_inc(combT_ready, 1)

            def xg_out(b, G, q):
                act.wait_ge(gath_done, G * 2 + (b + 1))
                nc.scalar.activation(xgT[:, q, 4 * b:4 * b + 4, :],
                                     ps[:, GB + b, :].rearrange("p (a b) -> p a b", a=4), ACT.Copy).then_inc(xg_ready, 1)

            def body(I, r):
                P0 = act.snap(I * BODY)
                n0 = act.snap(I * BC)
                G0 = act.snap(P0 + (r + 1))
                for h in range(BODY):
                    Pn, G = P0 + h, G0 + h
                    for b in range(2):
                        act.wait_ge(g_ready, Pn * 2 + (b + 1))
                        nc.scalar.activation(sig[:, b * HALF:(b + 1) * HALF], gate[:, b * HALF:(b + 1) * HALF],
                                             ACT.Sigmoid, scale=ALPHA).then_inc(sig_ready, 1)
                    for b in range(2):
                        xg_out(b, G, (h + 1) % 2)
                    act.wait_ge(woT_done, Pn + 2)
                    nc.scalar.activation(woT, ps[:, YB, 0:TOK].rearrange("p (a b) -> p a b", a=2),
                                         ACT.Copy).then_inc(woT_ready, 1)
                    for b in range(2):
                        act.wait_ge(hT_done, Pn * 2 + (b + 1))
                        nc.scalar.activation(hT[:, 4 * b:4 * b + 4, :],
                                             ps[:, GB + b, :].rearrange("p (a b) -> p a b", a=4),
                                             ACT.Copy).then_inc(hTe_ready, 1)
                    act.wait_ge(moe_free, n0 + (RING + (h + 1) * PC))
                    nc.scalar.activation(yb.rearrange("p (a b) -> p a b", a=2), ps[:, YB:YB + 2, :],
                                         ACT.Copy).then_inc(y_ready, 1)

            for b in range(2):
                xg_out(b, 0, 0)
            with act.Fori(0, PAIRS // BODY) as i:
                body(i, 0)

            def run(r):
                for b in range(2):
                    xg_out(b, r * (PAIRS + 1), 0)
                with act.Fori(0, PAIRS // BODY) as i:
                    body(i + r * (PAIRS // BODY), r)
            further_rounds(act, run)

            for t in range(2):
                act.wait_ge(fin_ss, t + 1)
                nc.scalar.activation(gtf[:, t, :], x[:, t, :], ACT.Square, accum_out=ssq[:, t:t + 1]).then_inc(ssq_ready, 1)
            act.wait_ge(A_ready, 4)
            nc.scalar.activation(rstd, misc[:, 0:2], ACT.Sqrt).then_inc(root_ready, 1)

        @block.vector
        def _(dve):
            k = [0]

            def link(ins):
                k[0] += 1
                ins.then_inc(dve_step, 1)
                dve.wait_ge(dve_step, k[0])

            V = nc.vector

            def rsqrt_of_mean(n):
                dve.wait_ge(ssq_ready, 2 * n)
                V.tensor_scalar(misc[:, 0:2], ssq, 1.0 / D, EPS, ALU.mult, ALU.add).then_inc(A_ready, 1)
                dve.wait_ge(root_ready, n)
                link(V.reciprocal(rstd, rstd))

            def doubled(dst, src, s):
                lo, hi = 1 << s, PW - (1 << s) + 1
                a, b = (1, 0) if s == 0 else (1 << s >> 1, 1 << s >> 1)
                return V.tensor_tensor(dst[..., lo:hi], src[..., lo - a:hi - a], src[..., lo + b:hi + b], ALU.add)

            V.memset(pscr[:, :, :, :], 0.0)
            link(V.memset(cnt[:, :, :], 0.0))
            link(V.memset(pscr[:, 0, 0, PAD:PAD + P], 1.0))
            for g in range(4):
                src, dst = pscr[:, g % 2, 0, :], (pscr[:, (g + 1) % 2, 0, :])
                v = slice(PAD, PAD + P)
                link(doubled(dst, src, g))
                link(V.tensor_copy(cnt[:, g, v], dst[:, v]))
            V.memset(upad[:, :, :, 0:PAD], 0.0)
            link(V.memset(upad[:, :, :, PAD + P:PW], 0.0))

            rsqrt_of_mean(1)
            for t in range(2):
                V.tensor_scalar(xn[:, t, :], x[:, t, :], rstd[:, t:t + 1], None, ALU.mult).then_inc(xn_ready, 1)
            dve.wait_ge(vec_t, 1)
            V.tensor_copy(cT[:, :], ps[:, 7, 0:VEC]).then_inc(vec_c, 1)
            dve.wait_ge(silu_ready, 1)
            for g in range(2):
                ins = V.tensor_tensor(cs[:, :, 16 * g:16 * g + 16],
                                      cT[:, 8 * g:8 * g + 8].unsqueeze(2).to_broadcast([P, KB, 16]),
                                      misc[:, 8 * g:8 * g + 8].unsqueeze(2).to_broadcast([P, KB, 16]), ALU.mult)
            ins.then_inc(silu_ready, 1)

            def mod_rows(m, bank):
                dve.wait_ge(pro_used, (C_ADA0, C_ADA1, C_ADA2)[m] + KB)
                dve.wait_ge(L["bada"], 64)
                V.tensor_tensor(modrow[:, m, :], ps[:, bank, :], bada[:, m, :], ALU.add).then_inc(row_ready, 1)

            mod_rows(0, 0)
            dve.wait_ge(modT_done, 1)
            link(V.tensor_copy(modT, ps[:, 5, :].rearrange("p (a b) -> p a b", a=4)))
            for g in range(2):
                for hi in range(2):
                    at = 64 + 32 * hi + 16 * g
                    ins = V.scalar_tensor_tensor(out=Am[:, g, 4 * hi:4 * hi + 4], in0=modT[:, :, at], scalar=1.0,
                                                 in1=cT[:, 16 + 4 * hi:20 + 4 * hi], op0=ALU.add, op1=ALU.mult)
            ins.then_inc(A_ready, 1)
            dve.wait_ge(A_ready, 2)
            dve.wait_ge(x_t, 2)
            for t in range(2):
                for j in range(4):
                    V.tensor_scalar(hTm[:, j, t * P:(t + 1) * P], ps[:, 1 + 2 * t, j * P:(j + 1) * P],
                                    Am[:, t, j:j + 1], modT[:, j, 16 * t:16 * t + 1], ALU.mult,
                                    ALU.add).then_inc(hT_ready, 1)
            dve.sem_inc(pooled_ready, 1)

            dve.wait_ge(S_done, 1)
            link(V.tensor_reduce(mx[:, 0, :], ps[:, 4:6, :].rearrange("p a (b n) -> p (a b) n", b=4), AX.X, ALU.max))
            V.tensor_scalar(mx[:, 0, :], mx[:, 0, :], -SCALE, None, ALU.mult).then_inc(mx_ready, 1)
            dve.wait_ge(S_done, 2)
            dve.wait_ge(bias_ready, 1)
            for b in range(2):
                V.scalar_tensor_tensor(out=Ss[:, 4 * b:4 * b + 4, 0:P],
                                       in0=ps[:, 6 + b, :].rearrange("p (a b) -> p a b", a=4), scalar=SCALE,
                                       in1=biasM[:, 4 * b:4 * b + 4, :], op0=ALU.mult, op1=ALU.add)\
                    .then_inc(S_read, 1)

            def normalise(n, S, width):
                dve.wait_ge(exp_done, HEADS * (n + 1))
                link(V.reciprocal(rsum[:, n, :], ssum[:, n, :]))
                V.tensor_tensor(S, S, rsum[:, n, :].unsqueeze(2).to_broadcast([P, HEADS, width]),
                                ALU.mult).then_inc(prob_ready, 1)

            normalise(0, Sp, P)
            dve.wait_ge(S_done, 3)
            for b in range(2):
                link(V.tensor_scalar(Ss[:, 4 * b:4 * b + 4, P:TOK],
                                     ps[:, 4 + b, :].rearrange("p (a b) -> p a b", a=4), SCALE, None, ALU.mult))
            V.tensor_reduce(mx[:, 1, :], Ss, AX.X, ALU.max, negate=True).then_inc(mx_ready, 1)
            dve.wait_ge(z_read, 4)
            link(V.memset(pscr[:, :, :, :], 0.0))
            for g in range(4):
                src = upad[:, g, :, :]
                for s in range(g + 1):
                    dst = pscr[:, s % 2, :, :]
                    link(doubled(dst, src, s))
                    src = dst
                if g == 0:
                    link(V.reciprocal(cnt[:, :, PAD:PAD + P], cnt[:, :, PAD:PAD + P]))
                o = pooled[:, g, :].rearrange("p (t n) -> p t n", t=2)
                link(V.tensor_tensor(o, src[:, :, PAD:PAD + P],
                                     cnt[:, g:g + 1, PAD:PAD + P].to_broadcast([P, 2, P]), ALU.mult))
                ins = V.tensor_tensor(o, o, upad[:, g, :, PAD:PAD + P], ALU.subtract)
                if g < 3:
                    link(ins)
            ins.then_inc(pooled_ready, 1)
            normalise(1, Ss, TOK)

            mod_rows(1, 6)
            mod_rows(2, 7)
            dve.wait_ge(L["gffn"], 16)
            for t in range(2):
                dve.wait_ge(bc_done, 3 + t)
                b = 4 * t
                V.scalar_tensor_tensor(out=Af[:, t, :], in0=ps[:, b:b + 2, :].rearrange("p a b -> p (a b)"), scalar=1.0,
                                       in1=gffn, op0=ALU.add, op1=ALU.mult).then_inc(Af_ready, 1)
            for j in range(KB):
                dve.wait_ge(br_done, j + 1)
                b = 4 + j % 4
                V.tensor_tensor(sgA[:, j, :], ps[:, b, 0:TOK], sgA[:, j, :], ALU.mult)
                link(V.tensor_tensor(sgB[:, j, :], ps[:, b, TOK:HALF], sgB[:, j, :], ALU.mult))
                V.tensor_tensor(sgA[:, j, :], sgA[:, j, :], sgB[:, j, :], ALU.add).then_inc(merged_ready, 1)
            dve.wait_ge(moe_free, 12)
            dve.wait_ge(bc_read, 2)
            for t in range(2):
                for n in range(2):
                    c = slice(n * HALF, (n + 1) * HALF)
                    link(V.tensor_tensor(tmp[:, n, :], ps[:, 2 * t + n, :], gtm[:, t, c], ALU.mult))
                    ins = V.tensor_tensor(x[:, t, c], x[:, t, c], tmp[:, n, :], ALU.add)
                ins.then_inc(x2_ready, 1)
            rsqrt_of_mean(2)
            for t in range(2):
                link(V.scalar_tensor_tensor(out=h2[:, t, :], in0=x[:, t, :], scalar=rstd[:, t:t + 1],
                                            in1=Af[:, t, :], op0=ALU.mult, op1=ALU.mult))
                V.tensor_tensor(h2[:, t, :], h2[:, t, :], shf[:, t, :], ALU.add).then_inc(h2_ready, 1)
            dve.wait_ge(h2_ready, 2)
            dve.sem_inc(moe_free, 4)
            dve.wait_ge(const_ready, 3)

            dve.wait_ge(L["brt"], 16)
            for t in range(2):
                dve.wait_ge(logit_done, t + 1)
                R = [rt[:, t, n, :] for n in range(8)]
                link(V.tensor_tensor(R[0], ps[:, t, 0:E], brt[:, :], ALU.add))
                link(V.max(top8[:, t, :], R[0]))
                V.tensor_scalar(misc[:, 4 + t:5 + t], top8[:, t, 0:1], -1.0, None, ALU.mult).then_inc(top_ready, 1)
                fourth = top8[:, t, TOPK - 1:TOPK]
                link(V.tensor_scalar(R[2], R[0], fourth, None, ALU.is_gt))
                link(V.tensor_reduce(misc[:, 6 + t:7 + t], R[2], AX.X, ALU.add))
                link(V.tensor_scalar(R[3], R[0], fourth, None, ALU.is_equal))
                link(V.tensor_tensor_scan(R[4], ones[:, 0:E], R[3], misc[:, 6 + t:7 + t], ALU.mult, ALU.add))
                link(V.tensor_scalar(R[4], R[4], float(TOPK), None, ALU.is_le))
                link(V.tensor_tensor(R[3], R[3], R[4], ALU.mult))
                V.tensor_tensor(R[5], R[2], R[3], ALU.add).then_inc(mask_ready, 1)
            for t in range(2):
                R = [rt[:, t, n, :] for n in range(8)]
                dve.wait_ge(mask_ready, t + 1)
                dve.wait_ge(e_ready, t + 1)
                link(V.tensor_tensor(R[6], R[1], R[5], ALU.mult))
                link(V.tensor_reduce(misc[:, 2 + t:3 + t], R[6], AX.X, ALU.add))
                link(V.reciprocal(misc[:, 2 + t:3 + t], misc[:, 2 + t:3 + t]))
                V.tensor_scalar(R[6], R[6], misc[:, 2 + t:3 + t], None, ALU.mult).then_inc(comb_ready, 1)
            dve.wait_ge(comb_ready, 2)
            link(V.memset(tab[:, PAIRS, :], -1.0))
            for t in range(2):
                dve.wait_ge(rank_done, t + 1)
                R = [rt[:, t, n, :] for n in range(8)]
                pairs = tab[:, 0:PAIRS, :]
                link(V.tensor_scalar(R[7], ps[:, 2 + t, 0:E], 1.0, None, ALU.add))
                link(V.tensor_tensor(R[7], R[7], R[5], ALU.mult))
                link(V.tensor_scalar(pairs[:, :, 2 * t:2 * t + 2], R[7].rearrange("p (a b) -> p a b", b=2), 1.0, None,
                                     ALU.subtract))
                link(V.tensor_copy(pairs[:, :, 4 + 2 * t:6 + 2 * t], R[6].rearrange("p (a b) -> p a b", b=2)))
            link(V.tensor_reduce(misc[:, 9:10], ps[:, 3, E:2 * E], AX.X, ALU.max))
            for r in range(ROUNDS):
                ins = V.tensor_scalar(flags[:, r:r + 1], misc[:, 9:10], float(CAP * r), None, ALU.is_gt)
            ins.then_inc(flag_ready, 1)
            dve.wait_ge(bd_done, 1)
            for t in range(2):
                ins = V.tensor_copy(acc[:, t, :], ps[:, 4 + 2 * t:6 + 2 * t, :].rearrange("p a b -> p (a b)"))
            link(ins)

            def one_hots(p, G):
                V.tensor_copy(cur[:, :], tab[:, bass.ds(p, 1), :].rearrange("p a b -> p (a b)")).then_inc(cur_ready, 1)
                dve.wait_ge(cur_ready, G + 1)
                for t in range(2):
                    for a in range(2):
                        ins = V.tensor_scalar(oh[:, t, CAP * a:CAP * a + CAP], iota[:, :], cur[:, 2 * t + a:2 * t + a + 1],
                                              None, ALU.is_equal)
                ins.then_inc(oh_ready, 1)

            def add_acc(Pn, n):
                t, c = n // 2, slice((n % 2) * HALF, (n % 2 + 1) * HALF)
                dve.wait_ge(scat_done, Pn * 4 + (n + 1))
                V.tensor_tensor(acc[:, t, c], ps[:, GB + n, :], acc[:, t, c], ALU.add).then_inc(acc_done, 1)

            def body(I, i, r):
                P0 = dve.snap(I * BODY)
                G0 = dve.snap(P0 + (r + 1))
                p0 = dve.snap(i * BODY)
                n0 = dve.snap(I * BC)
                for h in range(BODY):
                    Pn, G = P0 + h, G0 + h
                    dve.wait_ge(woT_done, Pn + 1)
                    dve.wait_ge(oh_ready, G)
                    for t in range(2):
                        for a in range(2):
                            ins = V.tensor_scalar(wo[:, t, CAP * a:CAP * a + CAP], oh[:, t, CAP * a:CAP * a + CAP],
                                                  cur[:, 4 + 2 * t + a:5 + 2 * t + a], None, ALU.mult)
                    ins.then_inc(wo_ready, 1)
                    dve.wait_ge(wo_ready, Pn + 1)
                    dve.wait_ge(gath_done, G * 2)
                    one_hots(p0 + (h + 1), G)
                    dve.wait_ge(moe_free, n0 + (RING + h * PC + UPC))
                    for b in range(2):
                        V.tensor_scalar(gate[:, b * HALF:(b + 1) * HALF], ps[:, b, :], LIMIT, None,
                                        ALU.min).then_inc(g_ready, 1)
                    V.tensor_scalar(hid, ps[:, 2:4, :].rearrange("p a b -> p (a b)"), LIMIT, -LIMIT, ALU.min,
                                    ALU.max).then_inc(u_read, 1)
                    add_acc(Pn, 0)
                    add_acc(Pn, 1)
                    dve.wait_ge(u_read, Pn + 2)
                    for b in range(2):
                        c = slice(b * HALF, (b + 1) * HALF)
                        dve.wait_ge(sig_ready, Pn * 2 + (b + 1))
                        V.tensor_tensor(sig[:, c], sig[:, c], gate[:, c], ALU.mult).then_inc(glu_ready, 1)
                        dve.wait_ge(glu_ready, Pn * 2 + (b + 1))
                        V.scalar_tensor_tensor(out=hid[:, c], in0=hid[:, c], scalar=1.0, in1=sig[:, c],
                                               op0=ALU.add, op1=ALU.mult).then_inc(hid_ready, 1)
                    add_acc(Pn, 2)
                    add_acc(Pn, 3)

            V.memset(woT, 0.0).then_inc(woT_ready, 1)
            V.memset(yb, 0.0).then_inc(y_ready, 1)
            V.memset(wo, 0.0).then_inc(u_read, 1)
            one_hots(0, 0)
            with dve.Fori(0, PAIRS // BODY) as i:
                body(i, i, 0)

            def run(r):
                dve.wait_ge(oh_ready, r * (PAIRS + 1))
                V.tensor_scalar(tab[:, :, 0:4], tab[:, :, 0:4], float(CAP), None, ALU.subtract).then_inc(tab_ready, 1)
                dve.wait_ge(tab_ready, r)
                dve.wait_ge(gath_done, 2 * r * (PAIRS + 1))
                one_hots(0, r * (PAIRS + 1))
                with dve.Fori(0, PAIRS // BODY) as i:
                    body(i + r * (PAIRS // BODY), i, r)
            further_rounds(dve, run)

            for n in range(4):
                t, c = n // 2, slice((n % 2) * HALF, (n % 2 + 1) * HALF)
                dve.wait_ge(last_scat, n + 1)
                link(V.tensor_tensor(acc[:, t, c], ps[:, GB + n, :], acc[:, t, c], ALU.add))
                link(V.tensor_tensor(acc[:, t, c], acc[:, t, c], gtf[:, t, c], ALU.mult))
                ins = V.tensor_tensor(x[:, t, c], x[:, t, c], acc[:, t, c], ALU.add)
                if n % 2:
                    ins.then_inc(fin_ss, 1)
            rsqrt_of_mean(3)
            dve.wait_ge(L["gfin"], 16)
            for t in range(2):
                V.scalar_tensor_tensor(out=x[:, t, :], in0=x[:, t, :], scalar=rstd[:, t:t + 1], in1=gfin,
                                       op0=ALU.mult, op1=ALU.mult).then_inc(fin_ready, 1)

        @block.tensor
        def _(pe):
            mm, tp = nc.tensor.matmul, nc.tensor.transpose

            def landed(c):
                pe.wait_ge(pro_loaded[c % RING0], 16 * (c // RING0 + 1))
                return ring[:, c % RING0, :]

            pe.wait_ge(L["vec"], 64)
            pe.wait_ge(const_ready, 1)
            tp(ps[:, 7, 0:VEC], vecs[:, :], ident[0:VEC, 0:VEC]).then_inc(vec_t, 1)
            pe.wait_ge(L["kc"], 16)
            for b in range(4):
                ins = tp(ps[:, 6, b * P:(b + 1) * P], kc[:, b * P:(b + 1) * P], ident[:, :])
            ins.then_inc(kc_t, 1)
            for t in range(2):
                pe.wait_ge(xn_ready, t + 1)
                for j in range(KB):
                    ins = tp(ps[:, 1 + 2 * t + j // 4, (j % 4) * P:(j % 4 + 1) * P], xn[:, t, j * P:(j + 1) * P], ident[:, :])
                ins.then_inc(x_t, 1)

            pe.wait_ge(L["rpb"], 16 * 8)
            pe.wait_ge(const_ready, 2)
            pe.wait_ge(kcT_ready, 1)
            pe.wait_ge(vec_c, 1)
            for b in range(2):
                ins = mm(ps[:, 6 + b, :], flip, bias_rev[:, 4 * b:4 * b + 4, :], start=True, stop=True)
            ins.then_inc(bias_t, 1)

            def modulation(m, bank, c0):
                for kk in range(KB):
                    w = landed(c0 + kk)
                    for q in range(4):
                        ins = mm(ps[32 * q:32 * q + 32, bank, :], cs[:, kk, :], w[:, q * HALF:(q + 1) * HALF],
                                 start=(kk == 0), stop=(kk == KB - 1))
                    ins.then_inc(pro_used, 1)

            pe.wait_ge(silu_ready, 2)
            modulation(0, 0, C_ADA0)
            pe.wait_ge(row_ready, 1)
            for j in range(4):
                ins = tp(ps[:, 5, j * P:(j + 1) * P], modrow[:, 0, j * P:(j + 1) * P], ident[:, :])
            ins.then_inc(modT_done, 1)
            pe.wait_ge(hT_ready, 16)

            def project(cc):
                if cc >= 2:
                    pe.wait_ge(z_read, cc - 1)
                bank = 2 * (cc % 2)
                w = [landed(C_IN + 2 * cc + s).rearrange("p (k n) -> p k n", k=4) for s in range(2)]
                for b in range(2 if cc == 2 else 4):
                    for kk in range(KB):
                        wk = w[kk // 4][:, kk % 4, :]
                        if cc == 2:
                            ins = mm(ps[:, bank + b, :], hTm[:, kk, b * P:(b + 1) * P], wk,
                                     start=(kk == 0), stop=(kk == KB - 1))
                        else:
                            ins = mm(ps[:, bank + b // 2, (b % 2) * TOK:(b % 2 + 1) * TOK], wk[:, b * P:(b + 1) * P],
                                     hTm[:, kk, :], start=(kk == 0), stop=(kk == KB - 1))
                        if b == (1 if cc == 2 else 3) and kk == 3:
                            ins.then_inc(pro_used, 1)
                ins.then_inc(pro_used, 1)

            def scores(n, keys, bank):
                for h in range(HEADS):
                    b, o = h // 2, DH * (h % 2)
                    ins = mm(ps[:, bank + h % 2, b * P:(b + 1) * P], qT[o:o + DH, b, (n > 0) * P:(n > 0) * P + P],
                             keys[o:o + DH, b, :], start=True, stop=True)
                ins.then_inc(S_done, 1)

            def prob_t(src, bank):
                for hh in range(HEADS):
                    ins = tp(ps[:, bank + hh // 4, (hh % 4) * P:(hh % 4 + 1) * P], src[:, hh, :], ident[:, :])
                ins.then_inc(PT_done, 1)

            project(0)
            project(1)
            project(2)
            pe.wait_ge(z_read, 2)
            scores(0, kT[:, :, 0:P], 4)
            pe.wait_ge(kcT_ready, 1)
            scores(1, kT[:, :, P:TOK], 6)
            project(3)
            pe.wait_ge(exp_done, HEADS)
            scores(2, kcT, 4)
            pe.wait_ge(S_read, 2)
            for b in range(4):
                ins = tp(ps[:, 6, b * P:(b + 1) * P], kT[:, b, 0:P], ident[:, :])
            ins.then_inc(k_t, 1)
            project(4)
            pe.wait_ge(prob_ready, 1)
            pe.wait_ge(knew_ready, 1)
            prob_t(Sp, 6)
            project(5)
            pe.wait_ge(prob_ready, 2)
            prob_t(Ss[:, :, 0:P], 4)
            project(6)
            pe.wait_ge(PT_read, 1)
            prob_t(Ss[:, :, P:TOK], 6)
            project(7)
            pe.wait_ge(PT_read, 3)
            pe.wait_ge(z_read, 7)
            pe.wait_ge(L["vc"], 16)
            for b in range(4):
                for par in range(2):
                    h, hh, o = 2 * b + par, 4 * par + b, DH * par
                    mm(ps[o:o + DH, 0, b * P:(b + 1) * P], vm[:, 0, h * DH:(h + 1) * DH], PTp[:, hh, :], start=True, stop=True)
            for b in range(4):
                for par in range(2):
                    h, hh, o = 2 * b + par, 4 * par + b, DH * par
                    mm(ps[o:o + DH, 1, b * P:(b + 1) * P], vm[:, 1, h * DH:(h + 1) * DH], PTs[:, 0, hh, :], start=True, stop=False)
                    ins = mm(ps[o:o + DH, 1, b * P:(b + 1) * P], vc[:, h * DH:(h + 1) * DH], PTs[:, 1, hh, :],
                             start=False, stop=True)
            ins.then_inc(O_done, 1)
            pe.wait_ge(pooled_ready, 2)
            pe.wait_ge(L["wpool"], 16)
            for g in range(4):
                ins = mm(ps[:, 4 + g // 2, (g % 2) * TOK:(g % 2 + 1) * TOK], wpool[:, g, :], pooled[:, g, :],
                         start=True, stop=True)
            ins.then_inc(pool_done, 1)
            pe.wait_ge(pool_done, 1)
            pe.sem_inc(moe_free, 3)

            modulation(1, 6, C_ADA1)
            modulation(2, 7, C_ADA2)
            pe.wait_ge(pro_used, C_PA)
            pe.sem_inc(moe_free, 1)
            pe.wait_ge(const_ready, 3)
            for n in range(4):
                m, t = n // 2, n % 2
                b = 4 * (n % 2)
                pe.wait_ge(row_ready, 3)
                if n == 0:
                    pe.wait_ge(oT_ready, 1)
                    pe.wait_ge(z_read, 8)
                    pe.wait_ge(kv_stored, 32)
                if n == 1:
                    pe.wait_ge(yT_ready, 1)
                if n >= 2:
                    pe.wait_ge(bc_read, n - 1)
                for q in range(4):
                    ins = mm(ps[:, b + q, :], selrow[32 * q:32 * q + 32, t, :], modrow[32 * q:32 * q + 32, 1 + m, :],
                             start=True, stop=True)
                ins.then_inc(bc_done, 1)
            wa = [landed(C_PA + s).rearrange("p (k n) -> p k n", k=2) for s in range(2)]
            wb = [landed(C_PB + s).rearrange("p (k n) -> p k n", k=2) for s in range(2)]
            pe.wait_ge(bc_read, 4)
            pe.wait_ge(Af_ready, 2)
            for j in range(KB):
                if j >= 4:
                    pe.wait_ge(merged_ready, j - 3)
                for half, (w, src) in enumerate(((wa, yT), (wb, oT))):
                    for kk in range(4):
                        ins = mm(ps[:, 4 + j % 4, half * TOK:(half + 1) * TOK], w[kk // 2][:, kk % 2, j * P:(j + 1) * P],
                                 src[:, kk, :], start=(kk == 0), stop=(kk == 3))
                ins.then_inc(br_done, 1)
            pe.wait_ge(br_done, KB)
            pe.sem_inc(moe_free, 4)
            for kk in range(KB):
                c = C_OUT + kk // 2
                w = landed(c).rearrange("p (k n) -> p k n", k=2)
                pe.wait_ge(merged_ready, kk + 1)
                for t in range(2):
                    for n in range(2):
                        ins = mm(ps[:, 2 * t + n, :], sgA[:, kk, t * P:(t + 1) * P], w[:, kk % 2, n * HALF:(n + 1) * HALF],
                                 start=(kk == 0), stop=(kk == KB - 1))
                if kk % 2:
                    ins.then_inc(moe_free, 1)
            for t in range(2):
                pe.wait_ge(h2_ready, t + 1)
                for j in range(KB):
                    ins = tp(ps[:, 4 + 2 * t + j // 4, (j % 4) * P:(j % 4 + 1) * P], h2[:, t, j * P:(j + 1) * P], ident[:, :])
                    if j % 4 == 3:
                        ins.then_inc(h2_t, 1)
            pe.wait_ge(L["wrt"], 16)
            for t in range(2):
                pe.wait_ge(h2T_ready, 2 * t + 2)
                for kk in range(KB):
                    ins = mm(ps[:, t, 0:E], h2T[:, kk, t * P:(t + 1) * P], wrt[:, kk, :],
                             start=(kk == 0), stop=(kk == KB - 1))
                ins.then_inc(logit_done, 1)
            pe.wait_ge(mask_ready, 1)
            mm(ps[:, 2, 0:E], tri[:, :], rt[:, 0, 5, :], start=True, stop=True).then_inc(rank_done, 1)
            pe.wait_ge(mask_ready, 2)
            mm(ps[:, 3, 0:E], ones[:, :], rt[:, 0, 5, :], start=True, stop=False)
            mm(ps[:, 3, 0:E], tri[:, :], rt[:, 1, 5, :], start=False, stop=True)
            mm(ps[:, 3, E:2 * E], ones[:, :], rt[:, 0, 5, :], start=True, stop=False)
            mm(ps[:, 3, E:2 * E], ones[:, :], rt[:, 1, 5, :], start=False, stop=True).then_inc(rank_done, 1)
            pe.wait_ge(comb_ready, 2)
            for t in range(2):
                ins = tp(ps[0:E, 1, t * P:(t + 1) * P], rt[:, t, 6, :], ident[:, :])
            ins.then_inc(comb_t, 1)
            pe.wait_ge(combT_ready, 1)
            pe.wait_ge(L["bdn"], 16)
            for t in range(2):
                for n in range(2):
                    ins = mm(ps[:, 4 + 2 * t + n, :], combT[:, t * P:(t + 1) * P], bdn[:, n * HALF:(n + 1) * HALF],
                             start=True, stop=True)
            ins.then_inc(bd_done, 1)

            def gather(G):
                pe.wait_ge(oh_ready, G + 1)
                for j in range(KB):
                    for t in range(2):
                        ins = mm(ps[:, GB + j // 4, (j % 4) * P:(j % 4 + 1) * P], h2[:, t, j * P:(j + 1) * P],
                                 oh[:, t, :], start=(t == 0), stop=(t == 1))
                    if j % 4 == 3:
                        ins.then_inc(gath_done, 1)

            def scatter(done):
                for n in range(4):
                    t = n // 2
                    mm(ps[:, GB + n, :], woT[:, t, :], yb[:, (n % 2) * HALF:(n % 2 + 1) * HALF],
                       start=True, stop=True).then_inc(done, 1)

            def body(I, r):
                P0 = pe.snap(I * BODY)
                G0 = pe.snap(P0 + (r + 1))
                lap0 = pe.snap(I * (16 * LAPS))

                def chunk(n):
                    pe.wait_ge(moe_loaded[n % RING], lap0 + 16 * (n // RING + 1))
                    return ring[:, ORDER[n % RING], :]

                for h in range(BODY):
                    Pn, G = P0 + h, G0 + h
                    pe.wait_ge(xg_ready, G * 2)
                    pe.wait_ge(u_read, Pn + 1)
                    pe.wait_ge(sel_ready, Pn + 1)
                    for n in range(4):
                        for a in range(2):
                            mm(ps[CAP * a:CAP * a + CAP, n, :], selbuf[:, a, :], bparts[:, n * HALF:(n + 1) * HALF],
                               start=True, stop=False)
                    for kk in range(KB):
                        w = [chunk(h * PC + 2 * kk + a) for a in range(2)]
                        for n in range(4):
                            for a in range(2):
                                ins = mm(ps[CAP * a:CAP * a + CAP, n, :], xgT[:, h, kk, CAP * a:CAP * a + CAP],
                                         w[a][:, n * HALF:(n + 1) * HALF], start=False, stop=(kk == KB - 1))
                                if n == 3:
                                    ins.then_inc(moe_free, 1)
                    pe.wait_ge(y_ready, Pn + 1)
                    pe.wait_ge(woT_ready, Pn + 1)
                    scatter(scat_done)
                    pe.wait_ge(acc_done, Pn * 4 + 2)
                    gather(G)
                    pe.wait_ge(wo_ready, Pn + 1)
                    pe.wait_ge(acc_done, Pn * 4 + 3)
                    for t in range(2):
                        ins = tp(ps[:, YB, t * P:(t + 1) * P], wo[:, t, :], ident[:, :])
                    ins.then_inc(woT_done, 1)
                    for f in range(KB):
                        if f % 4 == 0:
                            pe.wait_ge(hid_ready, Pn * 2 + (f // 4 + 1))
                            pe.wait_ge(xg_ready, G * 2 + (f // 4 + 1))
                        ins = tp(ps[:, GB + f // 4, (f % 4) * P:(f % 4 + 1) * P], hid[:, f * P:(f + 1) * P], ident[:, :])
                        if f % 4 == 3:
                            ins.then_inc(hT_done, 1)
                    pe.wait_ge(woT_ready, Pn + 2)
                    pe.wait_ge(acc_done, Pn * 4 + 4)
                    for f in range(KB):
                        if f % 4 == 0:
                            pe.wait_ge(hTe_ready, Pn * 2 + (f // 4 + 1))
                        if f % 2 == 0:
                            w = [chunk(h * PC + UPC + f + a) for a in range(2)]
                        for n in range(2):
                            for a in range(2):
                                ins = mm(ps[CAP * a:CAP * a + CAP, YB + n, :], hT[:, f, CAP * a:CAP * a + CAP],
                                         w[a][:, (f % 2) * D + n * HALF:(f % 2) * D + (n + 1) * HALF],
                                         start=(f == 0), stop=(f == KB - 1))
                                if f % 2 and n == 1:
                                    ins.then_inc(moe_free, 1)

            pe.sem_inc(woT_done, 1)
            gather(0)
            with pe.Fori(0, PAIRS // BODY) as i:
                body(i, 0)
            pe.wait_ge(y_ready, 1 + PAIRS)
            pe.wait_ge(woT_ready, 1 + PAIRS)

            def run(r):
                gather(r * (PAIRS + 1))
                with pe.Fori(0, PAIRS // BODY) as i:
                    body(i + r * (PAIRS // BODY), r)
                pe.wait_ge(y_ready, 1 + (r + 1) * PAIRS)
                pe.wait_ge(woT_ready, 1 + (r + 1) * PAIRS)
            further_rounds(pe, run)
            scatter(last_scat)


_INS = ['x_prompt', 'x_sample', 'cache_k', 'cache_v', 'c', 'c_ctx', 'w_ada', 'b_ada', 'g_mix', 'w_in', 'w_pool',
        'pool_scale', 'w_pa', 'w_pb', 'rpb', 'w_out', 'g_ffn', 'w_router', 'b_router', 'w_up', 'b_up', 'w_down',
        'b_down', 'g_final']
_OUTS = [((1, 128, 1024), 'float32'), ((1, 128, 1024), 'float32'),
         ((1, 1, 8, 128, 64), 'float32'), ((1, 1, 8, 128, 64), 'float32')]


def kernel(**inputs):
    import numpy as _np
    import concourse.bacc as _bacc
    from concourse import mybir as _mybir
    from concourse.bass_utils import run_bass_kernel_spmd as _run

    nc = _bacc.Bacc("TRN2", target_bir_lowering=False, num_devices=1)
    arrays, args = {}, []
    for name in _INS:
        a = _np.ascontiguousarray(inputs[name])
        arrays[f"in_{name}_dram"] = a
        args.append(nc.dram_tensor(f"in_{name}_dram", a.shape, _mybir.dt.from_np(a.dtype), kind="ExternalInput").ap())
    for i, (shape, dtype) in enumerate(_OUTS):
        dt = _mybir.dt.from_np(_np.dtype(dtype))
        args.append(nc.dram_tensor(f"out_{i}_dram", shape, dt, kind="ExternalOutput").ap())
    layer_kernel(nc, *args)
    r = _run(nc, [arrays], core_ids=[0])
    return tuple(r.results[0][f"out_{i}_dram"] for i in range(len(_OUTS)))
```

```python
from contextlib import ExitStack

import concourse.bass as bass
from concourse import mybir

F32 = mybir.dt.float32
BF16 = mybir.dt.bfloat16
I32 = mybir.dt.int32
ALU = mybir.AluOpType
ACT = mybir.ActivationFunctionType
AX = mybir.AxisListType

P = 128
D = 1024
KB = D // P
TOK = 2 * P
HEADS, DH = 8, 64
GRID_W, WIN_C, WIN_R = 64, 16, 8
RPB_W = 2 * WIN_C - 1
RPB_H = (2 * WIN_R - 1) * RPB_W
SCALE = DH ** -0.5
NEG = -1e30
EPS = 1e-6
E, TOPK, FF = 32, 4, 1024
LIMIT, ALPHA = 7.0, 1.702
HALF = 512
PAD = 8
PW = P + 2 * PAD

SLOT = 2048
RING = 16
RING0 = 9
ORDER = [10, 11, 12, 3, 4, 5, 6, 7, 8, 0, 1, 2, 9, 13, 14, 15]
CAP = 64
PAIRS = E // 2
ROUNDS = TOK // CAP
BODY = 2
UPC = 16
DNC = 8
PC = UPC + DNC
BC = BODY * PC
LAPS = BC // RING
VEC = 28

MIX = [("ada", 0, k) for k in range(KB)]
for _j in range(4):
    MIX += [("in", _j, 0), ("in", _j, 1)] + [("ada", 1 + _j // 2, 4 * (_j % 2) + k) for k in range(4)]
MIX += [("in", j, h) for j in range(4, 8) for h in range(2)]
MIX += [("pa", 0, h) for h in range(2)] + [("pb", 0, h) for h in range(2)] + [("out", 0, h) for h in range(4)]
AT = {key: n for n, key in enumerate(MIX)}


def layer_kernel(nc, A_x_prompt, A_x_sample, A_cache_k, A_cache_v, A_c, A_c_ctx, A_w_ada, A_b_ada, A_g_mix,
                 A_w_in, A_w_pool, A_pool_scale, A_w_pa, A_w_pb, A_rpb, A_w_out, A_g_ffn, A_w_router,
                 A_b_router, A_w_up, A_b_up, A_w_down, A_b_down, A_g_final,
                 y_prompt, y_sample, new_k, new_v):
    w_in_v = A_w_in[0].rearrange("(k p) n -> p k n", p=P)
    w_ada_v = A_w_ada[0].rearrange("(k p) n -> p k n", p=P)
    w_pa_v = A_w_pa[0].rearrange("(k p) n -> p k n", p=P)
    w_pb_v = A_w_pb[0].rearrange("(k p) n -> p k n", p=P)
    w_out_v = A_w_out[0].rearrange("(k p) n -> p k n", p=P)
    w_up_v = A_w_up[0].rearrange("e (k p) n -> e p k n", p=P)
    w_down_v = A_w_down[0].rearrange("e (k p) n -> e p k n", p=P)

    with ExitStack() as ctx:
        def sb(name, shape, dt=F32):
            return ctx.enter_context(nc.sbuf_tensor(name, shape, dt))

        def sem(name):
            return ctx.enter_context(nc.semaphore(name))

        ring = sb("ring", [P, RING, SLOT])
        arena = sb("arena", [P, 13056])
        x = sb("x", [P, 2, D])
        gtf = sb("gtf", [P, 2, D])
        bparts = sb("bparts", [96, 2 * FF], BF16)
        sel = sb("sel", [96, E], BF16)
        selbuf = sb("selbuf", [96, 2, CAP], BF16)
        ident = sb("ident", [P, P])
        iota = sb("iota", [P, CAP])
        iota_i = sb("iota_i", [P, CAP], I32)
        tab = sb("tab", [P, PAIRS + 1, 8])
        cur = sb("cur", [P, 8])
        small = sb("small", [P, 256])
        flags = sb("flags", [P, 4], I32)
        mhalf = sb("mhalf", [P, 1])

        def region(at, *shape):
            n = 1
            for s in shape:
                n *= s
            ap = arena[:, at:at + n]
            if len(shape) == 2:
                ap = ap.rearrange("p (a b) -> p a b", a=shape[0])
            if len(shape) == 3:
                ap = ap.rearrange("p (a b c) -> p a b c", a=shape[0], b=shape[1])
            return ap

        def in_slot(s, at, *shape):
            n = 1
            for v in shape:
                n *= v
            ap = ring[:, s, at:at + n]
            if len(shape) == 2:
                ap = ap.rearrange("p (a b) -> p a b", a=shape[0])
            if len(shape) == 3:
                ap = ap.rearrange("p (a b c) -> p a b c", a=shape[0], b=shape[1])
            return ap

        acc = region(0, 2, D)
        h2 = region(2048, 2, D)
        xgT = region(4096, 2, KB, P)
        oh = region(6144, 2, P)
        wo = region(6400, 2, P)
        woT = region(6656, 2, P)
        gate = region(6912, D)
        sig = region(7936, D)
        hid = region(8960, D)
        hT = region(9984, KB, P)
        yb = region(11008, D)
        sgA = region(0, KB, TOK)
        sgB = region(2048, KB, TOK)
        PTp = region(4096, HEADS, P)
        PTs = region(5120, 2, HEADS, P)
        xn = region(4096, 2, D)
        oT = region(7168, 4, TOK)
        pooled = region(8192, 4, TOK)
        yT = region(9216, 4, TOK)
        modrow = region(10240, 3, HALF)
        modT = region(11776, 4, P)
        knew = region(12288, HALF)
        h2T = region(4096, KB, TOK)
        bup = region(0, 2 * FF)
        brem = region(2048, 2 * FF)
        bada = gtf[:, :, :].rearrange("p a b -> p (a b)")[:, 0:3 * HALF].rearrange("p (a b) -> p a b", a=3)
        tmp = region(8192, 2, D)
        gfin = region(12032, D)
        hTm = in_slot(10, 0, KB, TOK)
        biasM = in_slot(11, 0, HEADS, P)
        bias_rev = in_slot(13, 0, HEADS, P)
        flip = in_slot(12, 1664, P)
        kc = in_slot(11, 1024, HALF)
        vc = in_slot(11, 1536, HALF)
        upad = in_slot(12, 0, 4, 2, PW)
        kcT = in_slot(12, 1152, 4, P)
        Ss = in_slot(13, 0, HEADS, TOK)
        qT = in_slot(14, 0, 4, TOK)
        kT = in_slot(14, 1024, 4, TOK)
        Sp = in_slot(15, 0, HEADS, P)
        vm = in_slot(15, 1024, 2, HALF)
        gtm = in_slot(14, 0, 2, D)
        Af = in_slot(13, 0, 2, D)
        shf = in_slot(15, 0, 2, D)

        vecs = sb("vecs", [VEC, P])
        cT = sb("cT", [P, VEC])
        gffn = in_slot(9, 0, D)
        cs = in_slot(9, 1024, KB, 32)
        wpool = in_slot(9, 1280, 4, P)
        pscr = region(6144, 2, 2, PW)
        cnt = region(6720, 4, PW)
        wrt = sb("wrt", [P, KB, E])
        brt = sb("brt", [P, E])
        selrow = sb("selrow", [P, 2, P])
        tri = sb("tri", [P, P])
        ones = sb("ones", [P, P])
        rt = sb("rt", [P, 2, 8, E])

        Am = small[:, 0:16].rearrange("p (g k) -> p g k", g=2)
        ssq = small[:, 16:18]
        rstd = small[:, 18:20]
        mx = small[:, 20:36].rearrange("p (a b) -> p a b", a=2)
        ssum = small[:, 36:52].rearrange("p (a b) -> p a b", a=2)
        rsum = small[:, 52:68].rearrange("p (a b) -> p a b", a=2)
        top8 = small[:, 68:84].rearrange("p (a b) -> p a b", a=2)
        misc = small[:, 84:100]

        ps = ctx.enter_context(nc.psum_tensor("ps", [P, 8, HALF], F32))

        pro_loaded = [sem(f"pro_loaded{s}") for s in range(RING0)]
        moe_loaded = [sem(f"moe_loaded{s}") for s in range(RING)]
        pro_used, moe_free = sem("pro_used"), sem("moe_free")
        L = {n: sem("ld_" + n) for n in ("vec", "x0", "x1", "bada", "bup", "gffn", "rpb", "kc", "vc", "wpool",
                                         "wrt", "brt", "bdn", "gfin")}
        pool_step, dve_step, act_step = sem("pool_step"), sem("dve_step"), sem("act_step")
        const_ready, bias_ready, split_done = sem("const_ready"), sem("bias_ready"), sem("split_done")
        vec_t, vec_c, silu_ready = sem("vec_t"), sem("vec_c"), sem("silu_ready")
        ssq_ready, root_ready, xn_ready = sem("ssq_ready"), sem("root_ready"), sem("xn_ready")
        kc_t, kcT_ready, x_t = sem("kc_t"), sem("kcT_ready"), sem("x_t")
        row_ready, modT_done, A_ready = sem("row_ready"), sem("modT_done"), sem("A_ready")
        hT_ready, hT_ready2, z_read = sem("hT_ready"), sem("hT_ready2"), sem("z_read")
        S_done, S_read, mx_ready, exp_done = sem("S_done"), sem("S_read"), sem("mx_ready"), sem("exp_done")
        prob_ready, PT_done, PT_read = sem("prob_ready"), sem("PT_done"), sem("PT_read")
        k_t, knew_ready = sem("k_t"), sem("knew_ready")
        O_done, oT_ready, pooled_ready, pool_done, yT_ready = (sem("O_done"), sem("oT_ready"), sem("pooled_ready"),
                                                               sem("pool_done"), sem("yT_ready"))
        bc_done, bc_read, Af_ready = sem("bc_done"), sem("bc_read"), sem("Af_ready")
        br_done, br_read, merged_ready = sem("br_done"), sem("br_read"), sem("merged_ready")
        x2_ready, h2_ready, h2_t, h2T_ready = sem("x2_ready"), sem("h2_ready"), sem("h2_t"), sem("h2T_ready")
        logit_done, mask_ready, rank_done, e_ready, top_ready = (sem("logit_done"), sem("mask_ready"),
                                                                 sem("rank_done"), sem("e_ready"), sem("top_ready"))
        comb_ready, comb_t, out_done, zeroed, acc_zero, mean_ready = (sem("comb_ready"), sem("comb_t"), sem("out_done"),
                                                                      sem("zeroed"), sem("acc_zero"), sem("mean_ready"))
        flag_ready, tab_ready = sem("flag_ready"), sem("tab_ready")
        oh_ready, wo_ready, gath_done, xg_ready, sel_ready = (sem("oh_ready"), sem("wo_ready"), sem("gath_done"),
                                                              sem("xg_ready"), sem("sel_ready"))
        u_read, g_ready, sig_ready, hid_ready = sem("u_read"), sem("g_ready"), sem("sig_ready"), sem("hid_ready")
        scat_done, acc_done, woT_done, woT_ready = sem("scat_done"), sem("acc_done"), sem("woT_done"), sem("woT_ready")
        hT_done, hTe_ready, y_ready = sem("hT_done"), sem("hTe_ready"), sem("y_ready")
        cur_ready, glu_ready = sem("cur_ready"), sem("glu_ready")
        fin_ss, fin_ready, last_scat, stored = sem("fin_ss"), sem("fin_ready"), sem("last_scat"), sem("stored")
        kv_stored, bias_t, bias_copied = sem("kv_stored"), sem("bias_t"), sem("bias_copied")

        GB, YB = 4, 6

        block = ctx.enter_context(nc.Block())

        def further_rounds(eng, run):
            eng.wait_ge(flag_ready, 1)
            for r in range(1, ROUNDS):
                more = eng.value_load(flags[0:1, r:r + 1], min_val=0, max_val=1)
                with eng.If(more > 0):
                    run(r)

        @block.sync
        def _(sp):
            def mixing_chunk(c):
                s = ring[:, c % RING0, :]
                kind, m, k = MIX[c]
                if kind == "ada":
                    return s, w_ada_v[:, k, m * SLOT:(m + 1) * SLOT]
                if kind == "in":
                    return (s.rearrange("p (k n) -> p k n", k=4),
                            w_in_v[:, 4 * k:4 * k + 4, m * HALF:(m + 1) * HALF])
                w = {"pa": w_pa_v, "pb": w_pb_v, "out": w_out_v}[kind]
                return s.rearrange("p (k n) -> p k n", k=2), w[:, 2 * k:2 * k + 2, :]

            for row, src in ((0, A_c_ctx), (8, A_c[0]), (16, A_g_mix[0])):
                sp.dma_start(vecs[row:row + 8, :], src.rearrange("(k p) -> k p", p=P)).then_inc(L["vec"], 16)
            sp.dma_start(vecs[24:28, :], A_pool_scale[0].rearrange("(k p) -> k p", p=P)).then_inc(L["vec"], 16)
            for c in range(len(MIX)):
                if c >= RING0:
                    sp.wait_ge(pro_used, c - RING0 + 1)
                if c == 2:
                    sp.dma_start(x[:, 0, :], A_x_prompt[0]).then_inc(L["x0"], 16)
                    sp.dma_start(x[:, 1, :], A_x_sample[0]).then_inc(L["x1"], 16)
                dst, src = mixing_chunk(c)
                sp.dma_start(dst, src).then_inc(pro_loaded[c % RING0], 16)

            def stream(I, i):
                n0 = sp.snap(I * BC)
                for h in range(BODY):
                    for c in range(PC):
                        n = h * PC + c
                        a = c % 2
                        e = i * (2 * BODY) + (2 * h + a)
                        slot = ring[:, ORDER[n % RING], :]
                        sp.wait_ge(moe_free, n0 + (n + 1))
                        if c < UPC:
                            src = w_up_v[e, :, c // 2, :]
                            dst = slot
                        else:
                            f = 2 * ((c - UPC) // 2)
                            src = w_down_v[e, :, f:f + 2, :]
                            dst = slot.rearrange("p (k n) -> p k n", k=2)
                        sp.dma_start(dst, src).then_inc(moe_loaded[n % RING], 16)

            with sp.Fori(0, PAIRS // BODY) as i:
                stream(i, i)

            def run(r):
                with sp.Fori(0, PAIRS // BODY) as i:
                    stream(i + r * (PAIRS // BODY), i)
            further_rounds(sp, run)

            sp.wait_ge(fin_ready, 1)
            sp.dma_start(y_prompt[0], x[:, 0, :]).then_inc(stored, 16)
            sp.wait_ge(fin_ready, 2)
            sp.dma_start(y_sample[0], x[:, 1, :]).then_inc(stored, 16)
            sp.wait_ge(stored, 32)
            sp.wait_ge(kv_stored, 32)

        @block.gpsimd
        def _(pool):
            def part_load(dst, src, s):
                pool.dma_start(dst, src).then_inc(s, 16)

            k = [0]

            def link(ins):
                k[0] += 1
                ins.then_inc(pool_step, 1)
                pool.wait_ge(pool_step, k[0])

            link(nc.gpsimd.memset(ident[:, :], 0.0))
            link(nc.gpsimd.affine_select(out=ident[:, :], in_=ident[:, :], compare_op=ALU.not_equal, fill=1.0,
                                         base=0, pattern=[[-1, P]], channel_multiplier=1))
            pool.sem_inc(const_ready, 1)
            link(nc.gpsimd.memset(mhalf[:, :], -0.5))
            link(nc.gpsimd.memset(flip, 0.0))
            for total in (GRID_W - 1, 3 * GRID_W - 1):
                link(nc.gpsimd.affine_select(out=flip, in_=flip, compare_op=ALU.not_equal, fill=1.0,
                                             base=-total, pattern=[[1, P]], channel_multiplier=1))
            pool.sem_inc(const_ready, 1)
            link(nc.gpsimd.memset(ones[:, :], 1.0))
            link(nc.gpsimd.memset(tri[:, :], 1.0))
            link(nc.gpsimd.memset(selrow[:, :, :], 0.0))
            link(nc.gpsimd.memset(sel[:, :], 1.0))
            link(nc.gpsimd.iota(iota_i[:, :], [[1, CAP]], base=0, channel_multiplier=0))
            link(nc.gpsimd.affine_select(out=tri[:, :], in_=tri[:, :], compare_op=ALU.is_gt, fill=0.0,
                                         base=0, pattern=[[1, P]], channel_multiplier=-1))
            for q in range(4):
                v = selrow[32 * q:32 * q + 32, :, :]
                link(nc.gpsimd.affine_select(out=v, in_=v, compare_op=ALU.not_equal, fill=1.0,
                                             base=0, pattern=[[-16, 2], [0, P]], channel_multiplier=1))
            for q in range(3):
                v = sel[32 * q:32 * q + 32, :]
                link(nc.gpsimd.affine_select(out=v, in_=v, compare_op=ALU.is_equal, fill=0.0,
                                             base=0, pattern=[[-1, E]], channel_multiplier=1))
            link(nc.gpsimd.tensor_copy(iota[:, :], iota_i[:, :]))
            pool.sem_inc(const_ready, 1)
            def root(n):
                pool.wait_ge(mean_ready, n + 1)
                nc.gpsimd.tensor_tensor(rstd[:, n % 2:n % 2 + 1], misc[:, n % 2:n % 2 + 1], mhalf[:, :],
                                        ALU.pow).then_inc(root_ready, 1)

            root(0)
            root(1)
            pool.wait_ge(pro_used, 5)
            part_load(kc, A_cache_k[0, 0].rearrange("h l d -> l h d"), L["kc"])
            for r in range(2):
                for kr in range(2):
                    for par in range(2):
                        at = par * RPB_H + (kr - r + WIN_R - 1) * RPB_W + WIN_C - GRID_W
                        src = bass.AP(A_rpb.tensor, A_rpb.offset + at,
                                      [[1, GRID_W], [2 * RPB_H, 4], [1, GRID_W]])
                        dst = bias_rev[64 * r:64 * r + 64, 4 * par:4 * par + 4, 64 * kr:64 * kr + 64]
                        part_load(dst, src, L["rpb"])
            part_load(wpool, A_w_pool[0].rearrange("g c d -> c g d"), L["wpool"])
            for q in range(3):
                part_load(bup[32 * q:32 * q + 32, :], A_b_up[0], L["bup"])
            part_load(vc.rearrange("p (h d) -> p h d", h=HEADS), A_cache_v[0, 0].rearrange("h l d -> l h d"), L["vc"])
            part_load(gffn, A_g_ffn.to_broadcast([P, D]), L["gffn"])
            part_load(wrt[:, :, :], A_w_router[0].rearrange("(k p) n -> p k n", p=P), L["wrt"])
            part_load(brt[:, :], A_b_router.to_broadcast([P, E]), L["brt"])
            pool.wait_ge(bias_copied, 1)
            for r in range(2):
                for kr in range(2):
                    v = biasM[64 * r:64 * r + 64, :, 64 * kr:64 * kr + GRID_W - WIN_C]
                    link(nc.gpsimd.affine_select(out=v, in_=v, compare_op=ALU.is_ge, fill=NEG, base=WIN_C // 2,
                                                 pattern=[[0, HEADS], [1, GRID_W - WIN_C]], channel_multiplier=-1))
                    v = biasM[64 * r:64 * r + 64, :, 64 * kr + WIN_C:64 * kr + GRID_W]
                    ins = nc.gpsimd.affine_select(out=v, in_=v, compare_op=ALU.is_ge, fill=NEG,
                                                  base=WIN_C // 2 - 1 - WIN_C,
                                                  pattern=[[0, HEADS], [-1, GRID_W - WIN_C]], channel_multiplier=1)
                    link(ins)
            pool.sem_inc(bias_ready, 1)
            pool.wait_ge(L["bup"], 48)
            link(nc.gpsimd.tensor_copy(bparts[:, :], bup[0:96, :]))
            for q in (1, 2):
                link(nc.gpsimd.tensor_tensor(brem[32 * q:32 * q + 32, :], bup[32 * q:32 * q + 32, :],
                                             bparts[32 * q:32 * q + 32, :], ALU.subtract))
                link(nc.gpsimd.tensor_copy(bparts[32 * q:32 * q + 32, :], brem[32 * q:32 * q + 32, :]))
            link(nc.gpsimd.tensor_tensor(bup[64:96, :], brem[64:96, :], bparts[64:96, :], ALU.subtract))
            nc.gpsimd.tensor_copy(bparts[64:96, :], bup[64:96, :]).then_inc(split_done, 1)
            pool.wait_ge(split_done, 1)
            pool.wait_ge(z_read, 4)
            pool.dma_start(new_v[0, 0].rearrange("h l d -> l h d"),
                           vm[:, 0, :].rearrange("p (h d) -> p h d", h=HEADS)).then_inc(kv_stored, 16)
            pool.wait_ge(knew_ready, 1)
            pool.dma_start(new_k[0, 0].rearrange("h l d -> l h d"),
                           knew.rearrange("p (h d) -> p h d", h=HEADS)).then_inc(kv_stored, 16)
            root(2)
            root(3)
            pool.wait_ge(moe_free, 12)
            nc.gpsimd.memset(acc, 0.0).then_inc(acc_zero, 1)

            def body(I, i):
                P0 = pool.snap(I * BODY)
                e0 = pool.snap(i * (2 * BODY))
                for h in range(BODY):
                    pool.wait_ge(u_read, P0 + (h + 1))
                    nc.gpsimd.tensor_copy(selbuf[:, :, :], sel[:, bass.ds(e0 + 2 * h, 2)].unsqueeze(2)
                                          .to_broadcast([96, 2, CAP])).then_inc(sel_ready, 1)

            with pool.Fori(0, PAIRS // BODY) as i:
                body(i, i)

            def run(r):
                with pool.Fori(0, PAIRS // BODY) as i:
                    body(i + r * (PAIRS // BODY), i)
            further_rounds(pool, run)
            root(4)
            root(5)

        @block.scalar
        def _(act):
            for q in range(4):
                src = A_b_ada[0].rearrange("(m q n) -> q m n", q=4, m=3)[q:q + 1]
                act.dma_start(bada[32 * q:32 * q + 32, :, :], src.to_broadcast([32, 3, HALF])).then_inc(L["bada"], 16)
            act.wait_ge(vec_c, 1)
            nc.scalar.activation(misc[:, 0:16], cT[:, 0:16], ACT.Sigmoid).then_inc(silu_ready, 1)
            for t in range(2):
                act.wait_ge(L[f"x{t}"], 16)
                nc.scalar.activation(xn[:, t, :], x[:, t, :], ACT.Square,
                                     accum_out=ssq[:, t:t + 1]).then_inc(ssq_ready, 1)
            act.wait_ge(A_ready, 1)
            act.wait_ge(x_t, 2)
            for t in range(2):
                for j in range(4, KB):
                    nc.scalar.activation(hTm[:, j, t * P:(t + 1) * P], ps[:, 2 + 2 * t, (j % 4) * P:(j % 4 + 1) * P],
                                         ACT.Identity, bias=modT[:, j % 4, 32 + 16 * t:33 + 16 * t],
                                         scale=Am[:, t, j:j + 1]).then_inc(hT_ready, 1)

            def z_out(cc):
                act.wait_ge(pro_used, AT["in", cc, 1] + 1)
                bank = 2 * (cc % 2)
                for b in range(2):
                    src = ps[:, bank + b, :]
                    if cc == 0:
                        dst, f = upad[:, 2 * b:2 * b + 2, :, PAD:PAD + P], ACT.Copy
                        src = src.rearrange("p (a t n) -> p a t n", a=2, t=2)
                    elif cc < 3:
                        dst, f = (qT, kT)[cc - 1][:, 2 * b:2 * b + 2, :], ACT.Copy
                        src = src.rearrange("p (a b) -> p a b", a=2)
                    elif cc == 3:
                        dst, f = vm[:, b, :], ACT.Copy
                    else:
                        g = sgA if cc < 6 else sgB
                        j = 4 * (cc % 2) + 2 * b
                        dst, f = g[:, j:j + 2, :], ACT.Sigmoid
                        src = src.rearrange("p (a b) -> p a b", a=2)
                    ins = nc.scalar.activation(dst, src, f)
                ins.then_inc(z_read, 1)

            act.wait_ge(pooled_ready, 1)
            z_out(0)
            act.wait_ge(kc_t, 1)
            nc.scalar.activation(kcT, ps[:, 6, :].rearrange("p (a b) -> p a b", a=4), ACT.Copy).then_inc(kcT_ready, 1)
            z_out(1)
            act.wait_ge(bias_t, 1)
            nc.scalar.activation(biasM, ps[:, 6:8, :].rearrange("p a (b c) -> p (a b) c", b=4), ACT.Copy)\
                .then_inc(bias_copied, 1)
            z_out(2)
            act.wait_ge(pool_done, 1)
            for g in range(4):
                ins = nc.scalar.activation(yT[:, g, :], ps[:, 6 + g // 2, (g % 2) * TOK:(g % 2 + 1) * TOK], ACT.Copy,
                                           scale=cT[:, 24 + g:25 + g])
            ins.then_inc(yT_ready, 1)
            z_out(3)
            act.wait_ge(mx_ready, 1)
            for hh in range(HEADS):
                nc.scalar.activation(Sp[:, hh, :], ps[:, 4 + hh // 4, (hh % 4) * P:(hh % 4 + 1) * P], ACT.Exp,
                                     bias=mx[:, 0, hh:hh + 1], scale=SCALE,
                                     accum_out=ssum[:, 0, hh:hh + 1]).then_inc(exp_done, 1)
            act.wait_ge(split_done, 1)
            z_out(4)
            act.wait_ge(k_t, 1)
            nc.scalar.activation(knew, ps[:, 6, :], ACT.Copy).then_inc(knew_ready, 1)
            act.wait_ge(mx_ready, 2)
            for hh in range(HEADS):
                nc.scalar.activation(Ss[:, hh, :], Ss[:, hh, :], ACT.Exp, bias=mx[:, 1, hh:hh + 1],
                                     accum_out=ssum[:, 1, hh:hh + 1]).then_inc(exp_done, 1)

            def pt_out(n):
                act.wait_ge(PT_done, n + 1)
                bank = (6, 4, 6)[n]
                dst = (PTp, PTs[:, 0], PTs[:, 1])[n]
                for b in range(2):
                    ins = nc.scalar.activation(dst[:, 4 * b:4 * b + 4, :],
                                               ps[:, bank + b, :].rearrange("p (a b) -> p a b", a=4), ACT.Copy)
                ins.then_inc(PT_read, 1)

            z_out(5)
            pt_out(0)
            z_out(6)
            pt_out(1)
            z_out(7)
            pt_out(2)

            def mod_out(n):
                m, t = n // 2, n % 2
                act.wait_ge(bc_done, n + 1)
                if m == 0:
                    nc.scalar.activation(gtm[:, t, :].rearrange("p (a b) -> p a b", a=2), ps[:, 2:4, :], ACT.Copy)
                    nc.scalar.activation(shf[:, t, :].rearrange("p (a b) -> p a b", a=2), ps[:, 4:6, :],
                                         ACT.Copy).then_inc(bc_read, 1)
                else:
                    nc.scalar.activation(gtf[:, t, :].rearrange("p (a b) -> p a b", a=2), ps[:, 4:6, :],
                                         ACT.Copy).then_inc(bc_read, 1)

            mod_out(0)
            act.wait_ge(O_done, 1)
            for t in range(2):
                ins = nc.scalar.activation(oT[:, :, t * P:(t + 1) * P],
                                           ps[:, t, :].rearrange("p (a b) -> p a b", a=4), ACT.Copy)
            ins.then_inc(oT_ready, 1)
            for n in range(1, 4):
                mod_out(n)
            act.dma_start(gfin, A_g_final.rearrange("(a n) -> a n", a=1).to_broadcast([P, D])).then_inc(L["gfin"], 16)
            act.wait_ge(zeroed, 1)
            act.dma_start(yb[0:E, :], A_b_down[0]).then_inc(L["bdn"], 16)
            for t in range(2):
                act.wait_ge(x2_ready, t + 1)
                nc.scalar.activation(h2[:, t, :], x[:, t, :], ACT.Square, accum_out=ssq[:, t:t + 1]).then_inc(ssq_ready, 1)
            nc.scalar.activation(misc[:, 12:13], mhalf[:, :], ACT.Exp)
            for b in range(4):
                act.wait_ge(h2_t, b + 1)
                t, jh = b // 2, b % 2
                nc.scalar.activation(h2T[:, 4 * jh:4 * jh + 4, t * P:(t + 1) * P],
                                     ps[:, 4 + b, :].rearrange("p (a b) -> p a b", a=4), ACT.Copy).then_inc(h2T_ready, 1)
            for t in range(2):
                act.wait_ge(top_ready, t + 1)
                nc.scalar.activation(rt[:, t, 1, :], rt[:, t, 0, :], ACT.Exp, bias=misc[:, 4 + t:5 + t]).then_inc(e_ready, 1)
            act.wait_ge(comb_t, 1)
            nc.scalar.activation(woT[0:E, :, :], ps[0:E, 1, 0:TOK].rearrange("p (a b) -> p a b", a=2),
                                 ACT.Copy).then_inc(woT_ready, 1)
            act.wait_ge(L["bdn"], 16)
            act.sem_inc(y_ready, 1)

            def xg_out(b, G, q):
                act.wait_ge(gath_done, G * 2 + (b + 1))
                nc.scalar.activation(xgT[:, q, 4 * b:4 * b + 4, :],
                                     ps[:, GB + b, :].rearrange("p (a b) -> p a b", a=4), ACT.Copy).then_inc(xg_ready, 1)

            def body(I, r):
                P0 = act.snap(I * BODY)
                n0 = act.snap(I * BC)
                G0 = act.snap(P0 + (r + 1))
                for h in range(BODY):
                    Pn, G = P0 + h, G0 + h
                    for b in range(2):
                        act.wait_ge(g_ready, Pn * 2 + (b + 1))
                        nc.scalar.activation(sig[:, b * HALF:(b + 1) * HALF], gate[:, b * HALF:(b + 1) * HALF],
                                             ACT.Sigmoid, scale=ALPHA).then_inc(sig_ready, 1)
                    for b in range(2):
                        xg_out(b, G, (h + 1) % 2)
                    act.wait_ge(woT_done, Pn + 2)
                    nc.scalar.activation(woT, ps[:, YB, 0:TOK].rearrange("p (a b) -> p a b", a=2),
                                         ACT.Copy).then_inc(woT_ready, 1)
                    for b in range(2):
                        act.wait_ge(hT_done, Pn * 2 + (b + 1))
                        nc.scalar.activation(hT[:, 4 * b:4 * b + 4, :],
                                             ps[:, GB + b, :].rearrange("p (a b) -> p a b", a=4),
                                             ACT.Copy).then_inc(hTe_ready, 1)
                    act.wait_ge(moe_free, n0 + (RING + (h + 1) * PC))
                    nc.scalar.activation(yb.rearrange("p (a b) -> p a b", a=2), ps[:, YB:YB + 2, :],
                                         ACT.Copy).then_inc(y_ready, 1)

            for b in range(2):
                xg_out(b, 0, 0)
            with act.Fori(0, PAIRS // BODY) as i:
                body(i, 0)

            def run(r):
                for b in range(2):
                    xg_out(b, r * (PAIRS + 1), 0)
                with act.Fori(0, PAIRS // BODY) as i:
                    body(i + r * (PAIRS // BODY), r)
            further_rounds(act, run)

            for t in range(2):
                act.wait_ge(fin_ss, t + 1)
                nc.scalar.activation(h2[:, t, :], x[:, t, :], ACT.Square, accum_out=ssq[:, t:t + 1]).then_inc(ssq_ready, 1)

        @block.vector
        def _(dve):
            k = [0]

            def link(ins):
                k[0] += 1
                ins.then_inc(dve_step, 1)
                dve.wait_ge(dve_step, k[0])

            V = nc.vector

            def mean(n):
                t = n % 2
                dve.wait_ge(ssq_ready, n + 1)
                V.tensor_scalar(misc[:, t:t + 1], ssq[:, t:t + 1], 1.0 / D, EPS, ALU.mult, ALU.add).then_inc(mean_ready, 1)

            def doubled(dst, src, s):
                lo, hi = 1 << s, PW - (1 << s) + 1
                a, b = (1, 0) if s == 0 else (1 << s >> 1, 1 << s >> 1)
                return V.tensor_tensor(dst[..., lo:hi], src[..., lo - a:hi - a], src[..., lo + b:hi + b], ALU.add)

            V.memset(pscr[:, :, :, :], 0.0)
            link(V.memset(cnt[:, :, :], 0.0))
            link(V.memset(pscr[:, 0, 0, PAD:PAD + P], 1.0))
            for g in range(4):
                src, dst = pscr[:, g % 2, 0, :], (pscr[:, (g + 1) % 2, 0, :])
                v = slice(PAD, PAD + P)
                link(doubled(dst, src, g))
                link(V.tensor_copy(cnt[:, g, v], dst[:, v]))
            V.memset(upad[:, :, :, 0:PAD], 0.0)
            link(V.memset(upad[:, :, :, PAD + P:PW], 0.0))

            dve.wait_ge(vec_t, 1)
            V.tensor_copy(cT[:, :], ps[:, 7, 0:VEC]).then_inc(vec_c, 1)
            dve.wait_ge(silu_ready, 1)
            for g in range(2):
                ins = V.tensor_tensor(cs[:, :, 16 * g:16 * g + 16],
                                      cT[:, 8 * g:8 * g + 8].unsqueeze(2).to_broadcast([P, KB, 16]),
                                      misc[:, 8 * g:8 * g + 8].unsqueeze(2).to_broadcast([P, KB, 16]), ALU.mult)
            ins.then_inc(silu_ready, 1)

            dve.wait_ge(silu_ready, 2)
            for t in range(2):
                mean(t)
            for t in range(2):
                dve.wait_ge(root_ready, t + 1)
                V.tensor_scalar(xn[:, t, :], x[:, t, :], rstd[:, t:t + 1], None, ALU.mult).then_inc(xn_ready, 1)

            def mod_rows(m, bank):
                dve.wait_ge(pro_used, AT["ada", m, KB - 1] + 1)
                dve.wait_ge(L["bada"], 64)
                V.tensor_tensor(modrow[:, m, :], ps[:, bank, :], bada[:, m, :], ALU.add).then_inc(row_ready, 1)

            mod_rows(0, 0)
            dve.wait_ge(modT_done, 1)
            link(V.tensor_copy(modT, ps[:, 5, :].rearrange("p (a b) -> p a b", a=4)))
            for g in range(2):
                for hi in range(2):
                    at = 64 + 32 * hi + 16 * g
                    ins = V.scalar_tensor_tensor(out=Am[:, g, 4 * hi:4 * hi + 4], in0=modT[:, :, at], scalar=1.0,
                                                 in1=cT[:, 16 + 4 * hi:20 + 4 * hi], op0=ALU.add, op1=ALU.mult)
            ins.then_inc(A_ready, 1)
            dve.wait_ge(A_ready, 1)
            dve.wait_ge(x_t, 2)
            for t in range(2):
                for j in range(4):
                    V.tensor_scalar(hTm[:, j, t * P:(t + 1) * P], ps[:, 1 + 2 * t, j * P:(j + 1) * P],
                                    Am[:, t, j:j + 1], modT[:, j, 16 * t:16 * t + 1], ALU.mult,
                                    ALU.add).then_inc(hT_ready2, 1)
            dve.sem_inc(pooled_ready, 1)

            dve.wait_ge(z_read, 1)
            link(V.memset(pscr[:, :, :, :], 0.0))
            for g in range(4):
                src = upad[:, g, :, :]
                for s in range(g + 1):
                    dst = pscr[:, s % 2, :, :]
                    link(doubled(dst, src, s))
                    src = dst
                if g == 0:
                    link(V.reciprocal(cnt[:, :, PAD:PAD + P], cnt[:, :, PAD:PAD + P]))
                o = pooled[:, g, :].rearrange("p (t n) -> p t n", t=2)
                link(V.tensor_tensor(o, src[:, :, PAD:PAD + P],
                                     cnt[:, g:g + 1, PAD:PAD + P].to_broadcast([P, 2, P]), ALU.mult))
                ins = V.tensor_tensor(o, o, upad[:, g, :, PAD:PAD + P], ALU.subtract)
                if g < 3:
                    link(ins)
            ins.then_inc(pooled_ready, 1)
            mod_rows(1, 4)
            mod_rows(2, 5)
            dve.wait_ge(S_done, 1)
            link(V.tensor_reduce(mx[:, 0, :], ps[:, 4:6, :].rearrange("p a (b n) -> p (a b) n", b=4), AX.X, ALU.max))
            V.tensor_scalar(mx[:, 0, :], mx[:, 0, :], -SCALE, None, ALU.mult).then_inc(mx_ready, 1)
            dve.wait_ge(S_done, 2)
            dve.wait_ge(bias_ready, 1)
            for b in range(2):
                V.scalar_tensor_tensor(out=Ss[:, 4 * b:4 * b + 4, 0:P],
                                       in0=ps[:, 6 + b, :].rearrange("p (a b) -> p a b", a=4), scalar=SCALE,
                                       in1=biasM[:, 4 * b:4 * b + 4, :], op0=ALU.mult, op1=ALU.add)\
                    .then_inc(S_read, 1)

            def normalise(n, S, width):
                dve.wait_ge(exp_done, HEADS * (n + 1))
                link(V.reciprocal(rsum[:, n, :], ssum[:, n, :]))
                V.tensor_tensor(S, S, rsum[:, n, :].unsqueeze(2).to_broadcast([P, HEADS, width]),
                                ALU.mult).then_inc(prob_ready, 1)

            normalise(0, Sp, P)
            dve.wait_ge(S_done, 3)
            for b in range(2):
                link(V.tensor_scalar(Ss[:, 4 * b:4 * b + 4, P:TOK],
                                     ps[:, 4 + b, :].rearrange("p (a b) -> p a b", a=4), SCALE, None, ALU.mult))
            V.tensor_reduce(mx[:, 1, :], Ss, AX.X, ALU.max, negate=True).then_inc(mx_ready, 1)
            normalise(1, Ss, TOK)

            dve.wait_ge(L["gffn"], 16)

            def scale_out(t):
                dve.wait_ge(bc_done, 3 + t)
                V.scalar_tensor_tensor(out=Af[:, t, :], in0=ps[:, 2:4, :].rearrange("p a b -> p (a b)"), scalar=1.0,
                                       in1=gffn, op0=ALU.add, op1=ALU.mult).then_inc(Af_ready, 1)

            for j in range(KB):
                if j in (4, 6):
                    scale_out((j - 4) // 2)
                dve.wait_ge(br_done, j + 1)
                b = 6 + j % 2
                V.tensor_tensor(sgA[:, j, :], ps[:, b, 0:TOK], sgA[:, j, :], ALU.mult)
                link(V.tensor_tensor(sgB[:, j, :], ps[:, b, TOK:HALF], sgB[:, j, :], ALU.mult))
                V.tensor_tensor(sgA[:, j, :], sgA[:, j, :], sgB[:, j, :], ALU.add).then_inc(merged_ready, 1)
            V.memset(woT, 0.0)
            V.memset(yb, 0.0).then_inc(zeroed, 1)
            for t in range(2):
                if t == 0:
                    dve.wait_ge(out_done, 1)
                    dve.wait_ge(bc_read, 2)
                else:
                    dve.wait_ge(moe_free, 12)
                link(V.tensor_tensor(tmp[:, t, :], ps[:, 2 * t:2 * t + 2, :].rearrange("p a b -> p (a b)"), gtm[:, t, :],
                                     ALU.mult))
                V.tensor_tensor(x[:, t, :], x[:, t, :], tmp[:, t, :], ALU.add).then_inc(x2_ready, 1)
                mean(2 + t)
                dve.wait_ge(root_ready, 3 + t)
                link(V.scalar_tensor_tensor(out=h2[:, t, :], in0=x[:, t, :], scalar=rstd[:, t:t + 1],
                                            in1=Af[:, t, :], op0=ALU.mult, op1=ALU.mult))
                V.tensor_tensor(h2[:, t, :], h2[:, t, :], shf[:, t, :], ALU.add).then_inc(h2_ready, 1)
            dve.wait_ge(h2_ready, 2)
            dve.sem_inc(moe_free, 4)
            dve.wait_ge(const_ready, 3)

            dve.wait_ge(L["brt"], 16)
            for t in range(2):
                dve.wait_ge(logit_done, t + 1)
                R = [rt[:, t, n, :] for n in range(8)]
                link(V.tensor_tensor(R[0], ps[:, t, 0:E], brt[:, :], ALU.add))
                link(V.max(top8[:, t, :], R[0]))
                V.tensor_scalar(misc[:, 4 + t:5 + t], top8[:, t, 0:1], -1.0, None, ALU.mult).then_inc(top_ready, 1)
                fourth = top8[:, t, TOPK - 1:TOPK]
                link(V.tensor_scalar(R[2], R[0], fourth, None, ALU.is_gt))
                link(V.tensor_reduce(misc[:, 6 + t:7 + t], R[2], AX.X, ALU.add))
                link(V.tensor_scalar(R[3], R[0], fourth, None, ALU.is_equal))
                link(V.tensor_tensor_scan(R[4], ones[:, 0:E], R[3], misc[:, 6 + t:7 + t], ALU.mult, ALU.add))
                link(V.tensor_scalar(R[4], R[4], float(TOPK), None, ALU.is_le))
                link(V.tensor_tensor(R[3], R[3], R[4], ALU.mult))
                V.tensor_tensor(R[5], R[2], R[3], ALU.add).then_inc(mask_ready, 1)
            for t in range(2):
                R = [rt[:, t, n, :] for n in range(8)]
                dve.wait_ge(mask_ready, t + 1)
                dve.wait_ge(e_ready, t + 1)
                link(V.tensor_tensor(R[6], R[1], R[5], ALU.mult))
                link(V.tensor_reduce(misc[:, 2 + t:3 + t], R[6], AX.X, ALU.add))
                link(V.reciprocal(misc[:, 2 + t:3 + t], misc[:, 2 + t:3 + t]))
                V.tensor_scalar(R[6], R[6], misc[:, 2 + t:3 + t], None, ALU.mult).then_inc(comb_ready, 1)
            dve.wait_ge(comb_ready, 2)
            link(V.memset(tab[:, PAIRS, :], -1.0))
            for t in range(2):
                dve.wait_ge(rank_done, t + 1)
                R = [rt[:, t, n, :] for n in range(8)]
                pairs = tab[:, 0:PAIRS, :]
                link(V.tensor_scalar(R[7], ps[:, 2 + t, 0:E], 1.0, None, ALU.add))
                link(V.tensor_tensor(R[7], R[7], R[5], ALU.mult))
                link(V.tensor_scalar(pairs[:, :, 2 * t:2 * t + 2], R[7].rearrange("p (a b) -> p a b", b=2), 1.0, None,
                                     ALU.subtract))
                link(V.tensor_copy(pairs[:, :, 4 + 2 * t:6 + 2 * t], R[6].rearrange("p (a b) -> p a b", b=2)))
            link(V.tensor_reduce(misc[:, 9:10], ps[:, 3, E:2 * E], AX.X, ALU.max))
            for r in range(ROUNDS):
                ins = V.tensor_scalar(flags[:, r:r + 1], misc[:, 9:10], float(CAP * r), None, ALU.is_gt)
            ins.then_inc(flag_ready, 1)

            def one_hots(p, G):
                V.tensor_copy(cur[:, :], tab[:, bass.ds(p, 1), :].rearrange("p a b -> p (a b)")).then_inc(cur_ready, 1)
                dve.wait_ge(cur_ready, G + 1)
                for t in range(2):
                    for a in range(2):
                        ins = V.tensor_scalar(oh[:, t, CAP * a:CAP * a + CAP], iota[:, :], cur[:, 2 * t + a:2 * t + a + 1],
                                              None, ALU.is_equal)
                ins.then_inc(oh_ready, 1)

            def add_acc(Pn, n):
                t, c = n // 2, slice((n % 2) * HALF, (n % 2 + 1) * HALF)
                dve.wait_ge(scat_done, Pn * 4 + (n + 1))
                V.tensor_tensor(acc[:, t, c], ps[:, GB + n, :], acc[:, t, c], ALU.add).then_inc(acc_done, 1)

            def body(I, i, r):
                P0 = dve.snap(I * BODY)
                G0 = dve.snap(P0 + (r + 1))
                p0 = dve.snap(i * BODY)
                n0 = dve.snap(I * BC)
                for h in range(BODY):
                    Pn, G = P0 + h, G0 + h
                    dve.wait_ge(woT_done, Pn + 1)
                    dve.wait_ge(oh_ready, G)
                    for t in range(2):
                        for a in range(2):
                            ins = V.tensor_scalar(wo[:, t, CAP * a:CAP * a + CAP], oh[:, t, CAP * a:CAP * a + CAP],
                                                  cur[:, 4 + 2 * t + a:5 + 2 * t + a], None, ALU.mult)
                    ins.then_inc(wo_ready, 1)
                    dve.wait_ge(wo_ready, Pn + 1)
                    dve.wait_ge(gath_done, G * 2)
                    one_hots(p0 + (h + 1), G)
                    dve.wait_ge(moe_free, n0 + (RING + h * PC + UPC))
                    for b in range(2):
                        V.tensor_scalar(gate[:, b * HALF:(b + 1) * HALF], ps[:, b, :], LIMIT, None,
                                        ALU.min).then_inc(g_ready, 1)
                    V.tensor_scalar(hid, ps[:, 2:4, :].rearrange("p a b -> p (a b)"), LIMIT, -LIMIT, ALU.min,
                                    ALU.max).then_inc(u_read, 1)
                    add_acc(Pn, 0)
                    add_acc(Pn, 1)
                    dve.wait_ge(u_read, Pn + 2)
                    for b in range(2):
                        c = slice(b * HALF, (b + 1) * HALF)
                        dve.wait_ge(sig_ready, Pn * 2 + (b + 1))
                        V.tensor_tensor(sig[:, c], sig[:, c], gate[:, c], ALU.mult).then_inc(glu_ready, 1)
                        dve.wait_ge(glu_ready, Pn * 2 + (b + 1))
                        V.scalar_tensor_tensor(out=hid[:, c], in0=hid[:, c], scalar=1.0, in1=sig[:, c],
                                               op0=ALU.add, op1=ALU.mult).then_inc(hid_ready, 1)
                    add_acc(Pn, 2)
                    add_acc(Pn, 3)

            dve.sem_inc(u_read, 1)
            dve.wait_ge(acc_zero, 1)
            one_hots(0, 0)
            with dve.Fori(0, PAIRS // BODY) as i:
                body(i, i, 0)
            dve.wait_ge(acc_done, 4 * PAIRS)

            def run(r):
                dve.wait_ge(oh_ready, r * (PAIRS + 1))
                V.tensor_scalar(tab[:, :, 0:4], tab[:, :, 0:4], float(CAP), None, ALU.subtract).then_inc(tab_ready, 1)
                dve.wait_ge(tab_ready, r)
                dve.wait_ge(gath_done, 2 * r * (PAIRS + 1))
                one_hots(0, r * (PAIRS + 1))
                with dve.Fori(0, PAIRS // BODY) as i:
                    body(i + r * (PAIRS // BODY), i, r)
                dve.wait_ge(acc_done, 4 * (r + 1) * PAIRS)
            further_rounds(dve, run)

            link(V.tensor_tensor(acc, acc, gtf[:, :, :], ALU.mult))
            link(V.tensor_tensor(x[:, :, :], x[:, :, :], acc, ALU.add))
            for t in range(2):
                for n in range(2):
                    c = slice(n * HALF, (n + 1) * HALF)
                    dve.wait_ge(last_scat, 2 * t + n + 1)
                    link(V.tensor_tensor(gate[:, c] if t == 0 else hid[:, c], ps[:, GB + 2 * t + n, :], gtf[:, t, c],
                                         ALU.mult))
                    ins = V.tensor_tensor(x[:, t, c], x[:, t, c], gate[:, c] if t == 0 else hid[:, c], ALU.add)
                ins.then_inc(fin_ss, 1)
            dve.wait_ge(L["gfin"], 16)
            for t in range(2):
                mean(4 + t)
                dve.wait_ge(root_ready, 5 + t)
                V.scalar_tensor_tensor(out=x[:, t, :], in0=x[:, t, :], scalar=rstd[:, t:t + 1], in1=gfin,
                                       op0=ALU.mult, op1=ALU.mult).then_inc(fin_ready, 1)

        @block.tensor
        def _(pe):
            mm, tp = nc.tensor.matmul, nc.tensor.transpose

            def landed(c):
                pe.wait_ge(pro_loaded[c % RING0], 16 * (c // RING0 + 1))
                return ring[:, c % RING0, :]

            pe.wait_ge(L["vec"], 64)
            pe.wait_ge(const_ready, 1)
            tp(ps[:, 7, 0:VEC], vecs[:, :], ident[0:VEC, 0:VEC]).then_inc(vec_t, 1)

            def modulation(m, bank, ks):
                for kk in ks:
                    w = landed(AT["ada", m, kk])
                    for q in range(4):
                        ins = mm(ps[32 * q:32 * q + 32, bank, :], cs[:, kk, :], w[:, q * HALF:(q + 1) * HALF],
                                 start=(kk == 0), stop=(kk == KB - 1))
                    ins.then_inc(pro_used, 1)

            def project(cc):
                if cc >= 2:
                    pe.wait_ge(z_read, cc - 1)
                bank = 2 * (cc % 2)
                w = [landed(AT["in", cc, h]).rearrange("p (k n) -> p k n", k=4) for h in range(2)]
                last = 1 if cc == 3 else 3
                for b in range(last + 1):
                    for kk in range(KB):
                        wk = w[kk // 4][:, kk % 4, :]
                        if cc == 3:
                            ins = mm(ps[:, bank + b, :], hTm[:, kk, b * P:(b + 1) * P], wk,
                                     start=(kk == 0), stop=(kk == KB - 1))
                        else:
                            ins = mm(ps[:, bank + b // 2, (b % 2) * TOK:(b % 2 + 1) * TOK], wk[:, b * P:(b + 1) * P],
                                     hTm[:, kk, :], start=(kk == 0), stop=(kk == KB - 1))
                        if b == last and kk % 4 == 3:
                            ins.then_inc(pro_used, 1)

            pe.wait_ge(silu_ready, 2)
            modulation(0, 0, range(5))
            for t in range(2):
                pe.wait_ge(xn_ready, t + 1)
                for j in range(KB):
                    ins = tp(ps[:, 1 + 2 * t + j // 4, (j % 4) * P:(j % 4 + 1) * P], xn[:, t, j * P:(j + 1) * P], ident[:, :])
                ins.then_inc(x_t, 1)
            modulation(0, 0, range(5, KB))
            pe.wait_ge(row_ready, 1)
            for j in range(4):
                ins = tp(ps[:, 5, j * P:(j + 1) * P], modrow[:, 0, j * P:(j + 1) * P], ident[:, :])
            ins.then_inc(modT_done, 1)
            pe.wait_ge(hT_ready, 8)
            pe.wait_ge(hT_ready2, 8)

            def scores(n, keys, bank):
                for h in range(HEADS):
                    b, o = h // 2, DH * (h % 2)
                    ins = mm(ps[:, bank + h % 2, b * P:(b + 1) * P], qT[o:o + DH, b, (n > 0) * P:(n > 0) * P + P],
                             keys[o:o + DH, b, :], start=True, stop=True)
                ins.then_inc(S_done, 1)

            def prob_t(src, bank):
                for hh in range(HEADS):
                    ins = tp(ps[:, bank + hh // 4, (hh % 4) * P:(hh % 4 + 1) * P], src[:, hh, :], ident[:, :])
                ins.then_inc(PT_done, 1)

            project(0)
            modulation(1, 4, range(4))
            pe.wait_ge(L["kc"], 16)
            for b in range(4):
                ins = tp(ps[:, 6, b * P:(b + 1) * P], kc[:, b * P:(b + 1) * P], ident[:, :])
            ins.then_inc(kc_t, 1)
            project(1)
            modulation(1, 4, range(4, KB))
            pe.wait_ge(L["rpb"], 16 * 8)
            pe.wait_ge(const_ready, 2)
            pe.wait_ge(kcT_ready, 1)
            for b in range(2):
                ins = mm(ps[:, 6 + b, :], flip, bias_rev[:, 4 * b:4 * b + 4, :], start=True, stop=True)
            ins.then_inc(bias_t, 1)
            project(2)
            modulation(2, 5, range(4))
            pe.wait_ge(bias_copied, 1)
            pe.wait_ge(pooled_ready, 2)
            pe.wait_ge(L["wpool"], 16)
            for g in range(4):
                ins = mm(ps[:, 6 + g // 2, (g % 2) * TOK:(g % 2 + 1) * TOK], wpool[:, g, :], pooled[:, g, :],
                         start=True, stop=True)
            ins.then_inc(pool_done, 1)
            project(3)
            modulation(2, 5, range(4, KB))
            pe.wait_ge(z_read, 3)
            pe.wait_ge(row_ready, 3)
            scores(0, kT[:, :, 0:P], 4)
            pe.wait_ge(yT_ready, 1)
            scores(1, kT[:, :, P:TOK], 6)
            project(4)
            pe.wait_ge(exp_done, HEADS)
            scores(2, kcT, 4)
            pe.wait_ge(S_read, 2)
            for b in range(4):
                ins = tp(ps[:, 6, b * P:(b + 1) * P], kT[:, b, 0:P], ident[:, :])
            ins.then_inc(k_t, 1)
            project(5)
            pe.wait_ge(prob_ready, 1)
            pe.wait_ge(knew_ready, 1)
            prob_t(Sp, 6)
            project(6)
            pe.wait_ge(prob_ready, 2)
            prob_t(Ss[:, :, 0:P], 4)
            project(7)
            pe.wait_ge(PT_read, 1)
            prob_t(Ss[:, :, P:TOK], 6)
            def spread(n):
                m, t = n // 2, n % 2
                if n == 0:
                    pe.wait_ge(PT_read, 2)
                    pe.wait_ge(z_read, 8)
                    pe.wait_ge(const_ready, 3)
                else:
                    pe.wait_ge(bc_read, n)
                if n == 1:
                    pe.wait_ge(kv_stored, 32)
                if n == 3:
                    pe.wait_ge(Af_ready, 1)
                for q in range(4):
                    ins = mm(ps[:, 2 + q, :], selrow[32 * q:32 * q + 32, t, :], modrow[32 * q:32 * q + 32, 1 + m, :],
                             start=True, stop=True)
                ins.then_inc(bc_done, 1)

            pe.wait_ge(z_read, 7)
            for b in range(4):
                for par in range(2):
                    h, hh, o = 2 * b + par, 4 * par + b, DH * par
                    mm(ps[o:o + DH, 0, b * P:(b + 1) * P], vm[:, 0, h * DH:(h + 1) * DH], PTp[:, hh, :], start=True, stop=True)
            spread(0)
            pe.wait_ge(PT_read, 3)
            pe.wait_ge(L["vc"], 16)
            for b in range(4):
                for par in range(2):
                    h, hh, o = 2 * b + par, 4 * par + b, DH * par
                    mm(ps[o:o + DH, 1, b * P:(b + 1) * P], vm[:, 1, h * DH:(h + 1) * DH], PTs[:, 0, hh, :], start=True, stop=False)
                    ins = mm(ps[o:o + DH, 1, b * P:(b + 1) * P], vc[:, h * DH:(h + 1) * DH], PTs[:, 1, hh, :],
                             start=False, stop=True)
            ins.then_inc(O_done, 1)
            wa = [landed(AT["pa", 0, h]).rearrange("p (k n) -> p k n", k=2) for h in range(2)]
            wb = [landed(AT["pb", 0, h]).rearrange("p (k n) -> p k n", k=2) for h in range(2)]
            for j in range(KB):
                if j in (1, 3, 5):
                    spread((j + 1) // 2)
                if j >= 2:
                    pe.wait_ge(merged_ready, j - 1)
                for half, (w, src) in enumerate(((wa, yT), (wb, oT))):
                    if j == 0 and half:
                        pe.wait_ge(O_done, 1)
                        pe.sem_inc(moe_free, 4)
                        pe.wait_ge(oT_ready, 1)
                    for kk in range(4):
                        ins = mm(ps[:, 6 + j % 2, half * TOK:(half + 1) * TOK], w[kk // 2][:, kk % 2, j * P:(j + 1) * P],
                                 src[:, kk, :], start=(kk == 0), stop=(kk == 3))
                ins.then_inc(br_done, 1)
            pe.wait_ge(br_done, KB)
            pe.sem_inc(moe_free, 4)
            wo_ = [landed(AT["out", 0, h]).rearrange("p (k n) -> p k n", k=2) for h in range(4)]
            for t in range(2):
                if t == 1:
                    pe.wait_ge(bc_read, 4)
                    pe.wait_ge(Af_ready, 2)
                for kk in range(KB):
                    if t == 0:
                        pe.wait_ge(merged_ready, kk + 1)
                    for n in range(2):
                        ins = mm(ps[:, 2 * t + n, :], sgA[:, kk, t * P:(t + 1) * P],
                                 wo_[kk // 2][:, kk % 2, n * HALF:(n + 1) * HALF], start=(kk == 0), stop=(kk == KB - 1))
                    if t == 1 and kk % 2:
                        ins.then_inc(moe_free, 1)
                if t == 0:
                    ins.then_inc(out_done, 1)
            pe.wait_ge(L["wrt"], 16)
            for t in range(2):
                pe.wait_ge(h2_ready, t + 1)
                for j in range(KB):
                    ins = tp(ps[:, 4 + 2 * t + j // 4, (j % 4) * P:(j % 4 + 1) * P], h2[:, t, j * P:(j + 1) * P], ident[:, :])
                    if j % 4 == 3:
                        ins.then_inc(h2_t, 1)
                for kk in range(KB):
                    if kk % 4 == 0:
                        pe.wait_ge(h2T_ready, 2 * t + kk // 4 + 1)
                    ins = mm(ps[:, t, 0:E], h2T[:, kk, t * P:(t + 1) * P], wrt[:, kk, :],
                             start=(kk == 0), stop=(kk == KB - 1))
                ins.then_inc(logit_done, 1)
            pe.wait_ge(mask_ready, 1)
            mm(ps[:, 2, 0:E], tri[:, :], rt[:, 0, 5, :], start=True, stop=True).then_inc(rank_done, 1)
            pe.wait_ge(mask_ready, 2)
            mm(ps[:, 3, 0:E], ones[:, :], rt[:, 0, 5, :], start=True, stop=False)
            mm(ps[:, 3, 0:E], tri[:, :], rt[:, 1, 5, :], start=False, stop=True)
            mm(ps[:, 3, E:2 * E], ones[:, :], rt[:, 0, 5, :], start=True, stop=False)
            mm(ps[:, 3, E:2 * E], ones[:, :], rt[:, 1, 5, :], start=False, stop=True).then_inc(rank_done, 1)
            pe.wait_ge(comb_ready, 2)
            for t in range(2):
                ins = tp(ps[0:E, 1, t * P:(t + 1) * P], rt[:, t, 6, :], ident[:, :])
            ins.then_inc(comb_t, 1)

            def gather(G):
                pe.wait_ge(oh_ready, G + 1)
                for j in range(KB):
                    for t in range(2):
                        ins = mm(ps[:, GB + j // 4, (j % 4) * P:(j % 4 + 1) * P], h2[:, t, j * P:(j + 1) * P],
                                 oh[:, t, :], start=(t == 0), stop=(t == 1))
                    if j % 4 == 3:
                        ins.then_inc(gath_done, 1)

            def scatter(done):
                for n in range(4):
                    t = n // 2
                    mm(ps[:, GB + n, :], woT[:, t, :], yb[:, (n % 2) * HALF:(n % 2 + 1) * HALF],
                       start=True, stop=True).then_inc(done, 1)

            def body(I, r):
                P0 = pe.snap(I * BODY)
                G0 = pe.snap(P0 + (r + 1))
                lap0 = pe.snap(I * (16 * LAPS))

                def chunk(n):
                    pe.wait_ge(moe_loaded[n % RING], lap0 + 16 * (n // RING + 1))
                    return ring[:, ORDER[n % RING], :]

                for h in range(BODY):
                    Pn, G = P0 + h, G0 + h
                    pe.wait_ge(xg_ready, G * 2)
                    pe.wait_ge(u_read, Pn + 1)
                    pe.wait_ge(sel_ready, Pn + 1)
                    for n in range(4):
                        for a in range(2):
                            mm(ps[CAP * a:CAP * a + CAP, n, :], selbuf[:, a, :], bparts[:, n * HALF:(n + 1) * HALF],
                               start=True, stop=False)
                    for kk in range(KB):
                        w = [chunk(h * PC + 2 * kk + a) for a in range(2)]
                        for n in range(4):
                            for a in range(2):
                                ins = mm(ps[CAP * a:CAP * a + CAP, n, :], xgT[:, h, kk, CAP * a:CAP * a + CAP],
                                         w[a][:, n * HALF:(n + 1) * HALF], start=False, stop=(kk == KB - 1))
                                if n == 3:
                                    ins.then_inc(moe_free, 1)
                    pe.wait_ge(y_ready, Pn + 1)
                    pe.wait_ge(woT_ready, Pn + 1)
                    scatter(scat_done)
                    pe.wait_ge(acc_done, Pn * 4 + 2)
                    gather(G)
                    pe.wait_ge(wo_ready, Pn + 1)
                    pe.wait_ge(acc_done, Pn * 4 + 3)
                    for t in range(2):
                        ins = tp(ps[:, YB, t * P:(t + 1) * P], wo[:, t, :], ident[:, :])
                    ins.then_inc(woT_done, 1)
                    for f in range(KB):
                        if f % 4 == 0:
                            pe.wait_ge(hid_ready, Pn * 2 + (f // 4 + 1))
                            pe.wait_ge(xg_ready, G * 2 + (f // 4 + 1))
                        ins = tp(ps[:, GB + f // 4, (f % 4) * P:(f % 4 + 1) * P], hid[:, f * P:(f + 1) * P], ident[:, :])
                        if f % 4 == 3:
                            ins.then_inc(hT_done, 1)
                    pe.wait_ge(woT_ready, Pn + 2)
                    pe.wait_ge(acc_done, Pn * 4 + 4)
                    for f in range(KB):
                        if f % 4 == 0:
                            pe.wait_ge(hTe_ready, Pn * 2 + (f // 4 + 1))
                        if f % 2 == 0:
                            w = [chunk(h * PC + UPC + f + a) for a in range(2)]
                        for n in range(2):
                            for a in range(2):
                                ins = mm(ps[CAP * a:CAP * a + CAP, YB + n, :], hT[:, f, CAP * a:CAP * a + CAP],
                                         w[a][:, (f % 2) * D + n * HALF:(f % 2) * D + (n + 1) * HALF],
                                         start=(f == 0), stop=(f == KB - 1))
                                if f % 2 and n == 1:
                                    ins.then_inc(moe_free, 1)

            pe.sem_inc(woT_done, 1)
            gather(0)
            with pe.Fori(0, PAIRS // BODY) as i:
                body(i, 0)
            pe.wait_ge(y_ready, 1 + PAIRS)
            pe.wait_ge(woT_ready, 1 + PAIRS)

            def run(r):
                gather(r * (PAIRS + 1))
                with pe.Fori(0, PAIRS // BODY) as i:
                    body(i + r * (PAIRS // BODY), r)
                pe.wait_ge(y_ready, 1 + (r + 1) * PAIRS)
                pe.wait_ge(woT_ready, 1 + (r + 1) * PAIRS)
            further_rounds(pe, run)
            scatter(last_scat)


_INS = ['x_prompt', 'x_sample', 'cache_k', 'cache_v', 'c', 'c_ctx', 'w_ada', 'b_ada', 'g_mix', 'w_in', 'w_pool',
        'pool_scale', 'w_pa', 'w_pb', 'rpb', 'w_out', 'g_ffn', 'w_router', 'b_router', 'w_up', 'b_up', 'w_down',
        'b_down', 'g_final']
_OUTS = [((1, 128, 1024), 'float32'), ((1, 128, 1024), 'float32'),
         ((1, 1, 8, 128, 64), 'float32'), ((1, 1, 8, 128, 64), 'float32')]


def kernel(**inputs):
    import numpy as _np
    import concourse.bacc as _bacc
    from concourse import mybir as _mybir
    from concourse.bass_utils import run_bass_kernel_spmd as _run

    nc = _bacc.Bacc("TRN2", target_bir_lowering=False, num_devices=1)
    arrays, args = {}, []
    for name in _INS:
        a = _np.ascontiguousarray(inputs[name])
        arrays[f"in_{name}_dram"] = a
        args.append(nc.dram_tensor(f"in_{name}_dram", a.shape, _mybir.dt.from_np(a.dtype), kind="ExternalInput").ap())
    for i, (shape, dtype) in enumerate(_OUTS):
        dt = _mybir.dt.from_np(_np.dtype(dtype))
        args.append(nc.dram_tensor(f"out_{i}_dram", shape, dt, kind="ExternalOutput").ap())
    layer_kernel(nc, *args)
    r = _run(nc, [arrays], core_ids=[0])
    return tuple(r.results[0][f"out_{i}_dram"] for i in range(len(_OUTS)))
```

```python
from contextlib import ExitStack

import concourse.bass as bass
from concourse import mybir

F32 = mybir.dt.float32
BF16 = mybir.dt.bfloat16
F32R = mybir.dt.float32r
I32 = mybir.dt.int32
ALU = mybir.AluOpType
ACT = mybir.ActivationFunctionType
AX = mybir.AxisListType

P = 128
D = 1024
KB = D // P
TOK = 2 * P
HEADS, DH = 8, 64
GRID_W, WIN_C, WIN_R = 64, 16, 8
RPB_W = 2 * WIN_C - 1
RPB_H = (2 * WIN_R - 1) * RPB_W
SCALE = DH ** -0.5
NEG = -1e30
EPS = 1e-6
E, TOPK, FF = 32, 4, 1024
LIMIT, ALPHA = 7.0, 1.702
HALF = 512
PAD = 8
PW = P + 2 * PAD

SLOT = 2048
RING = 16
RING0 = 9
RING1 = 6
NARROW = 27
ORDER = [1, 2, 3, 4, 7, 10, 6, 8, 5, 0, 11, 12, 9, 13, 14, 15]
CAP = 64
PAIRS = E // 2
ROUNDS = TOK // CAP
BODY = 2
UPC = 16
DNC = 8
PC = UPC + DNC
BC = BODY * PC
LAPS = BC // RING
VEC = 28

MIX = [("ada", 0, k) for k in range(KB)]
for _j in range(4):
    MIX += [("in", _j, 0), ("in", _j, 1)] + [("ada", 1 + _j // 2, 4 * (_j % 2) + k) for k in range(4)]
MIX += [("in", j, h) for j in range(4, 8) for h in range(2)]
MIX += [("pa", 0, h) for h in range(2)] + [("pb", 0, h) for h in range(2)] + [("out", 0, h) for h in range(4)]
AT = {key: n for n, key in enumerate(MIX)}


def place_mixing():
    slots = [c % RING0 if c < NARROW else (c - NARROW) % RING1 for c in range(len(MIX))]
    slots[-2:] = [11, 12]
    before = [max((b for b in range(c) if slots[b] == slots[c]), default=None) for c in range(len(MIX))]
    return slots, before, [slots[:c + 1].count(slots[c]) for c in range(len(MIX))]


def layer_kernel(nc, A_x_prompt, A_x_sample, A_cache_k, A_cache_v, A_c, A_c_ctx, A_w_ada, A_b_ada, A_g_mix,
                 A_w_in, A_w_pool, A_pool_scale, A_w_pa, A_w_pb, A_rpb, A_w_out, A_g_ffn, A_w_router,
                 A_b_router, A_w_up, A_b_up, A_w_down, A_b_down, A_g_final,
                 y_prompt, y_sample, new_k, new_v):
    mix_slot, mix_before, mix_held = place_mixing()
    w_in_v = A_w_in[0].rearrange("(k p) n -> p k n", p=P)
    w_ada_v = A_w_ada[0].rearrange("(k p) n -> p k n", p=P)
    w_pa_v = A_w_pa[0].rearrange("(k p) n -> p k n", p=P)
    w_pb_v = A_w_pb[0].rearrange("(k p) n -> p k n", p=P)
    w_out_v = A_w_out[0].rearrange("(k p) n -> p k n", p=P)
    w_up_v = A_w_up[0].rearrange("e (k p) n -> e p k n", p=P)
    w_down_v = A_w_down[0].rearrange("e (k p) n -> e p k n", p=P)

    with ExitStack() as ctx:
        def sb(name, shape, dt=F32):
            return ctx.enter_context(nc.sbuf_tensor(name, shape, dt))

        def sem(name):
            return ctx.enter_context(nc.semaphore(name))

        with nc.sbuf_tensor("parts", [P, 11, SLOT], F32R) as parts:
            pass
        ring = sb("ring", [P, RING, SLOT])
        arena = sb("arena", [P, 13056])
        x = sb("x", [P, 2, D])
        gtf = sb("gtf", [P, 2, D])
        bparts = sb("bparts", [96, 2 * FF], BF16)
        sel = sb("sel", [96, E], BF16)
        selbuf = sb("selbuf", [96, 2, CAP], BF16)
        ident = sb("ident", [P, P])
        iota = sb("iota", [P, CAP])
        iota_i = sb("iota_i", [P, CAP], I32)
        tab = sb("tab", [P, PAIRS + 1, 8])
        cur = sb("cur", [P, 8])
        small = sb("small", [P, 256])
        flags = sb("flags", [P, 4], I32)
        mhalf = sb("mhalf", [P, 1])

        def region(at, *shape):
            n = 1
            for s in shape:
                n *= s
            ap = arena[:, at:at + n]
            if len(shape) == 2:
                ap = ap.rearrange("p (a b) -> p a b", a=shape[0])
            if len(shape) == 3:
                ap = ap.rearrange("p (a b c) -> p a b c", a=shape[0], b=shape[1])
            return ap

        def in_slot(s, at, *shape):
            n = 1
            for v in shape:
                n *= v
            ap = ring[:, s, at:at + n]
            if len(shape) == 2:
                ap = ap.rearrange("p (a b) -> p a b", a=shape[0])
            if len(shape) == 3:
                ap = ap.rearrange("p (a b c) -> p a b c", a=shape[0], b=shape[1])
            return ap

        acc = region(0, 2, D)
        h2 = region(2048, 2, D)
        xgT = region(4096, 2, KB, P)
        oh = region(6144, 2, P)
        wo = region(6400, 2, P)
        woT = region(6656, 2, P)
        gate = region(6912, D)
        sig = region(7936, D)
        hid = region(8960, D)
        hT = region(9984, KB, P)
        yb = region(11008, D)
        sgA = region(0, KB, TOK)
        sgB = region(2048, KB, TOK)
        PTp = region(4096, HEADS, P)
        PTs = region(5120, 2, HEADS, P)
        xn = region(4096, 2, D)
        pooled = region(8192, 4, TOK)
        yT = region(9216, 4, TOK)
        modrow = region(10240, 3, HALF)
        modT = region(11776, 4, 8)
        knew = region(12288, HALF)
        h2T = region(4096, KB, TOK)
        bup = region(0, 2 * FF)
        brem = region(2048, 2 * FF)
        bada = gtf[:, :, :].rearrange("p a b -> p (a b)")[:, 0:3 * HALF].rearrange("p (a b) -> p a b", a=3)
        tmp = region(8192, 2, D)
        gfin = region(12032, D)
        hTm = in_slot(10, 0, KB, TOK)
        hT_top, hT_rest = (parts[:, s, :].rearrange("p (a b) -> p a b", a=KB) for s in (7, 10))
        w_top = parts[:, 6:9:2, 0:KB * P].rearrange("p u (a b) -> p u a b", a=KB)
        w_rest = parts[:, 6:9:2, KB * P:2 * KB * P].rearrange("p u (a b) -> p u a b", a=KB)
        yT_top, oT_top = (parts[:, 7, a:a + 1024].rearrange("p (a b) -> p a b", a=4) for a in (0, 1024))
        yT_rest, oT_rest = (parts[:, 10, a:a + 1024].rearrange("p (a b) -> p a b", a=4) for a in (0, 1024))
        biasM = in_slot(11, 0, HEADS, P)
        bias_rev = in_slot(13, 0, HEADS, P)
        flip = in_slot(12, 1664, P)
        kc = in_slot(11, 1024, HALF)
        vc = in_slot(11, 1536, HALF)
        upad = in_slot(12, 0, 4, 2, PW)
        kcT = in_slot(12, 1152, 4, P)
        Ss = in_slot(13, 0, HEADS, TOK)
        qT = in_slot(14, 0, 4, TOK)
        kT = in_slot(14, 1024, 4, TOK)
        Sp = in_slot(15, 0, HEADS, P)
        vm = in_slot(15, 1024, 2, HALF)
        gtm = in_slot(14, 0, 2, D)
        Af = in_slot(13, 0, 2, D)
        shf = in_slot(15, 0, 2, D)

        vecs = sb("vecs", [VEC, P])
        cT = sb("cT", [P, VEC])
        gffn = in_slot(9, 0, D)
        cs = in_slot(9, 1024, KB, 32)
        wpool = in_slot(9, 1280, 4, P)
        pscr = region(6144, 2, 2, PW)
        cnt = region(6720, 4, PW)
        wrt = sb("wrt", [P, KB, E])
        brt = sb("brt", [P, E])
        selrow = sb("selrow", [P, 2, P])
        tri = sb("tri", [P, P])
        ones = sb("ones", [P, P])
        rt = sb("rt", [P, 2, 8, E])

        Am = small[:, 0:16].rearrange("p (g k) -> p g k", g=2)
        ssq = small[:, 16:18]
        rstd = small[:, 18:20]
        mx = small[:, 20:36].rearrange("p (a b) -> p a b", a=2)
        ssum = small[:, 36:52].rearrange("p (a b) -> p a b", a=2)
        rsum = small[:, 52:68].rearrange("p (a b) -> p a b", a=2)
        top8 = small[:, 68:84].rearrange("p (a b) -> p a b", a=2)
        misc = small[:, 84:100]
        hsq = small[:, 100:108]

        ps = ctx.enter_context(nc.psum_tensor("ps", [P, 8, HALF], F32))

        pro_loaded = {s: sem(f"pro_loaded{s}") for s in sorted(set(mix_slot))}
        moe_loaded = [sem(f"moe_loaded{s}") for s in range(RING)]
        pro_used, moe_free = sem("pro_used"), sem("moe_free")
        L = {n: sem("ld_" + n) for n in ("vec", "x0", "x1", "bada", "bup", "gffn", "rpb", "kc", "vc", "wpool",
                                         "wrt", "brt", "bdn", "gfin")}
        pool_step, dve_step = sem("pool_step"), sem("dve_step")
        const_ready, bias_ready, split_done = sem("const_ready"), sem("bias_ready"), sem("split_done")
        vec_t, vec_c, silu_ready = sem("vec_t"), sem("vec_c"), sem("silu_ready")
        ssq_ready, root_ready, xn_ready = sem("ssq_ready"), sem("root_ready"), sem("xn_ready")
        kc_t, kcT_ready, x_t = sem("kc_t"), sem("kcT_ready"), sem("x_t")
        row_ready, modT_done, A_ready = sem("row_ready"), sem("modT_done"), sem("A_ready")
        hT_lo, hT_hi, z_read = sem("hT_lo"), sem("hT_hi"), sem("z_read")
        S_done, S_read, mx_ready, exp_done = sem("S_done"), sem("S_read"), sem("mx_ready"), sem("exp_done")
        prob_ready, PT_done, PT_read = sem("prob_ready"), sem("PT_done"), sem("PT_read")
        k_t, knew_ready = sem("k_t"), sem("knew_ready")
        O_done, oT_ready, pooled_ready, pool_done, yT_ready = (sem("O_done"), sem("oT_ready"), sem("pooled_ready"),
                                                               sem("pool_done"), sem("yT_ready"))
        bc_done, bc_read, Af_ready = sem("bc_done"), sem("bc_read"), sem("Af_ready")
        br_done, merged_ready = sem("br_done"), sem("merged_ready")
        x2_ready, h2_ready, h2_t, h2T_ready = sem("x2_ready"), sem("h2_ready"), sem("h2_t"), sem("h2T_ready")
        logit_done, mask_ready, rank_done, e_ready, top_ready = (sem("logit_done"), sem("mask_ready"),
                                                                 sem("rank_done"), sem("e_ready"), sem("top_ready"))
        comb_ready, comb_t, out_done, zeroed, acc_zero, mean_ready = (sem("comb_ready"), sem("comb_t"), sem("out_done"),
                                                                      sem("zeroed"), sem("acc_zero"), sem("mean_ready"))
        flag_ready, tab_ready, count_done = sem("flag_ready"), sem("tab_ready"), sem("count_done")
        oh_ready, wo_ready, gath_done, xg_ready, sel_ready = (sem("oh_ready"), sem("wo_ready"), sem("gath_done"),
                                                              sem("xg_ready"), sem("sel_ready"))
        u_read, g_ready, sig_ready, hid_ready = sem("u_read"), sem("g_ready"), sem("sig_ready"), sem("hid_ready")
        scat_done, acc_done, woT_done, woT_ready = sem("scat_done"), sem("acc_done"), sem("woT_done"), sem("woT_ready")
        hT_done, hTe_ready, y_ready = sem("hT_done"), sem("hTe_ready"), sem("y_ready")
        hT_split, unit_ready, unit_used = sem("hT_split"), sem("unit_ready"), sem("unit_used")
        yT_split, oT_top_ready, w_top_ready = sem("yT_split"), sem("oT_top_ready"), sem("w_top_ready")
        cur_ready, glu_ready = sem("cur_ready"), sem("glu_ready")
        fin_ss, fin_lo, fin_hi, last_scat, stored = (sem("fin_ss"), sem("fin_lo"), sem("fin_hi"), sem("last_scat"),
                                                     sem("stored"))
        xf_ready = sem("xf_ready")
        kv_stored, bias_t, bias_copied = sem("kv_stored"), sem("bias_t"), sem("bias_copied")

        GB, YB = 4, 6

        block = ctx.enter_context(nc.Block())

        def branch_block(eng, j):
            views = []
            for kind in ("pa", "pb"):
                for h in range(2):
                    c = AT[kind, 0, h]
                    eng.wait_ge(pro_loaded[mix_slot[c]], 16 * mix_held[c])
                s0 = mix_slot[AT[kind, 0, 0]]
                views.append(ring[:, s0:s0 + 2, :].rearrange("p s (k n) -> p (s k) n", k=2)[:, :, j * P:(j + 1) * P])
            return views

        def read_flags(eng):
            eng.wait_ge(flag_ready, 1)
            return [eng.value_load(flags[0:1, r:r + 1], min_val=0, max_val=1) for r in range(1, ROUNDS)]

        def further_rounds(eng, more, run, r=1):
            with eng.If(more[r - 1] > 0):
                run(r)
                if r + 1 < ROUNDS:
                    further_rounds(eng, more, run, r + 1)

        @block.sync
        def _(sp):
            def mixing_chunk(c):
                s = ring[:, mix_slot[c], :]
                kind, m, k = MIX[c]
                if kind == "ada":
                    return s, w_ada_v[:, k, m * SLOT:(m + 1) * SLOT]
                if kind == "in":
                    return (s.rearrange("p (k n) -> p k n", k=4),
                            w_in_v[:, 4 * k:4 * k + 4, m * HALF:(m + 1) * HALF])
                w = {"pa": w_pa_v, "pb": w_pb_v, "out": w_out_v}[kind]
                return s.rearrange("p (k n) -> p k n", k=2), w[:, 2 * k:2 * k + 2, :]

            for row, src in ((0, A_c_ctx), (8, A_c[0]), (16, A_g_mix[0])):
                sp.dma_start(vecs[row:row + 8, :], src.rearrange("(k p) -> k p", p=P)).then_inc(L["vec"], 16)
            sp.dma_start(vecs[24:28, :], A_pool_scale[0].rearrange("(k p) -> k p", p=P)).then_inc(L["vec"], 16)
            for c in range(len(MIX)):
                if mix_before[c] is not None:
                    sp.wait_ge(pro_used, mix_before[c] + 1)
                elif mix_slot[c] >= RING0:
                    sp.wait_ge(O_done, 1)
                if c == 2:
                    sp.dma_start(x[:, 0, :], A_x_prompt[0]).then_inc(L["x0"], 16)
                    sp.dma_start(x[:, 1, :], A_x_sample[0]).then_inc(L["x1"], 16)
                dst, src = mixing_chunk(c)
                sp.dma_start(dst, src).then_inc(pro_loaded[mix_slot[c]], 16)

            def stream(I, i):
                n0 = sp.snap(I * BC)
                for h in range(BODY):
                    for c in range(PC):
                        n = h * PC + c
                        a = c % 2
                        e = i * (2 * BODY) + (2 * h + a)
                        slot = ring[:, ORDER[n % RING], :]
                        sp.wait_ge(moe_free, n0 + (n + 1))
                        if c < UPC:
                            src = w_up_v[e, :, c // 2, :]
                            dst = slot
                        else:
                            f = 2 * ((c - UPC) // 2)
                            src = w_down_v[e, :, f:f + 2, :]
                            dst = slot.rearrange("p (k n) -> p k n", k=2)
                        sp.dma_start(dst, src).then_inc(moe_loaded[n % RING], 16)

            with sp.Fori(0, PAIRS // BODY) as i:
                stream(i, i)

            def run(r):
                with sp.Fori(0, PAIRS // BODY) as i:
                    stream(i + r * (PAIRS // BODY), i)
            further_rounds(sp, read_flags(sp), run)

            for t, y in enumerate((y_prompt, y_sample)):
                sp.wait_ge(fin_lo, t + 1)
                sp.wait_ge(fin_hi, t + 1)
                sp.dma_start(y[0], x[:, t, :]).then_inc(stored, 16)
            sp.wait_ge(stored, 32)
            sp.wait_ge(kv_stored, 32)

        @block.gpsimd
        def _(pool):
            def part_load(dst, src, s):
                pool.dma_start(dst, src).then_inc(s, 16)

            k = [0]

            def link(ins):
                k[0] += 1
                ins.then_inc(pool_step, 1)
                pool.wait_ge(pool_step, k[0])

            link(nc.gpsimd.memset(ident[:, :], 0.0))
            link(nc.gpsimd.affine_select(out=ident[:, :], in_=ident[:, :], compare_op=ALU.not_equal, fill=1.0,
                                         base=0, pattern=[[-1, P]], channel_multiplier=1))
            pool.sem_inc(const_ready, 1)
            link(nc.gpsimd.memset(mhalf[:, :], -0.5))
            link(nc.gpsimd.memset(flip, 0.0))
            for total in (GRID_W - 1, 3 * GRID_W - 1):
                link(nc.gpsimd.affine_select(out=flip, in_=flip, compare_op=ALU.not_equal, fill=1.0,
                                             base=-total, pattern=[[1, P]], channel_multiplier=1))
            pool.sem_inc(const_ready, 1)
            link(nc.gpsimd.memset(ones[:, :], 1.0))
            link(nc.gpsimd.memset(tri[:, :], 1.0))
            link(nc.gpsimd.memset(selrow[:, :, :], 0.0))
            link(nc.gpsimd.memset(sel[:, :], 1.0))
            link(nc.gpsimd.iota(iota_i[:, :], [[1, CAP]], base=0, channel_multiplier=0))
            link(nc.gpsimd.affine_select(out=tri[:, :], in_=tri[:, :], compare_op=ALU.is_gt, fill=0.0,
                                         base=0, pattern=[[1, P]], channel_multiplier=-1))
            for q in range(4):
                v = selrow[32 * q:32 * q + 32, :, :]
                link(nc.gpsimd.affine_select(out=v, in_=v, compare_op=ALU.not_equal, fill=1.0,
                                             base=0, pattern=[[-16, 2], [0, P]], channel_multiplier=1))
            for q in range(3):
                v = sel[32 * q:32 * q + 32, :]
                link(nc.gpsimd.affine_select(out=v, in_=v, compare_op=ALU.is_equal, fill=0.0,
                                             base=0, pattern=[[-1, E]], channel_multiplier=1))
            link(nc.gpsimd.tensor_copy(iota[:, :], iota_i[:, :]))
            pool.sem_inc(const_ready, 1)
            def root(n):
                pool.wait_ge(mean_ready, n + 1)
                nc.gpsimd.tensor_tensor(rstd[:, n % 2:n % 2 + 1], misc[:, n % 2:n % 2 + 1], mhalf[:, :],
                                        ALU.pow).then_inc(root_ready, 1)

            root(0)
            root(1)
            pool.wait_ge(pro_used, 5)
            part_load(kc, A_cache_k[0, 0].rearrange("h l d -> l h d"), L["kc"])
            for r in range(2):
                for kr in range(2):
                    for par in range(2):
                        at = par * RPB_H + (kr - r + WIN_R - 1) * RPB_W + WIN_C - GRID_W
                        src = bass.AP(A_rpb.tensor, A_rpb.offset + at,
                                      [[1, GRID_W], [2 * RPB_H, 4], [1, GRID_W]])
                        dst = bias_rev[64 * r:64 * r + 64, 4 * par:4 * par + 4, 64 * kr:64 * kr + 64]
                        part_load(dst, src, L["rpb"])
            part_load(wpool, A_w_pool[0].rearrange("g c d -> c g d"), L["wpool"])
            pool.wait_ge(bias_copied, 1)
            for q in range(3):
                part_load(bup[32 * q:32 * q + 32, :], A_b_up[0], L["bup"])
            part_load(vc.rearrange("p (h d) -> p h d", h=HEADS), A_cache_v[0, 0].rearrange("h l d -> l h d"), L["vc"])
            part_load(gffn, A_g_ffn.to_broadcast([P, D]), L["gffn"])
            part_load(wrt[:, :, :], A_w_router[0].rearrange("(k p) n -> p k n", p=P), L["wrt"])
            part_load(brt[:, :], A_b_router.to_broadcast([P, E]), L["brt"])
            for r in range(2):
                for kr in range(2):
                    v = biasM[64 * r:64 * r + 64, :, 64 * kr:64 * kr + GRID_W - WIN_C]
                    link(nc.gpsimd.affine_select(out=v, in_=v, compare_op=ALU.is_ge, fill=NEG, base=WIN_C // 2,
                                                 pattern=[[0, HEADS], [1, GRID_W - WIN_C]], channel_multiplier=-1))
                    v = biasM[64 * r:64 * r + 64, :, 64 * kr + WIN_C:64 * kr + GRID_W]
                    ins = nc.gpsimd.affine_select(out=v, in_=v, compare_op=ALU.is_ge, fill=NEG,
                                                  base=WIN_C // 2 - 1 - WIN_C,
                                                  pattern=[[0, HEADS], [-1, GRID_W - WIN_C]], channel_multiplier=1)
                    link(ins)
            pool.sem_inc(bias_ready, 1)
            pool.wait_ge(L["bup"], 48)
            link(nc.gpsimd.tensor_copy(bparts[:, :], bup[0:96, :]))
            for q in (1, 2):
                link(nc.gpsimd.tensor_tensor(brem[32 * q:32 * q + 32, :], bup[32 * q:32 * q + 32, :],
                                             bparts[32 * q:32 * q + 32, :], ALU.subtract))
                link(nc.gpsimd.tensor_copy(bparts[32 * q:32 * q + 32, :], brem[32 * q:32 * q + 32, :]))
            link(nc.gpsimd.tensor_tensor(bup[64:96, :], brem[64:96, :], bparts[64:96, :], ALU.subtract))
            nc.gpsimd.tensor_copy(bparts[64:96, :], bup[64:96, :]).then_inc(split_done, 1)
            pool.wait_ge(split_done, 1)
            pool.wait_ge(z_read, 4)
            pool.dma_start(new_v[0, 0].rearrange("h l d -> l h d"),
                           vm[:, 0, :].rearrange("p (h d) -> p h d", h=HEADS)).then_inc(kv_stored, 16)
            pool.wait_ge(knew_ready, 1)
            pool.dma_start(new_k[0, 0].rearrange("h l d -> l h d"),
                           knew.rearrange("p (h d) -> p h d", h=HEADS)).then_inc(kv_stored, 16)
            root(2)
            root(3)
            pool.wait_ge(moe_free, 12)
            nc.gpsimd.memset(acc, 0.0).then_inc(acc_zero, 1)

            def body(I, i):
                P0 = pool.snap(I * BODY)
                e0 = pool.snap(i * (2 * BODY))
                for h in range(BODY):
                    pool.wait_ge(u_read, P0 + (h + 1))
                    nc.gpsimd.tensor_copy(selbuf[:, :, :], sel[:, bass.ds(e0 + 2 * h, 2)].unsqueeze(2)
                                          .to_broadcast([96, 2, CAP])).then_inc(sel_ready, 1)

            more = read_flags(pool)
            with pool.Fori(0, PAIRS // BODY) as i:
                body(i, i)

            def run(r):
                with pool.Fori(0, PAIRS // BODY) as i:
                    body(i + r * (PAIRS // BODY), i)
            further_rounds(pool, more, run)
            root(4)
            root(5)

        @block.scalar
        def _(act):
            for q in range(4):
                src = A_b_ada[0].rearrange("(m q n) -> q m n", q=4, m=3)[q:q + 1]
                act.dma_start(bada[32 * q:32 * q + 32, :, :], src.to_broadcast([32, 3, HALF])).then_inc(L["bada"], 16)
            act.wait_ge(vec_c, 1)
            nc.scalar.activation(misc[:, 0:16], cT[:, 0:16], ACT.Sigmoid).then_inc(silu_ready, 1)
            for t in range(2):
                act.wait_ge(L[f"x{t}"], 16)
                nc.scalar.activation(xn[:, t, :], x[:, t, :], ACT.Square,
                                     accum_out=ssq[:, t:t + 1]).then_inc(ssq_ready, 1)
            act.wait_ge(A_ready, 1)
            act.wait_ge(x_t, 2)
            for j in range(4, KB):
                for t in range(2):
                    nc.scalar.activation(hTm[:, j, t * P:(t + 1) * P], ps[:, 2 + 2 * t, (j % 4) * P:(j % 4 + 1) * P],
                                         ACT.Identity, bias=modT[:, j % 4, 2 + t:3 + t],
                                         scale=Am[:, t, j:j + 1]).then_inc(hT_hi, 1)

            def z_out(cc):
                act.wait_ge(pro_used, AT["in", cc, 1] + 1)
                bank = 2 * (cc % 2)
                for b in range(2):
                    src = ps[:, bank + b, :]
                    if cc == 0:
                        dst, f = upad[:, 2 * b:2 * b + 2, :, PAD:PAD + P], ACT.Copy
                        src = src.rearrange("p (a t n) -> p a t n", a=2, t=2)
                    elif cc < 3:
                        dst, f = (qT, kT)[cc - 1][:, 2 * b:2 * b + 2, :], ACT.Copy
                        src = src.rearrange("p (a b) -> p a b", a=2)
                    elif cc == 3:
                        dst, f = vm[:, b, :], ACT.Copy
                    else:
                        g = sgA if cc < 6 else sgB
                        j = 4 * (cc % 2) + 2 * b
                        dst, f = g[:, j:j + 2, :], ACT.Sigmoid
                        src = src.rearrange("p (a b) -> p a b", a=2)
                    ins = nc.scalar.activation(dst, src, f)
                ins.then_inc(z_read, 1)

            act.wait_ge(pooled_ready, 1)
            z_out(0)
            act.wait_ge(kc_t, 1)
            nc.scalar.activation(kcT, ps[:, 6, :].rearrange("p (a b) -> p a b", a=4), ACT.Copy).then_inc(kcT_ready, 1)
            z_out(1)
            act.wait_ge(bias_t, 1)
            nc.scalar.activation(biasM, ps[:, 6:8, :].rearrange("p a (b c) -> p (a b) c", b=4), ACT.Copy)\
                .then_inc(bias_copied, 1)
            z_out(2)
            act.wait_ge(pool_done, 1)
            for g in range(4):
                ins = nc.scalar.activation(yT[:, g, :], ps[:, 6 + g // 2, (g % 2) * TOK:(g % 2 + 1) * TOK], ACT.Copy,
                                           scale=cT[:, 24 + g:25 + g])
            ins.then_inc(yT_ready, 1)
            z_out(3)
            act.wait_ge(mx_ready, 1)
            for hh in range(HEADS):
                nc.scalar.activation(Sp[:, hh, :], ps[:, 4 + hh // 4, (hh % 4) * P:(hh % 4 + 1) * P], ACT.Exp,
                                     bias=mx[:, 0, hh:hh + 1], scale=SCALE,
                                     accum_out=ssum[:, 0, hh:hh + 1]).then_inc(exp_done, 1)
            act.wait_ge(split_done, 1)
            z_out(4)
            act.wait_ge(k_t, 1)
            nc.scalar.activation(knew, ps[:, 6, :], ACT.Copy).then_inc(knew_ready, 1)
            act.wait_ge(mx_ready, 2)
            for hh in range(HEADS):
                nc.scalar.activation(Ss[:, hh, :], Ss[:, hh, :], ACT.Exp, bias=mx[:, 1, hh:hh + 1],
                                     accum_out=ssum[:, 1, hh:hh + 1]).then_inc(exp_done, 1)

            def pt_out(n):
                act.wait_ge(PT_done, n + 1)
                bank = (6, 4, 6)[n]
                dst = (PTp, PTs[:, 0], PTs[:, 1])[n]
                for b in range(2):
                    ins = nc.scalar.activation(dst[:, 4 * b:4 * b + 4, :],
                                               ps[:, bank + b, :].rearrange("p (a b) -> p a b", a=4), ACT.Copy)
                ins.then_inc(PT_read, 1)

            z_out(5)
            pt_out(0)
            z_out(6)
            pt_out(1)
            z_out(7)
            pt_out(2)

            def mod_out(n):
                m, t = n // 2, n % 2
                act.wait_ge(bc_done, n + 1)
                if m == 0:
                    nc.scalar.activation(gtm[:, t, :].rearrange("p (a b) -> p a b", a=2), ps[:, 2:4, :], ACT.Copy)
                    nc.scalar.activation(shf[:, t, :].rearrange("p (a b) -> p a b", a=2), ps[:, 4:6, :],
                                         ACT.Copy).then_inc(bc_read, 1)
                else:
                    nc.scalar.activation(gtf[:, t, :].rearrange("p (a b) -> p a b", a=2), ps[:, 4:6, :],
                                         ACT.Copy).then_inc(bc_read, 1)

            def branch_top(j):
                if j < 2:
                    act.wait_ge(unit_used, 15 + j)
                else:
                    act.wait_ge(br_done, j - 1)
                for n, w in enumerate(branch_block(act, j)):
                    ins = nc.scalar.activation(w_top[:, j % 2, 4 * n:4 * n + 4, :], w, ACT.Copy)
                ins.then_inc(w_top_ready, 1)

            branch_top(0)
            branch_top(1)
            mod_out(0)
            act.wait_ge(O_done, 1)
            for t in range(2):
                nc.scalar.activation(oT_top[:, :, t * P:(t + 1) * P], ps[:, t, :].rearrange("p (a b) -> p a b", a=4),
                                     ACT.Copy).then_inc(oT_top_ready, 1)
            for j in range(2, KB):
                branch_top(j)
                if j % 2 == 0:
                    mod_out(j // 2)
            act.dma_start(gfin, A_g_final.rearrange("(a n) -> a n", a=1).to_broadcast([P, D])).then_inc(L["gfin"], 16)
            act.wait_ge(zeroed, 1)
            act.dma_start(yb[0:E, :], A_b_down[0]).then_inc(L["bdn"], 16)
            def squares(t, ready):
                for n in range(2):
                    c = slice(n * HALF, (n + 1) * HALF)
                    act.wait_ge(ready, 2 * t + n + 1)
                    nc.scalar.activation(h2[:, t, c], x[:, t, c], ACT.Square, scale=D ** -0.5,
                                         accum_out=hsq[:, 2 * t + n:2 * t + n + 1]).then_inc(ssq_ready, 1)

            def exp_logits(t):
                act.wait_ge(top_ready, t + 1)
                nc.scalar.activation(rt[:, t, 1, :], rt[:, t, 0, :], ACT.Exp, bias=misc[:, 4 + t:5 + t]).then_inc(e_ready, 1)

            squares(0, x2_ready)
            for b in range(4):
                if b == 2:
                    squares(1, x2_ready)
                    nc.scalar.activation(misc[:, 12:13], mhalf[:, :], ACT.Exp)
                act.wait_ge(h2_t, b + 1)
                t, jh = b // 2, b % 2
                nc.scalar.activation(h2T[:, 4 * jh:4 * jh + 4, t * P:(t + 1) * P],
                                     ps[:, 4 + jh, :].rearrange("p (a b) -> p a b", a=4), ACT.Copy).then_inc(h2T_ready, 1)
            for t in range(2):
                exp_logits(t)
            act.wait_ge(comb_t, 1)
            nc.scalar.activation(woT[0:E, :, :], ps[0:E, 6, 0:TOK].rearrange("p (a b) -> p a b", a=2),
                                 ACT.Copy).then_inc(woT_ready, 1)
            act.wait_ge(L["bdn"], 16)
            act.sem_inc(y_ready, 1)

            def xg_out(b, H, q):
                act.wait_ge(gath_done, H + 1)
                nc.scalar.activation(xgT[:, q, 4 * b:4 * b + 4, :],
                                     ps[:, GB + b, :].rearrange("p (a b) -> p a b", a=4), ACT.Copy).then_inc(xg_ready, 1)

            def body(I, r):
                P0 = act.snap(I * BODY)
                n0 = act.snap(I * BC)
                H0 = act.snap(P0 * 2 + (r + 1))
                for h in range(BODY):
                    Pn, H = P0 + h, H0 + 2 * h
                    xg_out(1, H, h)
                    for b in range(2):
                        act.wait_ge(g_ready, Pn * 2 + (b + 1))
                        nc.scalar.activation(sig[:, b * HALF:(b + 1) * HALF], gate[:, b * HALF:(b + 1) * HALF],
                                             ACT.Sigmoid, scale=ALPHA).then_inc(sig_ready, 1)
                    xg_out(0, H + 1, (h + 1) % 2)
                    act.wait_ge(woT_done, Pn + 2)
                    nc.scalar.activation(woT, ps[:, YB, 0:TOK].rearrange("p (a b) -> p a b", a=2),
                                         ACT.Copy).then_inc(woT_ready, 1)
                    for b in range(2):
                        act.wait_ge(hT_done, Pn * 2 + (b + 1))
                        nc.scalar.activation(hT[:, 4 * b:4 * b + 4, :],
                                             ps[:, GB + b, :].rearrange("p (a b) -> p a b", a=4),
                                             ACT.Copy).then_inc(hTe_ready, 1)
                    act.wait_ge(moe_free, n0 + (RING + (h + 1) * PC))
                    nc.scalar.activation(yb.rearrange("p (a b) -> p a b", a=2), ps[:, YB:YB + 2, :],
                                         ACT.Copy).then_inc(y_ready, 1)

            xg_out(0, 0, 0)
            more = read_flags(act)
            with act.Fori(0, PAIRS // BODY) as i:
                body(i, 0)

            def run(r):
                xg_out(0, r * (2 * PAIRS + 1), 0)
                with act.Fori(0, PAIRS // BODY) as i:
                    body(i + r * (PAIRS // BODY), r)
            further_rounds(act, more, run)

            for t in range(2):
                squares(t, fin_ss)
            for t in range(2):
                act.wait_ge(xf_ready, 2 * t + 1)
                act.wait_ge(root_ready, 5 + t)
                nc.scalar.activation(x[:, t, 0:HALF], x[:, t, 0:HALF], ACT.Copy,
                                     scale=rstd[:, t:t + 1]).then_inc(fin_lo, 1)

        @block.vector
        def _(dve):
            k = [0]

            def link(ins):
                k[0] += 1
                ins.then_inc(dve_step, 1)
                dve.wait_ge(dve_step, k[0])

            V = nc.vector

            def mean(n):
                t = n % 2
                dve.wait_ge(ssq_ready, n + 1)
                V.tensor_scalar(misc[:, t:t + 1], ssq[:, t:t + 1], 1.0 / D, EPS, ALU.mult, ALU.add).then_inc(mean_ready, 1)

            def mean_of_halves(t, n):
                dve.wait_ge(ssq_ready, 2 + 4 * n + 2 * t + 2)
                V.tensor_scalar(misc[:, t:t + 1], hsq[:, 2 * t:2 * t + 1], hsq[:, 2 * t + 1:2 * t + 2], EPS, ALU.add,
                                ALU.add).then_inc(mean_ready, 1)

            def doubled(dst, src, s):
                lo, hi = 1 << s, PW - (1 << s) + 1
                a, b = (1, 0) if s == 0 else (1 << s >> 1, 1 << s >> 1)
                return V.tensor_tensor(dst[..., lo:hi], src[..., lo - a:hi - a], src[..., lo + b:hi + b], ALU.add)

            V.memset(pscr[:, :, :, :], 0.0)
            link(V.memset(cnt[:, :, :], 0.0))
            link(V.memset(pscr[:, 0, 0, PAD:PAD + P], 1.0))
            for g in range(4):
                src, dst = pscr[:, g % 2, 0, :], (pscr[:, (g + 1) % 2, 0, :])
                v = slice(PAD, PAD + P)
                link(doubled(dst, src, g))
                link(V.tensor_copy(cnt[:, g, v], dst[:, v]))
            V.memset(upad[:, :, :, 0:PAD], 0.0)
            link(V.memset(upad[:, :, :, PAD + P:PW], 0.0))

            dve.wait_ge(vec_t, 1)
            V.tensor_copy(cT[:, :], ps[:, 7, 0:VEC]).then_inc(vec_c, 1)
            dve.wait_ge(silu_ready, 1)
            for g in range(2):
                ins = V.tensor_tensor(cs[:, :, 16 * g:16 * g + 16],
                                      cT[:, 8 * g:8 * g + 8].unsqueeze(2).to_broadcast([P, KB, 16]),
                                      misc[:, 8 * g:8 * g + 8].unsqueeze(2).to_broadcast([P, KB, 16]), ALU.mult)
            ins.then_inc(silu_ready, 1)

            dve.wait_ge(silu_ready, 2)
            for t in range(2):
                mean(t)
            for t in range(2):
                dve.wait_ge(root_ready, t + 1)
                V.tensor_scalar(xn[:, t, :], x[:, t, :], rstd[:, t:t + 1], None, ALU.mult).then_inc(xn_ready, 1)

            def mod_rows(m, bank):
                dve.wait_ge(pro_used, AT["ada", m, KB - 1] + 1)
                dve.wait_ge(L["bada"], 64)
                V.tensor_tensor(modrow[:, m, :], ps[:, bank, :], bada[:, m, :], ALU.add).then_inc(row_ready, 1)

            mod_rows(0, 0)
            dve.wait_ge(modT_done, 1)
            link(V.tensor_copy(modT, ps[:, 5, :].rearrange("p (a b) -> p a b", a=4)[:, :, 0:P:16]))
            for g in range(2):
                for hi in range(2):
                    at = 4 + 2 * hi + g
                    ins = V.scalar_tensor_tensor(out=Am[:, g, 4 * hi:4 * hi + 4], in0=modT[:, :, at], scalar=1.0,
                                                 in1=cT[:, 16 + 4 * hi:20 + 4 * hi], op0=ALU.add, op1=ALU.mult)
            ins.then_inc(A_ready, 1)
            dve.wait_ge(A_ready, 1)
            dve.wait_ge(x_t, 2)
            for j in range(4):
                for t in range(2):
                    V.tensor_scalar(hTm[:, j, t * P:(t + 1) * P], ps[:, 1 + 2 * t, j * P:(j + 1) * P],
                                    Am[:, t, j:j + 1], modT[:, j, t:t + 1], ALU.mult,
                                    ALU.add).then_inc(hT_lo, 1)
            dve.sem_inc(pooled_ready, 1)

            dve.wait_ge(z_read, 1)
            link(V.memset(pscr[:, :, :, :], 0.0))
            for g in range(4):
                src = upad[:, g, :, :]
                for s in range(g + 1):
                    dst = pscr[:, s % 2, :, :]
                    link(doubled(dst, src, s))
                    src = dst
                if g == 0:
                    link(V.reciprocal(cnt[:, :, PAD:PAD + P], cnt[:, :, PAD:PAD + P]))
                o = pooled[:, g, :].rearrange("p (t n) -> p t n", t=2)
                link(V.tensor_tensor(o, src[:, :, PAD:PAD + P],
                                     cnt[:, g:g + 1, PAD:PAD + P].to_broadcast([P, 2, P]), ALU.mult))
                ins = V.tensor_tensor(o, o, upad[:, g, :, PAD:PAD + P], ALU.subtract)
                if g < 3:
                    link(ins)
            ins.then_inc(pooled_ready, 1)
            mod_rows(1, 4)
            dve.wait_ge(pro_used, NARROW - 1)
            dve.wait_ge(hT_hi, 8)
            V.tensor_copy(hT_top, hTm).then_inc(hT_split, 1)
            dve.wait_ge(hT_split, 1)
            dve.wait_ge(pro_used, AT["in", 3, 1] + 1)
            V.tensor_tensor(hT_rest, hTm, hT_top.bitcast(F32), ALU.subtract).then_inc(hT_split, 1)

            def split(n):
                cc, b = 4 + n // 4, n % 4
                if n >= 2:
                    dve.wait_ge(unit_used, n - 1)
                w = []
                for h in range(2):
                    c = AT["in", cc, h]
                    dve.wait_ge(pro_loaded[mix_slot[c]], 16 * mix_held[c])
                    w.append(ring[:, mix_slot[c], :].rearrange("p (k n) -> p k n", k=4)[:, :, b * P:(b + 1) * P])
                for h in range(2):
                    ins = V.tensor_copy(w_top[:, n % 2, 4 * h:4 * h + 4, :], w[h])
                link(ins)
                for h in range(2):
                    ins = V.tensor_tensor(w_rest[:, n % 2, 4 * h:4 * h + 4, :], w[h],
                                          w_top[:, n % 2, 4 * h:4 * h + 4, :].bitcast(F32), ALU.subtract)
                ins.then_inc(unit_ready, 1)

            mod_rows(2, 5)
            split(0)
            split(1)
            dve.wait_ge(S_done, 1)
            link(V.tensor_reduce(mx[:, 0, :], ps[:, 4:6, :].rearrange("p a (b n) -> p (a b) n", b=4), AX.X, ALU.max))
            V.tensor_scalar(mx[:, 0, :], mx[:, 0, :], -SCALE, None, ALU.mult).then_inc(mx_ready, 1)
            dve.wait_ge(S_done, 2)
            dve.wait_ge(bias_ready, 1)
            for b in range(2):
                V.scalar_tensor_tensor(out=Ss[:, 4 * b:4 * b + 4, 0:P],
                                       in0=ps[:, 6 + b, :].rearrange("p (a b) -> p a b", a=4), scalar=SCALE,
                                       in1=biasM[:, 4 * b:4 * b + 4, :], op0=ALU.mult, op1=ALU.add)\
                    .then_inc(S_read, 1)

            def normalise(n, S, width):
                dve.wait_ge(exp_done, HEADS * (n + 1))
                link(V.reciprocal(rsum[:, n, :], ssum[:, n, :]))
                V.tensor_tensor(S, S, rsum[:, n, :].unsqueeze(2).to_broadcast([P, HEADS, width]),
                                ALU.mult).then_inc(prob_ready, 1)

            split(2)
            split(3)
            normalise(0, Sp, P)
            split(4)
            split(5)
            dve.wait_ge(S_done, 3)
            for b in range(2):
                link(V.tensor_scalar(Ss[:, 4 * b:4 * b + 4, P:TOK],
                                     ps[:, 4 + b, :].rearrange("p (a b) -> p a b", a=4), SCALE, None, ALU.mult))
            V.tensor_reduce(mx[:, 1, :], Ss, AX.X, ALU.max, negate=True).then_inc(mx_ready, 1)
            for n in range(6, 10):
                split(n)
            normalise(1, Ss, TOK)
            for n in range(10, 16):
                split(n)

            dve.wait_ge(yT_ready, 1)
            dve.wait_ge(unit_used, 16)
            V.tensor_copy(yT_top, yT).then_inc(yT_split, 1)
            dve.wait_ge(yT_split, 1)
            V.tensor_tensor(yT_rest, yT, yT_top.bitcast(F32), ALU.subtract).then_inc(yT_split, 1)

            def branch_rest(j):
                dve.wait_ge(w_top_ready, j + 1)
                for n, w in enumerate(branch_block(dve, j)):
                    ins = V.tensor_tensor(w_rest[:, j % 2, 4 * n:4 * n + 4, :], w,
                                          w_top[:, j % 2, 4 * n:4 * n + 4, :].bitcast(F32), ALU.subtract)
                ins.then_inc(unit_ready, 1)

            branch_rest(0)
            branch_rest(1)
            for t in range(2):
                dve.wait_ge(oT_top_ready, t + 1)
                c = slice(t * P, (t + 1) * P)
                V.tensor_tensor(oT_rest[:, :, c], ps[:, t, :].rearrange("p (a b) -> p a b", a=4),
                                oT_top[:, :, c].bitcast(F32), ALU.subtract).then_inc(oT_ready, 1)
            dve.wait_ge(L["gffn"], 16)

            def scale_out(t):
                dve.wait_ge(bc_done, 3 + t)
                V.scalar_tensor_tensor(out=Af[:, t, :], in0=ps[:, 2:4, :].rearrange("p a b -> p (a b)"), scalar=1.0,
                                       in1=gffn, op0=ALU.add, op1=ALU.mult).then_inc(Af_ready, 1)

            for j in range(KB):
                if j in (3, 5):
                    scale_out((j - 3) // 2)
                dve.wait_ge(br_done, j + 1)
                b = 6 + j % 2
                V.tensor_tensor(sgA[:, j, :], ps[:, b, 0:TOK], sgA[:, j, :], ALU.mult)
                link(V.tensor_tensor(sgB[:, j, :], ps[:, b, TOK:HALF], sgB[:, j, :], ALU.mult))
                V.tensor_tensor(sgA[:, j, :], sgA[:, j, :], sgB[:, j, :], ALU.add).then_inc(merged_ready, 1)
                if j + 2 < KB:
                    branch_rest(j + 2)
            V.memset(woT, 0.0)
            V.memset(yb, 0.0).then_inc(zeroed, 1)
            def residual(t):
                for n in range(2):
                    c = slice(n * HALF, (n + 1) * HALF)
                    if (t, n) == (1, 1):
                        dve.wait_ge(moe_free, 12)
                    else:
                        dve.wait_ge(out_done, 2 * t + n + 1)
                    if t == 0 and n == 0:
                        dve.wait_ge(bc_read, 2)
                    link(V.tensor_tensor(tmp[:, t, c], ps[:, 2 * t + n, :], gtm[:, t, c], ALU.mult))
                    V.tensor_tensor(x[:, t, c], x[:, t, c], tmp[:, t, c], ALU.add).then_inc(x2_ready, 1)

            def norm(t):
                mean_of_halves(t, 0)
                dve.wait_ge(root_ready, 3 + t)
                for n in range(2):
                    c = slice(n * HALF, (n + 1) * HALF)
                    link(V.scalar_tensor_tensor(out=h2[:, t, c], in0=x[:, t, c], scalar=rstd[:, t:t + 1],
                                                in1=Af[:, t, c], op0=ALU.mult, op1=ALU.mult))
                    V.tensor_tensor(h2[:, t, c], h2[:, t, c], shf[:, t, c], ALU.add).then_inc(h2_ready, 1)

            def choose(t):
                dve.wait_ge(logit_done, t + 1)
                R = [rt[:, t, n, :] for n in range(8)]
                link(V.tensor_tensor(R[0], ps[:, t, 0:E], brt[:, :], ALU.add))
                link(V.max(top8[:, t, :], R[0]))
                V.tensor_scalar(misc[:, 4 + t:5 + t], top8[:, t, 0:1], -1.0, None, ALU.mult).then_inc(top_ready, 1)
                fourth = top8[:, t, TOPK - 1:TOPK]
                link(V.tensor_scalar(R[2], R[0], fourth, None, ALU.is_gt))
                V.tensor_scalar(R[3], R[0], fourth, None, ALU.is_equal)
                link(V.tensor_reduce(misc[:, 6 + t:7 + t], R[2], AX.X, ALU.add))
                link(V.tensor_tensor_scan(R[4], ones[:, 0:E], R[3], misc[:, 6 + t:7 + t], ALU.mult, ALU.add))
                link(V.scalar_tensor_tensor(out=R[3], in0=R[4], scalar=float(TOPK), in1=R[3], op0=ALU.is_le,
                                            op1=ALU.mult))
                V.tensor_tensor(R[5], R[2], R[3], ALU.add).then_inc(mask_ready, 1)

            def weigh(t):
                R = [rt[:, t, n, :] for n in range(8)]
                dve.wait_ge(mask_ready, t + 1)
                dve.wait_ge(e_ready, t + 1)
                link(V.tensor_tensor(R[6], R[1], R[5], ALU.mult))
                link(V.tensor_reduce(misc[:, 2 + t:3 + t], R[6], AX.X, ALU.add))
                link(V.reciprocal(misc[:, 2 + t:3 + t], misc[:, 2 + t:3 + t]))
                V.tensor_scalar(R[6], R[6], misc[:, 2 + t:3 + t], None, ALU.mult).then_inc(comb_ready, 1)
                dve.wait_ge(comb_ready, t + 1)

            def tabulate(t):
                dve.wait_ge(rank_done, t + 1)
                R = [rt[:, t, n, :] for n in range(8)]
                pairs = tab[:, 0:PAIRS, :]
                link(V.scalar_tensor_tensor(out=R[7], in0=ps[:, 6 + t, 0:E], scalar=1.0, in1=R[5], op0=ALU.add,
                                            op1=ALU.mult))
                V.tensor_scalar(pairs[:, :, 2 * t:2 * t + 2], R[7].rearrange("p (a b) -> p a b", b=2), 1.0, None,
                                ALU.subtract)
                link(V.tensor_copy(pairs[:, :, 4 + 2 * t:6 + 2 * t], R[6].rearrange("p (a b) -> p a b", b=2)))

            residual(0)
            norm(0)
            dve.wait_ge(L["brt"], 16)
            dve.wait_ge(const_ready, 3)
            V.memset(tab[:, PAIRS, :], -1.0)
            residual(1)
            norm(1)
            dve.wait_ge(h2_ready, 4)
            dve.sem_inc(moe_free, 4)
            choose(0)
            weigh(0)
            choose(1)
            tabulate(0)
            weigh(1)
            tabulate(1)

            def one_hots(p, G):
                V.tensor_copy(cur[:, :], tab[:, bass.ds(p, 1), :].rearrange("p a b -> p (a b)")).then_inc(cur_ready, 1)
                dve.wait_ge(cur_ready, G + 1)
                for t in range(2):
                    for a in range(2):
                        ins = V.tensor_scalar(oh[:, t, CAP * a:CAP * a + CAP], iota[:, :], cur[:, 2 * t + a:2 * t + a + 1],
                                              None, ALU.is_equal)
                ins.then_inc(oh_ready, 1)

            def add_acc(Pn, n):
                t, c = n // 2, slice((n % 2) * HALF, (n % 2 + 1) * HALF)
                dve.wait_ge(scat_done, Pn * 4 + (n + 1))
                V.tensor_tensor(acc[:, t, c], ps[:, GB + n, :], acc[:, t, c], ALU.add).then_inc(acc_done, 1)

            def body(I, i, r):
                P0 = dve.snap(I * BODY)
                G0 = dve.snap(P0 + (r + 1))
                H0 = dve.snap(P0 * 2 + (r + 2))
                p0 = dve.snap(i * BODY)
                n0 = dve.snap(I * BC)
                for h in range(BODY):
                    Pn, G = P0 + h, G0 + h
                    dve.wait_ge(woT_done, Pn + 1)
                    dve.wait_ge(oh_ready, G)
                    for t in range(2):
                        for a in range(2):
                            ins = V.tensor_scalar(wo[:, t, CAP * a:CAP * a + CAP], oh[:, t, CAP * a:CAP * a + CAP],
                                                  cur[:, 4 + 2 * t + a:5 + 2 * t + a], None, ALU.mult)
                    ins.then_inc(wo_ready, 1)
                    dve.wait_ge(wo_ready, Pn + 1)
                    dve.wait_ge(gath_done, H0 + 2 * h)
                    one_hots(p0 + (h + 1), G)
                    dve.wait_ge(moe_free, n0 + (RING + h * PC + UPC))
                    for b in range(2):
                        V.tensor_scalar(gate[:, b * HALF:(b + 1) * HALF], ps[:, b, :], LIMIT, None,
                                        ALU.min).then_inc(g_ready, 1)
                    V.tensor_scalar(hid, ps[:, 2:4, :].rearrange("p a b -> p (a b)"), LIMIT, -LIMIT, ALU.min,
                                    ALU.max).then_inc(u_read, 1)
                    add_acc(Pn, 0)
                    add_acc(Pn, 1)
                    dve.wait_ge(u_read, Pn + 2)
                    for b in range(2):
                        c = slice(b * HALF, (b + 1) * HALF)
                        dve.wait_ge(sig_ready, Pn * 2 + (b + 1))
                        V.tensor_tensor(sig[:, c], sig[:, c], gate[:, c], ALU.mult).then_inc(glu_ready, 1)
                        dve.wait_ge(glu_ready, Pn * 2 + (b + 1))
                        V.scalar_tensor_tensor(out=hid[:, c], in0=hid[:, c], scalar=1.0, in1=sig[:, c],
                                               op0=ALU.add, op1=ALU.mult).then_inc(hid_ready, 1)
                    add_acc(Pn, 2)
                    add_acc(Pn, 3)

            one_hots(0, 0)
            dve.wait_ge(count_done, 1)
            link(V.tensor_reduce(misc[:, 9:10], ps[:, 3, 0:E], AX.X, ALU.max))
            for r in range(ROUNDS):
                ins = V.tensor_scalar(flags[:, r:r + 1], misc[:, 9:10], float(CAP * r), None, ALU.is_gt)
            ins.then_inc(flag_ready, 1)
            dve.sem_inc(u_read, 1)
            dve.wait_ge(acc_zero, 1)
            more = read_flags(dve)
            with dve.Fori(0, PAIRS // BODY) as i:
                body(i, i, 0)
            dve.wait_ge(acc_done, 4 * PAIRS)

            def run(r):
                dve.wait_ge(oh_ready, r * (PAIRS + 1))
                V.tensor_scalar(tab[:, :, 0:4], tab[:, :, 0:4], float(CAP), None, ALU.subtract).then_inc(tab_ready, 1)
                dve.wait_ge(tab_ready, r)
                dve.wait_ge(gath_done, r * (2 * PAIRS + 1))
                one_hots(0, r * (PAIRS + 1))
                with dve.Fori(0, PAIRS // BODY) as i:
                    body(i + r * (PAIRS // BODY), i, r)
                dve.wait_ge(acc_done, 4 * (r + 1) * PAIRS)
            further_rounds(dve, more, run)

            link(V.tensor_tensor(acc, acc, gtf[:, :, :], ALU.mult))
            link(V.tensor_tensor(x[:, :, :], x[:, :, :], acc, ALU.add))

            def last_add(t):
                for n in range(2):
                    c = slice(n * HALF, (n + 1) * HALF)
                    dve.wait_ge(last_scat, 2 * t + n + 1)
                    link(V.tensor_tensor(acc[:, t, c], ps[:, GB + 2 * t + n, :], gtf[:, t, c], ALU.mult))
                    V.tensor_tensor(x[:, t, c], x[:, t, c], acc[:, t, c], ALU.add).then_inc(fin_ss, 1)

            def last_gain(t):
                for n in range(2):
                    c = slice(n * HALF, (n + 1) * HALF)
                    dve.wait_ge(ssq_ready, 6 + 2 * t + n + 1)
                    V.tensor_tensor(x[:, t, c], x[:, t, c], gfin[:, c], ALU.mult).then_inc(xf_ready, 1)

            def last_scale(t):
                dve.wait_ge(xf_ready, 2 * t + 2)
                dve.wait_ge(root_ready, 5 + t)
                V.tensor_scalar(x[:, t, HALF:D], x[:, t, HALF:D], rstd[:, t:t + 1], None, ALU.mult).then_inc(fin_hi, 1)

            dve.wait_ge(L["gfin"], 16)
            last_add(0)
            last_add(1)
            mean_of_halves(0, 1)
            last_gain(0)
            last_scale(0)
            mean_of_halves(1, 1)
            last_gain(1)
            last_scale(1)

        @block.tensor
        def _(pe):
            mm, tp = nc.tensor.matmul, nc.tensor.transpose

            def landed(c):
                pe.wait_ge(pro_loaded[mix_slot[c]], 16 * mix_held[c])
                return ring[:, mix_slot[c], :]

            pe.wait_ge(L["vec"], 64)
            pe.wait_ge(const_ready, 1)
            tp(ps[:, 7, 0:VEC], vecs[:, :], ident[0:VEC, 0:VEC]).then_inc(vec_t, 1)

            def modulation(m, bank, ks):
                for kk in ks:
                    w = landed(AT["ada", m, kk])
                    for q in range(4):
                        ins = mm(ps[32 * q:32 * q + 32, bank, :], cs[:, kk, :], w[:, q * HALF:(q + 1) * HALF],
                                 start=(kk == 0), stop=(kk == KB - 1))
                    ins.then_inc(pro_used, 1)

            def keep_busy(n, bank):
                for _ in range(n):
                    mm(ps[:, bank, 0:TOK], tri[:, :], selrow[:, :, :].rearrange("p a b -> p (a b)"), start=True, stop=True)

            def project(cc):
                if cc >= 2:
                    pe.wait_ge(z_read, cc - 1)
                bank = 2 * (cc % 2)
                w = [landed(AT["in", cc, h]).rearrange("p (k n) -> p k n", k=4) for h in range(2)]
                last = 1 if cc == 3 else 3
                for b in range(last + 1):
                    for kk in range(KB):
                        if cc == 0 and b == 0:
                            pe.wait_ge(hT_lo if kk < 4 else hT_hi, 2 * (kk % 4 + 1))
                        wk = w[kk // 4][:, kk % 4, :]
                        if cc == 3:
                            ins = mm(ps[:, bank + b, :], hTm[:, kk, b * P:(b + 1) * P], wk,
                                     start=(kk == 0), stop=(kk == KB - 1))
                        else:
                            ins = mm(ps[:, bank + b // 2, (b % 2) * TOK:(b % 2 + 1) * TOK], wk[:, b * P:(b + 1) * P],
                                     hTm[:, kk, :], start=(kk == 0), stop=(kk == KB - 1))
                        if b == last and kk % 4 == 3:
                            ins.then_inc(pro_used, 1)

            def project_gate(cc):
                pe.wait_ge(z_read, cc - 1)
                bank = 2 * (cc % 2)
                for b in range(4):
                    n = 4 * (cc - 4) + b
                    pe.wait_ge(unit_ready, n + 1)
                    out = ps[:, bank + b // 2, (b % 2) * TOK:(b % 2 + 1) * TOK]
                    for kk in range(KB):
                        mm(out, w_top[:, n % 2, kk, :], hT_top[:, kk, :], start=(kk == 0), stop=False)
                        mm(out, w_top[:, n % 2, kk, :], hT_rest[:, kk, :], start=False, stop=False)
                        ins = mm(out, w_rest[:, n % 2, kk, :], hT_top[:, kk, :], start=False, stop=(kk == KB - 1))
                    ins.then_inc(unit_used, 1)
                pe.wait_ge(unit_used, 4 * (cc - 3))
                pe.sem_inc(pro_used, 2)

            pe.wait_ge(silu_ready, 2)
            modulation(0, 0, range(5))
            for t in range(2):
                pe.wait_ge(xn_ready, t + 1)
                for j in range(KB):
                    ins = tp(ps[:, 1 + 2 * t + j // 4, (j % 4) * P:(j % 4 + 1) * P], xn[:, t, j * P:(j + 1) * P], ident[:, :])
                ins.then_inc(x_t, 1)
            modulation(0, 0, range(5, KB))
            pe.wait_ge(row_ready, 1)
            for j in range(4):
                ins = tp(ps[:, 5, j * P:(j + 1) * P], modrow[:, 0, j * P:(j + 1) * P], ident[:, :])
            ins.then_inc(modT_done, 1)
            pe.wait_ge(const_ready, 3)
            keep_busy(5, 7)

            def scores(n, keys, bank):
                for h in range(HEADS):
                    b, o = h // 2, DH * (h % 2)
                    ins = mm(ps[:, bank + h % 2, b * P:(b + 1) * P], qT[o:o + DH, b, (n > 0) * P:(n > 0) * P + P],
                             keys[o:o + DH, b, :], start=True, stop=True)
                ins.then_inc(S_done, 1)

            def prob_t(src, bank):
                for hh in range(HEADS):
                    ins = tp(ps[:, bank + hh // 4, (hh % 4) * P:(hh % 4 + 1) * P], src[:, hh, :], ident[:, :])
                ins.then_inc(PT_done, 1)

            project(0)
            modulation(1, 4, range(4))
            pe.wait_ge(L["kc"], 16)
            for b in range(4):
                ins = tp(ps[:, 6, b * P:(b + 1) * P], kc[:, b * P:(b + 1) * P], ident[:, :])
            ins.then_inc(kc_t, 1)
            project(1)
            modulation(1, 4, range(4, KB))
            pe.wait_ge(L["rpb"], 16 * 8)
            pe.wait_ge(const_ready, 2)
            pe.wait_ge(kcT_ready, 1)
            for b in range(2):
                ins = mm(ps[:, 6 + b, :], flip, bias_rev[:, 4 * b:4 * b + 4, :], start=True, stop=True)
            ins.then_inc(bias_t, 1)
            project(2)
            modulation(2, 5, range(4))
            project(3)
            pe.wait_ge(bias_copied, 1)
            pe.wait_ge(pooled_ready, 2)
            pe.wait_ge(L["wpool"], 16)
            for g in range(4):
                ins = mm(ps[:, 6 + g // 2, (g % 2) * TOK:(g % 2 + 1) * TOK], wpool[:, g, :], pooled[:, g, :],
                         start=True, stop=True)
            ins.then_inc(pool_done, 1)
            modulation(2, 5, range(4, KB))
            pe.wait_ge(z_read, 3)
            pe.wait_ge(row_ready, 3)
            scores(0, kT[:, :, 0:P], 4)
            pe.wait_ge(yT_ready, 1)
            scores(1, kT[:, :, P:TOK], 6)
            pe.wait_ge(hT_split, 2)
            project_gate(4)
            pe.wait_ge(exp_done, HEADS)
            scores(2, kcT, 4)
            pe.wait_ge(S_read, 2)
            for b in range(4):
                ins = tp(ps[:, 6, b * P:(b + 1) * P], kT[:, b, 0:P], ident[:, :])
            ins.then_inc(k_t, 1)
            project_gate(5)
            pe.wait_ge(prob_ready, 1)
            pe.wait_ge(knew_ready, 1)
            prob_t(Sp, 6)
            project_gate(6)
            pe.wait_ge(prob_ready, 2)
            prob_t(Ss[:, :, 0:P], 4)
            project_gate(7)
            pe.wait_ge(PT_read, 1)
            prob_t(Ss[:, :, P:TOK], 6)
            def spread(n):
                m, t = n // 2, n % 2
                if n == 0:
                    pe.wait_ge(PT_read, 2)
                    pe.wait_ge(z_read, 8)
                    pe.wait_ge(const_ready, 3)
                else:
                    pe.wait_ge(bc_read, n)
                if n == 1:
                    pe.wait_ge(kv_stored, 32)
                if n == 3:
                    pe.wait_ge(Af_ready, 1)
                for q in range(4):
                    ins = mm(ps[:, 2 + q, :], selrow[32 * q:32 * q + 32, t, :], modrow[32 * q:32 * q + 32, 1 + m, :],
                             start=True, stop=True)
                ins.then_inc(bc_done, 1)

            pe.wait_ge(z_read, 7)
            for b in range(4):
                for par in range(2):
                    h, hh, o = 2 * b + par, 4 * par + b, DH * par
                    mm(ps[o:o + DH, 0, b * P:(b + 1) * P], vm[:, 0, h * DH:(h + 1) * DH], PTp[:, hh, :], start=True, stop=True)
            spread(0)
            pe.wait_ge(PT_read, 3)
            pe.wait_ge(L["vc"], 16)
            for b in range(4):
                for par in range(2):
                    h, hh, o = 2 * b + par, 4 * par + b, DH * par
                    mm(ps[o:o + DH, 1, b * P:(b + 1) * P], vm[:, 1, h * DH:(h + 1) * DH], PTs[:, 0, hh, :], start=True, stop=False)
                    ins = mm(ps[o:o + DH, 1, b * P:(b + 1) * P], vc[:, h * DH:(h + 1) * DH], PTs[:, 1, hh, :],
                             start=False, stop=True)
            ins.then_inc(O_done, 1)
            pe.wait_ge(yT_split, 2)
            for j in range(KB):
                if j in (1, 3, 5):
                    spread((j + 1) // 2)
                if j >= 2:
                    pe.wait_ge(merged_ready, j - 1)
                pe.wait_ge(unit_ready, 16 + j + 1)
                for half, (top, rest) in enumerate(((yT_top, yT_rest), (oT_top, oT_rest))):
                    if j == 0 and half:
                        pe.wait_ge(oT_ready, 2)
                    out = ps[:, 6 + j % 2, half * TOK:(half + 1) * TOK]
                    for kk in range(4):
                        wt, wr = w_top[:, j % 2, 4 * half + kk, :], w_rest[:, j % 2, 4 * half + kk, :]
                        mm(out, wt, top[:, kk, :], start=(kk == 0), stop=False)
                        mm(out, wt, rest[:, kk, :], start=False, stop=False)
                        ins = mm(out, wr, top[:, kk, :], start=False, stop=(kk == 3))
                ins.then_inc(br_done, 1)
            pe.wait_ge(br_done, KB)
            pe.sem_inc(moe_free, 8)

            def turn_h2(t):
                for j in range(KB):
                    if j % 4 == 0:
                        pe.wait_ge(h2_ready, 2 * t + j // 4 + 1)
                        if t == 1:
                            pe.wait_ge(h2T_ready, j // 4 + 1)
                    ins = tp(ps[:, 4 + j // 4, (j % 4) * P:(j % 4 + 1) * P], h2[:, t, j * P:(j + 1) * P], ident[:, :])
                    if j % 4 == 3:
                        ins.then_inc(h2_t, 1)

            def router(t):
                pe.wait_ge(L["wrt"], 16)
                for kk in range(KB):
                    if kk % 4 == 0:
                        pe.wait_ge(h2T_ready, 2 * t + kk // 4 + 1)
                    ins = mm(ps[:, t, 0:E], h2T[:, kk, t * P:(t + 1) * P], wrt[:, kk, :],
                             start=(kk == 0), stop=(kk == KB - 1))
                ins.then_inc(logit_done, 1)

            wo_ = [landed(AT["out", 0, h]).rearrange("p (k n) -> p k n", k=2) for h in range(4)]
            for t in range(2):
                if t == 1:
                    pe.wait_ge(bc_read, 4)
                    pe.wait_ge(Af_ready, 2)
                for n in range(2):
                    for kk in range(KB):
                        if t == 0 and n == 0:
                            pe.wait_ge(merged_ready, kk + 1)
                        ins = mm(ps[:, 2 * t + n, :], sgA[:, kk, t * P:(t + 1) * P],
                                 wo_[kk // 2][:, kk % 2, n * HALF:(n + 1) * HALF], start=(kk == 0), stop=(kk == KB - 1))
                        if (t, n) == (1, 1) and kk % 2:
                            ins.then_inc(moe_free, 1)
                        if (t, n, kk) == (1, 1, 1):
                            turn_h2(0)
                    if (t, n) != (1, 1):
                        ins.then_inc(out_done, 1)
            router(0)
            keep_busy(6, 7)
            turn_h2(1)
            router(1)
            pe.wait_ge(mask_ready, 1)
            mm(ps[:, 6, 0:E], tri[:, :], rt[:, 0, 5, :], start=True, stop=True).then_inc(rank_done, 1)
            keep_busy(4, 3)
            pe.wait_ge(mask_ready, 2)
            mm(ps[:, 7, 0:E], ones[:, :], rt[:, 0, 5, :], start=True, stop=False)
            mm(ps[:, 7, 0:E], tri[:, :], rt[:, 1, 5, :], start=False, stop=True).then_inc(rank_done, 1)
            mm(ps[:, 3, 0:E], ones[:, :], rt[:, 0, 5, :], start=True, stop=False)
            mm(ps[:, 3, 0:E], ones[:, :], rt[:, 1, 5, :], start=False, stop=True).then_inc(count_done, 1)
            pe.wait_ge(comb_ready, 2)
            for t in range(2):
                ins = tp(ps[0:E, 6, t * P:(t + 1) * P], rt[:, t, 6, :], ident[:, :])
            ins.then_inc(comb_t, 1)

            def gather(G, b):
                pe.wait_ge(oh_ready, G + 1)
                for j in range(4 * b, 4 * b + 4):
                    for t in range(2):
                        ins = mm(ps[:, GB + b, (j % 4) * P:(j % 4 + 1) * P], h2[:, t, j * P:(j + 1) * P],
                                 oh[:, t, :], start=(t == 0), stop=(t == 1))
                ins.then_inc(gath_done, 1)

            def scatter(done):
                for n in range(4):
                    t = n // 2
                    mm(ps[:, GB + n, :], woT[:, t, :], yb[:, (n % 2) * HALF:(n % 2 + 1) * HALF],
                       start=True, stop=True).then_inc(done, 1)

            def body(I, r):
                P0 = pe.snap(I * BODY)
                G0 = pe.snap(P0 + (r + 1))
                H0 = pe.snap(P0 * 2 + r)
                lap0 = pe.snap(I * (16 * LAPS))

                def chunk(n):
                    pe.wait_ge(moe_loaded[n % RING], lap0 + 16 * (n // RING + 1))
                    return ring[:, ORDER[n % RING], :]

                for h in range(BODY):
                    Pn, G, H = P0 + h, G0 + h, H0 + 2 * h
                    pe.wait_ge(u_read, Pn + 1)
                    pe.wait_ge(sel_ready, Pn + 1)
                    for n in range(4):
                        for a in range(2):
                            mm(ps[CAP * a:CAP * a + CAP, n, :], selbuf[:, a, :], bparts[:, n * HALF:(n + 1) * HALF],
                               start=True, stop=False)
                    for kk in range(KB):
                        if kk % 4 == 0:
                            pe.wait_ge(xg_ready, H + (kk // 4 + 1))
                        if kk == 3:
                            gather(G - 1, 1)
                        w = [chunk(h * PC + 2 * kk + a) for a in range(2)]
                        for n in range(4):
                            for a in range(2):
                                ins = mm(ps[CAP * a:CAP * a + CAP, n, :], xgT[:, h, kk, CAP * a:CAP * a + CAP],
                                         w[a][:, n * HALF:(n + 1) * HALF], start=False, stop=(kk == KB - 1))
                                if n == 3:
                                    ins.then_inc(moe_free, 1)
                    pe.wait_ge(y_ready, Pn + 1)
                    pe.wait_ge(woT_ready, Pn + 1)
                    scatter(scat_done)
                    pe.wait_ge(acc_done, Pn * 4 + 1)
                    gather(G, 0)
                    pe.wait_ge(wo_ready, Pn + 1)
                    pe.wait_ge(acc_done, Pn * 4 + 3)
                    for t in range(2):
                        ins = tp(ps[:, YB, t * P:(t + 1) * P], wo[:, t, :], ident[:, :])
                    ins.then_inc(woT_done, 1)
                    for f in range(KB):
                        if f % 4 == 0:
                            pe.wait_ge(hid_ready, Pn * 2 + (f // 4 + 1))
                            if f == 0:
                                pe.wait_ge(xg_ready, H + 3)
                            else:
                                pe.wait_ge(acc_done, Pn * 4 + 2)
                        ins = tp(ps[:, GB + f // 4, (f % 4) * P:(f % 4 + 1) * P], hid[:, f * P:(f + 1) * P], ident[:, :])
                        if f % 4 == 3:
                            ins.then_inc(hT_done, 1)
                    pe.wait_ge(woT_ready, Pn + 2)
                    pe.wait_ge(acc_done, Pn * 4 + 4)
                    for f in range(KB):
                        if f % 4 == 0:
                            pe.wait_ge(hTe_ready, Pn * 2 + (f // 4 + 1))
                        if f % 2 == 0:
                            w = [chunk(h * PC + UPC + f + a) for a in range(2)]
                        for n in range(2):
                            for a in range(2):
                                ins = mm(ps[CAP * a:CAP * a + CAP, YB + n, :], hT[:, f, CAP * a:CAP * a + CAP],
                                         w[a][:, (f % 2) * D + n * HALF:(f % 2) * D + (n + 1) * HALF],
                                         start=(f == 0), stop=(f == KB - 1))
                                if f % 2 and n == 1:
                                    ins.then_inc(moe_free, 1)

            pe.sem_inc(woT_done, 1)
            gather(0, 0)
            more = read_flags(pe)
            with pe.Fori(0, PAIRS // BODY) as i:
                body(i, 0)
            pe.wait_ge(y_ready, 1 + PAIRS)
            pe.wait_ge(woT_ready, 1 + PAIRS)

            def run(r):
                gather(r * (PAIRS + 1), 0)
                with pe.Fori(0, PAIRS // BODY) as i:
                    body(i + r * (PAIRS // BODY), r)
                pe.wait_ge(y_ready, 1 + (r + 1) * PAIRS)
                pe.wait_ge(woT_ready, 1 + (r + 1) * PAIRS)
            further_rounds(pe, more, run)
            scatter(last_scat)


_INS = ['x_prompt', 'x_sample', 'cache_k', 'cache_v', 'c', 'c_ctx', 'w_ada', 'b_ada', 'g_mix', 'w_in', 'w_pool',
        'pool_scale', 'w_pa', 'w_pb', 'rpb', 'w_out', 'g_ffn', 'w_router', 'b_router', 'w_up', 'b_up', 'w_down',
        'b_down', 'g_final']
_OUTS = [((1, 128, 1024), 'float32'), ((1, 128, 1024), 'float32'),
         ((1, 1, 8, 128, 64), 'float32'), ((1, 1, 8, 128, 64), 'float32')]


def kernel(**inputs):
    import numpy as _np
    import concourse.bacc as _bacc
    from concourse import mybir as _mybir
    from concourse.bass_utils import run_bass_kernel_spmd as _run

    nc = _bacc.Bacc("TRN2", target_bir_lowering=False, num_devices=1)
    arrays, args = {}, []
    for name in _INS:
        a = _np.ascontiguousarray(inputs[name])
        arrays[f"in_{name}_dram"] = a
        args.append(nc.dram_tensor(f"in_{name}_dram", a.shape, _mybir.dt.from_np(a.dtype), kind="ExternalInput").ap())
    for i, (shape, dtype) in enumerate(_OUTS):
        dt = _mybir.dt.from_np(_np.dtype(dtype))
        args.append(nc.dram_tensor(f"out_{i}_dram", shape, dt, kind="ExternalOutput").ap())
    layer_kernel(nc, *args)
    r = _run(nc, [arrays], core_ids=[0])
    return tuple(r.results[0][f"out_{i}_dram"] for i in range(len(_OUTS)))
```
